# Optimizing a Trainium2 kernel written in Bass

```python
import jax, jax.numpy as jnp
from jax import lax
import numpy as np
import math

D_MODEL = 1024
BATCH = 1
SEQ = 256
DEPTH = 2

HEAD_DIM = 64
SWA_Q_HEADS = 8
SWA_KV_HEADS = 2
SWA_G = SWA_Q_HEADS // SWA_KV_HEADS
DSA_Q_HEADS = 8
DSA_KV_HEADS = 1
DSA_G = DSA_Q_HEADS // DSA_KV_HEADS
IDX_HEADS = 8
IDX_DIM = 32
TOPK_MAX = 256
WINDOW = 128
BLOCK = 128
ROPE_THETA = 10000.0
PLE_DIM = 256
MIX_WIDTH = (SWA_Q_HEADS + DSA_Q_HEADS) * HEAD_DIM
D_FF = -(-(8 * D_MODEL) // (3 * 256)) * 256
DN_ALPHA = (2 * DEPTH) ** 0.25
DN_BETA = (8 * DEPTH) ** -0.25
LN_EPS = 1e-5
NEG = -1e30
IN_SIZES = (SWA_Q_HEADS * HEAD_DIM, SWA_KV_HEADS * HEAD_DIM, SWA_KV_HEADS * HEAD_DIM,
            DSA_Q_HEADS * HEAD_DIM, DSA_KV_HEADS * HEAD_DIM, DSA_KV_HEADS * HEAD_DIM,
            IDX_HEADS * IDX_DIM, IDX_DIM, IDX_HEADS)
IN_COLS = sum(IN_SIZES)


def layer_norm(x, g, b):
    xf = x.astype(jnp.float32)
    mu = xf.mean(-1, keepdims=True)
    var = jnp.square(xf - mu).mean(-1, keepdims=True)
    y = (xf - mu) * lax.rsqrt(var + LN_EPS)
    return (y * g.astype(jnp.float32) + b.astype(jnp.float32)).astype(x.dtype)

def rope(x, positions):
    half = x.shape[-1] // 2
    inv = ROPE_THETA ** (-jnp.arange(half, dtype=jnp.float32) / half)
    ang = positions.astype(jnp.float32)[..., None] * inv
    ang = ang.reshape(ang.shape[:2] + (1,) * (x.ndim - 3) + (half,))
    cos, sin = jnp.cos(ang), jnp.sin(ang)
    x1 = x[..., :half].astype(jnp.float32)
    x2 = x[..., half:].astype(jnp.float32)
    return jnp.concatenate([x1 * cos - x2 * sin, x2 * cos + x1 * sin], -1).astype(x.dtype)

def swa_sink_attention(q, k, v, sinks):
    B, S, Hkv, G, D = q.shape
    nb = S // BLOCK
    qb = q.reshape(B, nb, BLOCK, Hkv, G, D)
    kb = k.reshape(B, nb, BLOCK, Hkv, D)
    vb = v.reshape(B, nb, BLOCK, Hkv, D)
    prev = lambda t: jnp.concatenate([jnp.zeros_like(t[:, :1]), t[:, :-1]], axis=1)
    kk = jnp.concatenate([prev(kb), kb], axis=2)
    vv = jnp.concatenate([prev(vb), vb], axis=2)
    s = jnp.einsum('bnqhgd,bnkhd->bnhgqk', qb, kk).astype(jnp.float32) * (D ** -0.5)
    i = jnp.arange(BLOCK)[:, None]
    j = jnp.arange(2 * BLOCK)[None, :]
    diff = BLOCK + i - j
    band = (diff >= 0) & (diff < WINDOW)
    not_pad = (jnp.arange(nb)[:, None, None] > 0) | (j[None] >= BLOCK)
    mask = band[None] & not_pad
    s = jnp.where(mask[None, :, None, None], s, NEG)
    sink = sinks.astype(jnp.float32)[None, None, :, :, None, None]
    m = jnp.maximum(s.max(-1, keepdims=True), sink)
    pr = jnp.exp(s - m)
    denom = pr.sum(-1, keepdims=True) + jnp.exp(sink - m)
    o = jnp.einsum('bnhgqk,bnkhd->bnqhgd', (pr / denom).astype(v.dtype), vv)
    return o.reshape(B, S, Hkv * G * D)

def dsa_sparse_attention(q, k, v, qi, ki, wi, k_top):
    B, S, Hkv, G, D = q.shape
    nb = S // BLOCK
    to_blocks = lambda t: jnp.moveaxis(t.reshape((B, nb, BLOCK) + t.shape[2:]), 1, 0)
    gather = jax.vmap(lambda kv, ix: kv[ix])
    key_pos = jnp.arange(S)

    def one_block(args):
        n, qb, qib, wib = args
        t = n * BLOCK + jnp.arange(BLOCK)
        sc = jnp.einsum('bqhd,bsd->bqhs', qib, ki).astype(jnp.float32)
        idx_score = jnp.einsum('bqhs,bqh->bqs', jax.nn.relu(sc), wib.astype(jnp.float32))
        causal = key_pos[None, :] <= t[:, None]
        idx_score = jnp.where(causal[None], idx_score, NEG)
        _, sel = lax.top_k(idx_score, k_top)
        ks = gather(k, sel)
        vs = gather(v, sel)
        s = jnp.einsum('bqhgd,bqjhd->bqhgj', qb, ks).astype(jnp.float32) * (D ** -0.5)
        valid = sel <= t[None, :, None]
        s = jnp.where(valid[:, :, None, None, :], s, NEG)
        pr = jax.nn.softmax(s, axis=-1)
        o = jnp.einsum('bqhgj,bqjhd->bqhgd', pr.astype(v.dtype), vs)
        return o.reshape(B, BLOCK, Hkv * G * D)

    out = lax.map(one_block, (jnp.arange(nb), to_blocks(q), to_blocks(qi), to_blocks(wi)))
    return jnp.moveaxis(out, 0, 1).reshape(B, S, Hkv * G * D)

def hybrid_layer(x, p_i, positions, w_in, sinks, idx_k_g, idx_k_b, w_o, ln1_g, ln1_b,
                 w_gu, w_down, w_pg, w_pp, ln2_g, ln2_b):
    B, S, _ = x.shape
    k_top = min(TOPK_MAX, S // 4)
    h = x @ w_in
    cuts = [int(c) for c in np.cumsum(IN_SIZES)[:-1]]
    qa, ka, va, qb, kb, vb, qi, ki, wi = jnp.split(h, cuts, axis=-1)
    qa = rope(qa.reshape(B, S, SWA_KV_HEADS, SWA_G, HEAD_DIM), positions)
    ka = rope(ka.reshape(B, S, SWA_KV_HEADS, HEAD_DIM), positions)
    va = va.reshape(B, S, SWA_KV_HEADS, HEAD_DIM)
    qb = rope(qb.reshape(B, S, DSA_KV_HEADS, DSA_G, HEAD_DIM), positions)
    kb = rope(kb.reshape(B, S, DSA_KV_HEADS, HEAD_DIM), positions)
    vb = vb.reshape(B, S, DSA_KV_HEADS, HEAD_DIM)
    qi = rope(qi.reshape(B, S, IDX_HEADS, IDX_DIM), positions)
    ki = rope(layer_norm(ki, idx_k_g, idx_k_b), positions)
    wi = wi * (IDX_HEADS ** -0.5 * IDX_DIM ** -0.5)
    oa = swa_sink_attention(qa, ka, va, sinks.reshape(SWA_KV_HEADS, SWA_G))
    ob = dsa_sparse_attention(qb, kb, vb, qi, ki, wi, k_top)
    mix = jnp.concatenate([oa, ob], axis=-1) @ w_o
    x = layer_norm(DN_ALPHA * x + mix, ln1_g, ln1_b)
    g, u = jnp.split(x @ w_gu, 2, axis=-1)
    ffn = (jax.nn.silu(g) * u) @ w_down
    ple = (p_i @ w_pp) * jax.nn.sigmoid(x @ w_pg)
    return layer_norm(DN_ALPHA * x + ffn + ple, ln2_g, ln2_b)

def first_inputs(seed: int = 0) -> dict:
    key = jax.random.key(seed)
    ks = jax.random.split(key, 20)
    nrm = lambda k, shape, scale: jax.random.normal(k, shape, jnp.float32) * scale
    L = DEPTH
    offs = jax.random.randint(ks[2], (BATCH, 1), 0, 1024)
    positions = (offs + jnp.arange(SEQ)[None, :]).astype(jnp.int32)
    return {
        "x": nrm(ks[0], (BATCH, SEQ, D_MODEL), 1.0),
        "p": nrm(ks[1], (DEPTH, BATCH, SEQ, PLE_DIM), 1.0),
        "positions": positions,
        "ln_in_g": 1.0 + nrm(ks[3], (D_MODEL,), 0.02),
        "ln_in_b": nrm(ks[4], (D_MODEL,), 0.02),
        "w_in": nrm(ks[5], (L, D_MODEL, IN_COLS), D_MODEL ** -0.5),
        "attn_sinks": nrm(ks[6], (L, SWA_Q_HEADS), 0.5),
        "idx_k_g": 1.0 + nrm(ks[7], (L, IDX_DIM), 0.02),
        "idx_k_b": nrm(ks[8], (L, IDX_DIM), 0.02),
        "w_o": nrm(ks[9], (L, MIX_WIDTH, D_MODEL), DN_BETA * MIX_WIDTH ** -0.5),
        "ln1_g": 1.0 + nrm(ks[10], (L, D_MODEL), 0.02),
        "ln1_b": nrm(ks[11], (L, D_MODEL), 0.02),
        "w_gu": nrm(ks[12], (L, D_MODEL, 2 * D_FF), D_MODEL ** -0.5),
        "w_down": nrm(ks[13], (L, D_FF, D_MODEL), DN_BETA * D_FF ** -0.5),
        "w_pg": nrm(ks[14], (L, D_MODEL, D_MODEL), D_MODEL ** -0.5),
        "w_pp": nrm(ks[15], (L, PLE_DIM, D_MODEL), DN_BETA * PLE_DIM ** -0.5),
        "ln2_g": 1.0 + nrm(ks[16], (L, D_MODEL), 0.02),
        "ln2_b": nrm(ks[17], (L, D_MODEL), 0.02),
    }

def first_block(x, p, positions, ln_in_g, ln_in_b, w_in, attn_sinks, idx_k_g, idx_k_b, w_o,
              ln1_g, ln1_b, w_gu, w_down, w_pg, w_pp, ln2_g, ln2_b):
    x = layer_norm(x, ln_in_g, ln_in_b)
    for i in range(DEPTH):
        x = hybrid_layer(x, p[i], positions, w_in[i], attn_sinks[i], idx_k_g[i], idx_k_b[i],
                         w_o[i], ln1_g[i], ln1_b[i], w_gu[i], w_down[i], w_pg[i], w_pp[i],
                         ln2_g[i], ln2_b[i])
    return x


MEM_LEN = 256
MLA_HEADS = 8
MLA_NOPE = 64
MLA_ROPE = 32
MLA_V = 64
MLA_Q_RANK = 384
MLA_KV_RANK = 256
ROPE_BASE = 10000.0
NSA_HEADS = 8
NSA_KV_HEADS = 2
NSA_GROUP = NSA_HEADS // NSA_KV_HEADS
NSA_DH = 64
CMP_STRIDE = 16
CMP_BLOCK = 2 * CMP_STRIDE
CMP_HIDDEN = 128
SEL_BLOCK = 64
N_SEL = 16
WINDOW_2 = 512
FORCED_SCORE = 1e4
XA_HEADS = 4
XA_DH = D_MODEL // XA_HEADS
D_FF_2 = 2816
CONV_W = 3
QB = 128
DEEPNORM_ALPHA = (2.0 * DEPTH) ** 0.25
DEEPNORM_BETA = (8.0 * DEPTH) ** -0.25
RMS_EPS = 1e-6
NEG_2 = -1e30

IN_SPLITS = (
    MLA_Q_RANK,
    MLA_KV_RANK,
    MLA_ROPE,
    NSA_HEADS * NSA_DH,
    NSA_KV_HEADS * NSA_DH,
    NSA_KV_HEADS * NSA_DH,
    NSA_KV_HEADS * NSA_DH,
    NSA_KV_HEADS * NSA_DH,
    NSA_KV_HEADS * NSA_DH,
    NSA_KV_HEADS * NSA_DH,
    NSA_HEADS * 3,
)
IN_COLS_2 = sum(IN_SPLITS)
MIX_WIDTH_2 = MLA_HEADS * MLA_V + NSA_HEADS * NSA_DH


def layer_norm_2(x, g, b):
    xf = x.astype(jnp.float32)
    mu = jnp.mean(xf, -1, keepdims=True)
    var = jnp.mean(jnp.square(xf - mu), -1, keepdims=True)
    return ((xf - mu) * lax.rsqrt(var + LN_EPS) * g + b).astype(x.dtype)

def rms_norm(x, g):
    xf = x.astype(jnp.float32)
    return (xf * lax.rsqrt(jnp.mean(xf * xf, -1, keepdims=True) + RMS_EPS) * g).astype(x.dtype)

def masked_softmax(s, mask):
    s = jnp.where(mask, s, NEG_2)
    m = jnp.max(s, -1, keepdims=True)
    e = jnp.where(mask, jnp.exp(s - m), 0.0)
    d = jnp.sum(e, -1, keepdims=True)
    return e / jnp.maximum(d, 1e-30)

def alibi_slopes(n):
    return 2.0 ** (-8.0 * jnp.arange(1, n + 1, dtype=jnp.float32) / n)

def rope_tables(S):
    inv = ROPE_BASE ** (-jnp.arange(0, MLA_ROPE, 2, dtype=jnp.float32) / MLA_ROPE)
    ang = jnp.arange(S, dtype=jnp.float32)[:, None] * inv[None, :]
    return jnp.cos(ang), jnp.sin(ang)

def apply_rope(x, cos, sin):
    x1, x2 = jnp.split(x, 2, axis=-1)
    c = cos[None, :, None, :].astype(x.dtype)
    s = sin[None, :, None, :].astype(x.dtype)
    return jnp.concatenate([x1 * c - x2 * s, x1 * s + x2 * c], axis=-1)

def to_blocks(x):
    B, S = x.shape[:2]
    return x.reshape(B, S // QB, QB, *x.shape[2:]).swapaxes(0, 1)

def from_blocks(y):
    nq, B = y.shape[:2]
    return y.swapaxes(0, 1).reshape(B, nq * QB, *y.shape[3:])

def mla_mixer(cq, ckv, kr, cq_g, w_uq, ckv_g, w_ukv, cos, sin):
    B, S, _ = cq.shape
    q = (rms_norm(cq, cq_g) @ w_uq).reshape(B, S, MLA_HEADS, MLA_NOPE + MLA_ROPE)
    kv = (rms_norm(ckv, ckv_g) @ w_ukv).reshape(B, S, MLA_HEADS, MLA_NOPE + MLA_V)
    q_nope = q[..., :MLA_NOPE]
    q_rope = apply_rope(q[..., MLA_NOPE:], cos, sin)
    k_nope, v = kv[..., :MLA_NOPE], kv[..., MLA_NOPE:]
    k_rope = apply_rope(kr[:, :, None, :], cos, sin)[:, :, 0]
    scale = (MLA_NOPE + MLA_ROPE) ** -0.5
    kpos = jnp.arange(S)

    def block(args):
        i, qn, qr = args
        s = (jnp.einsum('bqhd,bkhd->bhqk', qn, k_nope)
             + jnp.einsum('bqhd,bkd->bhqk', qr, k_rope)).astype(jnp.float32) * scale
        qpos = i * QB + jnp.arange(QB)
        p = masked_softmax(s, kpos[None, :] <= qpos[:, None])
        return jnp.einsum('bhqk,bkhd->bqhd', p.astype(v.dtype), v)

    o = lax.map(block, (jnp.arange(S // QB), to_blocks(q_nope), to_blocks(q_rope)))
    return from_blocks(o).reshape(B, S, MLA_HEADS * MLA_V)

def compress_blocks(kv, pe, w1, b1, w2):
    B, S, G, D = kv.shape
    ch = kv.reshape(B, S // CMP_STRIDE, CMP_STRIDE, G, D)
    blk = jnp.concatenate([ch[:, :-1], ch[:, 1:]], axis=2) + pe[None, None, :, None, :]
    flat = blk.transpose(0, 1, 3, 2, 4).reshape(B, -1, G, CMP_BLOCK * D)
    return jax.nn.gelu(flat @ w1 + b1) @ w2

def nsa_mixer(q, k_cmp, v_cmp, k_slc, v_slc, k_win, v_win, gate_logits,
              pe_k, w1_k, b1_k, w2_k, pe_v, w1_v, b1_v, w2_v):
    B, S, _ = q.shape
    G, R, D = NSA_KV_HEADS, NSA_GROUP, NSA_DH
    scale = D ** -0.5
    slopes = alibi_slopes(NSA_HEADS).reshape(G, R)
    kv4 = lambda a: a.reshape(B, S, G, D)

    kc = compress_blocks(kv4(k_cmp), pe_k, w1_k, b1_k, w2_k)
    vc = compress_blocks(kv4(v_cmp), pe_v, w1_v, b1_v, w2_v)
    NC = kc.shape[1]
    c_start = jnp.arange(NC) * CMP_STRIDE
    c_end = c_start + CMP_BLOCK - 1

    NS = S // SEL_BLOCK
    n_sel = min(N_SEL, NS)
    s_start = jnp.arange(NS) * SEL_BLOCK
    overlap = jnp.clip(jnp.minimum(c_start[:, None] + CMP_BLOCK, s_start[None, :] + SEL_BLOCK)
                       - jnp.maximum(c_start[:, None], s_start[None, :]), 0).astype(jnp.float32) / CMP_BLOCK
    ks_blk = kv4(k_slc).reshape(B, NS, SEL_BLOCK, G, D).transpose(0, 3, 1, 2, 4).reshape(B, G, NS, SEL_BLOCK * D)
    vs_blk = kv4(v_slc).reshape(B, NS, SEL_BLOCK, G, D).transpose(0, 3, 1, 2, 4).reshape(B, G, NS, SEL_BLOCK * D)

    kw_pad = jnp.pad(kv4(k_win), ((0, 0), (WINDOW_2, 0), (0, 0), (0, 0)))
    vw_pad = jnp.pad(kv4(v_win), ((0, 0), (WINDOW_2, 0), (0, 0), (0, 0)))

    gates = jax.nn.sigmoid(gate_logits.astype(jnp.float32)).reshape(B, S, G, R, 3).astype(q.dtype)
    qg = q.reshape(B, S, G, R, D)
    M = n_sel * SEL_BLOCK
    blk_ids = jnp.arange(NS)

    def block(args):
        i, qi, gi = args
        t = i * QB + jnp.arange(QB)
        s = jnp.einsum('bqgrd,bngd->bgrqn', qi, kc).astype(jnp.float32) * scale
        s = s - slopes[:, :, None, None] * (t[:, None] - c_end[None, :]).astype(jnp.float32)
        p_c = masked_softmax(s, c_end[None, :] <= t[:, None])
        o_c = jnp.einsum('bgrqn,bngd->bqgrd', p_c.astype(vc.dtype), vc)
        imp = jnp.einsum('bgrqn,nj->bgqj', p_c, overlap)
        cur = t // SEL_BLOCK
        valid = blk_ids[None, :] <= cur[:, None]
        forced = (blk_ids[None, :] == 0) | (blk_ids[None, :] == cur[:, None]) | (blk_ids[None, :] == cur[:, None] - 1)
        score = jnp.where(forced, FORCED_SCORE, jnp.where(valid, imp, -1.0))
        top_score, idx = lax.top_k(score, n_sel)
        sel_ok = top_score >= 0
        flat_idx = idx.reshape(B, G, QB * n_sel)[..., None]
        kg = jnp.take_along_axis(ks_blk, flat_idx, axis=2).reshape(B, G, QB, M, D)
        vg = jnp.take_along_axis(vs_blk, flat_idx, axis=2).reshape(B, G, QB, M, D)
        pos5 = idx[..., None] * SEL_BLOCK + jnp.arange(SEL_BLOCK)
        dist5 = t[None, None, :, None, None] - pos5
        mask_s = (sel_ok[..., None] & (dist5 >= 0)).reshape(B, G, 1, QB, M)
        dist_s = dist5.reshape(B, G, 1, QB, M).astype(jnp.float32)
        s = jnp.einsum('bqgrd,bgqmd->bgrqm', qi, kg).astype(jnp.float32) * scale
        s = s - slopes[None, :, :, None, None] * dist_s
        p_s = masked_softmax(s, mask_s)
        o_s = jnp.einsum('bgrqm,bgqmd->bqgrd', p_s.astype(vg.dtype), vg)
        kw = lax.dynamic_slice_in_dim(kw_pad, i * QB, WINDOW_2 + QB, axis=1)
        vw = lax.dynamic_slice_in_dim(vw_pad, i * QB, WINDOW_2 + QB, axis=1)
        kpos = i * QB - WINDOW_2 + jnp.arange(WINDOW_2 + QB)
        dist = t[:, None] - kpos[None, :]
        s = jnp.einsum('bqgrd,bkgd->bgrqk', qi, kw).astype(jnp.float32) * scale
        s = s - slopes[:, :, None, None] * dist.astype(jnp.float32)
        p_w = masked_softmax(s, (dist >= 0) & (dist < WINDOW_2) & (kpos[None, :] >= 0))
        o_w = jnp.einsum('bgrqk,bkgd->bqgrd', p_w.astype(vw.dtype), vw)
        return gi[..., 0:1] * o_c + gi[..., 1:2] * o_s + gi[..., 2:3] * o_w

    o = lax.map(block, (jnp.arange(S // QB), to_blocks(qg), to_blocks(gates)))
    return from_blocks(o).reshape(B, S, NSA_HEADS * NSA_DH)

def memory_cross_attn(x, memn, wq, wkv, wo):
    B, S, _ = x.shape
    Mm = memn.shape[1]
    q = (x @ wq).reshape(B, S, XA_HEADS, XA_DH)
    k, v = jnp.split(memn @ wkv, 2, axis=-1)
    k = k.reshape(B, Mm, XA_HEADS, XA_DH)
    v = v.reshape(B, Mm, XA_HEADS, XA_DH)
    s = jnp.einsum('bshd,bmhd->bhsm', q, k).astype(jnp.float32) * (XA_DH ** -0.5)
    p = jax.nn.softmax(s, axis=-1)
    o = jnp.einsum('bhsm,bmhd->bshd', p.astype(v.dtype), v).reshape(B, S, XA_HEADS * XA_DH)
    return o @ wo

def conv_ffn(x, w_up, conv_w, conv_b, w_down):
    u = x @ w_up
    C = u.shape[-1]
    u = lax.conv_general_dilated(u, conv_w[:, None, :].astype(u.dtype), window_strides=(1,),
                                 padding=[(CONV_W - 1, 0)],
                                 dimension_numbers=('NWC', 'WIO', 'NWC'),
                                 feature_group_count=C) + conv_b
    a, g = jnp.split(u, 2, axis=-1)
    return (a * jax.nn.silu(g)) @ w_down

def second_inputs(seed: int = 0) -> dict:
    key = jax.random.key(seed)
    keys = iter(jax.random.split(key, 40))
    L = DEPTH

    def nrm(shape, scale):
        return jax.random.normal(next(keys), shape, jnp.float32) * scale

    def gain(shape):
        return 1.0 + nrm(shape, 0.02)

    cmp_in = CMP_BLOCK * NSA_DH
    return {
        'x': nrm((BATCH, SEQ, D_MODEL), 1.0),
        'mem': nrm((BATCH, MEM_LEN, D_MODEL), 1.0),
        'ln_in_g': gain((D_MODEL,)),
        'ln_in_b': nrm((D_MODEL,), 0.02),
        'ln_mem_g': gain((D_MODEL,)),
        'ln_mem_b': nrm((D_MODEL,), 0.02),
        'w_in': nrm((L, D_MODEL, IN_COLS_2), D_MODEL ** -0.5),
        'mla_cq_g': gain((L, MLA_Q_RANK)),
        'mla_w_uq': nrm((L, MLA_Q_RANK, MLA_HEADS * (MLA_NOPE + MLA_ROPE)), MLA_Q_RANK ** -0.5),
        'mla_ckv_g': gain((L, MLA_KV_RANK)),
        'mla_w_ukv': nrm((L, MLA_KV_RANK, MLA_HEADS * (MLA_NOPE + MLA_V)), MLA_KV_RANK ** -0.5),
        'nsa_pe_k': nrm((L, CMP_BLOCK, NSA_DH), 0.02),
        'nsa_w1_k': nrm((L, cmp_in, CMP_HIDDEN), cmp_in ** -0.5),
        'nsa_b1_k': nrm((L, CMP_HIDDEN), 0.02),
        'nsa_w2_k': nrm((L, CMP_HIDDEN, NSA_DH), CMP_HIDDEN ** -0.5),
        'nsa_pe_v': nrm((L, CMP_BLOCK, NSA_DH), 0.02),
        'nsa_w1_v': nrm((L, cmp_in, CMP_HIDDEN), cmp_in ** -0.5),
        'nsa_b1_v': nrm((L, CMP_HIDDEN), 0.02),
        'nsa_w2_v': nrm((L, CMP_HIDDEN, NSA_DH), CMP_HIDDEN ** -0.5),
        'w_out': nrm((L, MIX_WIDTH_2, D_MODEL), DEEPNORM_BETA * MIX_WIDTH_2 ** -0.5),
        'ln1_g': gain((L, D_MODEL)),
        'ln1_b': nrm((L, D_MODEL), 0.02),
        'xa_wq': nrm((L, D_MODEL, XA_HEADS * XA_DH), D_MODEL ** -0.5),
        'xa_wkv': nrm((L, D_MODEL, 2 * XA_HEADS * XA_DH), D_MODEL ** -0.5),
        'xa_wo': nrm((L, XA_HEADS * XA_DH, D_MODEL), DEEPNORM_BETA * (XA_HEADS * XA_DH) ** -0.5),
        'ln2_g': gain((L, D_MODEL)),
        'ln2_b': nrm((L, D_MODEL), 0.02),
        'ffn_w_up': nrm((L, D_MODEL, 2 * D_FF_2), D_MODEL ** -0.5),
        'ffn_conv_w': nrm((L, CONV_W, 2 * D_FF_2), CONV_W ** -0.5),
        'ffn_conv_b': nrm((L, 2 * D_FF_2), 0.02),
        'ffn_w_down': nrm((L, D_FF_2, D_MODEL), DEEPNORM_BETA * D_FF_2 ** -0.5),
        'ln3_g': gain((L, D_MODEL)),
        'ln3_b': nrm((L, D_MODEL), 0.02),
    }

def second_block(x, mem, ln_in_g, ln_in_b, ln_mem_g, ln_mem_b, w_in,
              mla_cq_g, mla_w_uq, mla_ckv_g, mla_w_ukv,
              nsa_pe_k, nsa_w1_k, nsa_b1_k, nsa_w2_k,
              nsa_pe_v, nsa_w1_v, nsa_b1_v, nsa_w2_v,
              w_out, ln1_g, ln1_b, xa_wq, xa_wkv, xa_wo, ln2_g, ln2_b,
              ffn_w_up, ffn_conv_w, ffn_conv_b, ffn_w_down, ln3_g, ln3_b):
    S = x.shape[1]
    x = layer_norm_2(x, ln_in_g, ln_in_b)
    memn = layer_norm_2(mem, ln_mem_g, ln_mem_b)
    cos, sin = rope_tables(S)
    split_at = [int(v) for v in np.cumsum(IN_SPLITS)[:-1]]
    for l in range(DEPTH):
        h = x @ w_in[l]
        cq, ckv, kr, nq, kc, vc, ks, vs, kw, vw, gl = jnp.split(h, split_at, axis=-1)
        o_a = mla_mixer(cq, ckv, kr, mla_cq_g[l], mla_w_uq[l], mla_ckv_g[l], mla_w_ukv[l], cos, sin)
        o_b = nsa_mixer(nq, kc, vc, ks, vs, kw, vw, gl,
                        nsa_pe_k[l], nsa_w1_k[l], nsa_b1_k[l], nsa_w2_k[l],
                        nsa_pe_v[l], nsa_w1_v[l], nsa_b1_v[l], nsa_w2_v[l])
        mix = jnp.concatenate([o_a, o_b], axis=-1) @ w_out[l]
        x = layer_norm_2(DEEPNORM_ALPHA * x + mix, ln1_g[l], ln1_b[l])
        xa = memory_cross_attn(x, memn, xa_wq[l], xa_wkv[l], xa_wo[l])
        x = layer_norm_2(DEEPNORM_ALPHA * x + xa, ln2_g[l], ln2_b[l])
        f = conv_ffn(x, ffn_w_up[l], ffn_conv_w[l], ffn_conv_b[l], ffn_w_down[l])
        x = layer_norm_2(DEEPNORM_ALPHA * x + f, ln3_g[l], ln3_b[l])
    return x


def setup_inputs(seed=0):
    out = dict(first_inputs(seed))
    for name, value in second_inputs(seed + 1).items():
        if name != "x":
            out[name + "_2"] = value
    return out


def reference(
    x, p, positions, ln_in_g, ln_in_b, w_in, attn_sinks, idx_k_g, idx_k_b, w_o, ln1_g, ln1_b,
    w_gu, w_down, w_pg, w_pp, ln2_g, ln2_b, mem_2, ln_in_g_2, ln_in_b_2, ln_mem_g_2, ln_mem_b_2,
    w_in_2, mla_cq_g_2, mla_w_uq_2, mla_ckv_g_2, mla_w_ukv_2, nsa_pe_k_2, nsa_w1_k_2,
    nsa_b1_k_2, nsa_w2_k_2, nsa_pe_v_2, nsa_w1_v_2, nsa_b1_v_2, nsa_w2_v_2, w_out_2, ln1_g_2,
    ln1_b_2, xa_wq_2, xa_wkv_2, xa_wo_2, ln2_g_2, ln2_b_2, ffn_w_up_2, ffn_conv_w_2,
    ffn_conv_b_2, ffn_w_down_2, ln3_g_2, ln3_b_2,
):
    x = first_block(
        x, p, positions, ln_in_g, ln_in_b, w_in, attn_sinks, idx_k_g, idx_k_b, w_o, ln1_g,
        ln1_b, w_gu, w_down, w_pg, w_pp, ln2_g, ln2_b,
    )
    return second_block(
        x, mem_2, ln_in_g_2, ln_in_b_2, ln_mem_g_2, ln_mem_b_2, w_in_2, mla_cq_g_2, mla_w_uq_2,
        mla_ckv_g_2, mla_w_ukv_2, nsa_pe_k_2, nsa_w1_k_2, nsa_b1_k_2, nsa_w2_k_2, nsa_pe_v_2,
        nsa_w1_v_2, nsa_b1_v_2, nsa_w2_v_2, w_out_2, ln1_g_2, ln1_b_2, xa_wq_2, xa_wkv_2,
        xa_wo_2, ln2_g_2, ln2_b_2, ffn_w_up_2, ffn_conv_w_2, ffn_conv_b_2, ffn_w_down_2,
        ln3_g_2, ln3_b_2,
    )


_drawn_inputs = setup_inputs


def setup_inputs(seed=0):
    import zlib

    import numpy as np

    out = dict(_drawn_inputs(seed))
    spreads = {}
    factors = {'attn_sinks': 8.0,
     'idx_k_g': 7.342,
     'idx_k_b': 8.0,
     'ln_in_g_2': 2.711,
     'ln_mem_g_2': 8.0,
     'ln_mem_b_2': 5.586,
     'mla_cq_g_2': 8.0,
     'mla_ckv_g_2': 8.0,
     'nsa_pe_k_2': 8.0,
     'nsa_w1_k_2': 3.11,
     'nsa_b1_k_2': 8.0,
     'nsa_w2_k_2': 3.294,
     'nsa_pe_v_2': 8.0,
     'nsa_b1_v_2': 8.0,
     'ffn_conv_b_2': 6.466}
    for name, (base, spread) in spreads.items():
        noise = np.random.default_rng([zlib.crc32(name.encode()), seed]).standard_normal(out[name].shape)
        drawn = base * np.exp(spread * noise) if base else spread * noise
        out[name] = __import__('jax').numpy.asarray(drawn.astype(out[name].dtype))
    for name, factor in factors.items():
        out[name] = (out[name] * factor).astype(out[name].dtype)
    return out
```

```python
from contextlib import ExitStack
import math

import numpy as np

import concourse.bass as bass
from concourse import mybir

F32 = mybir.dt.float32
F32R = mybir.dt.float32r
I32 = mybir.dt.int32
ALU = mybir.AluOpType
ACT = mybir.ActivationFunctionType
AX = mybir.AxisListType

P = 128
S = 256
NT = S // P
D = 1024
KD = D // P
L = 2
TC = 256
FF = 2816
FS = FF // TC
H = 8
DH = 64
LN_EPS = 1e-5
RMS_EPS = 1e-6
ALPHA = (2 * L) ** 0.25
MASKED = -1e31
NEG = -1e30
TAKEN = -3e38
TOPK = min(256, S // 4)
LOWEST = -3.4e38

QA, KA, VA, QB, KB, VB, QI, KI, WI, IN1 = 0, 512, 640, 768, 1280, 1344, 1408, 1664, 1696, 1704
IN1_ORDER = (6, 5, 3, 4, 0, 1, 2)
CQ, CKV, KR, NQ, KC, KSL, VSL, KWN, VWN, GL, IN2 = 0, 384, 640, 672, 1184, 1440, 1568, 1696, 1824, 1952, 1976
QR, KVR = 384, 256
NC = 15
MD = 96
KVW = 160

NRAW = 2
NW = 3

SWA, DSA, SLC, WIN, MLA = "swa", "dsa", "slc", "win", "mla"


def constants():
    i = np.arange(P)[:, None]
    j = np.arange(S)[None, :]
    diag = (j - P) > i
    causal = np.where(diag, MASKED, 0.0)
    band = np.where(diag | ((j < P) & (j <= i)), MASKED, 0.0)
    slope = 2.0 ** -np.arange(1, H + 1)
    dist = P + i - j
    alibi = np.where(dist[:, None, :] < 0, MASKED, -slope[None, :, None] * dist[:, None, :] * DH ** 0.5)
    t = np.arange(NT)[None, :, None, None] * P + i[:, :, None, None]
    end = np.arange(NC + 1)[None, None, None, :] * 16 + 31
    ok = (end <= t) & (end < NC * 16 + 31)
    cmp = np.where(ok, -slope[None, None, :, None] * (t - end), NEG)
    valid = (np.arange(NT)[None, :] * P + i >= 31).astype(np.float64)
    inv = (10000.0 ** -(np.arange(32) / 32)).astype(np.float32)
    ang = (np.arange(S, dtype=np.float32)[:, None] * inv[None, ::2]).astype(np.float32)
    ang = ang.reshape(NT, P, 16).transpose(1, 0, 2).reshape(P, NT * 16)
    out = {
        "ident": np.eye(P), "causal": causal, "band": band, "alibi": alibi.reshape(P, H * S),
        "cmpbias": cmp.reshape(P, NT * H * (NC + 1)), "valid": valid,
        "inv": np.broadcast_to(inv, (P, 32)), "mcos": np.cos(ang), "msin": np.sin(ang),
    }
    return {k: np.ascontiguousarray(v, dtype=np.float32) for k, v in out.items()}


def plan_tiles(w):
    tiles = []

    def rows(a):
        return a.rearrange("(k p) n -> p k n", p=P)

    def ffn(block, l, gate, up, down):
        def gu(s):
            tiles.append(((block, "g", l, s), gate[:, :, s * TC:(s + 1) * TC]))
            tiles.append(((block, "u", l, s), up[:, :, s * TC:(s + 1) * TC]))

        def d(s):
            tiles.append(((block, "d", l, s), down[:, 2 * s:2 * s + 2, :]))
        gu(0)
        for s in range(1, FS):
            gu(s)
            d(s - 1)
        d(FS - 1)

    for l in range(L):
        tiles.append(((1, "pp", l, 0), rows(w["w_pp"][l])))
        for k in IN1_ORDER:
            tiles.append(((1, "in", l, k), rows(w["w_in"][l])[:, :, k * TC:min((k + 1) * TC, IN1)]))
        for k in range(4):
            tiles.append(((1, "o", l, k), rows(w["w_o"][l])[:, :, k * TC:(k + 1) * TC]))
        for k in range(4):
            tiles.append(((1, "pg", l, k), rows(w["w_pg"][l])[:, :, k * TC:(k + 1) * TC]))
        gu = rows(w["w_gu"][l])
        ffn(1, l, gu[:, :, 0:FF], gu[:, :, FF:2 * FF], rows(w["w_down"][l]))
    for l in range(L):
        for k in range(8):
            tiles.append(((2, "in", l, k), rows(w["w_in_2"][l])[:, :, k * TC:min((k + 1) * TC, IN2)]))
        for k in range(2):
            tiles.append(((2, "uq", l, k), rows(w["mla_w_uq_2"][l])[:, :, k * 384:(k + 1) * 384]))
        tiles.append(((2, "ukv", l, 0), rows(w["mla_w_ukv_2"][l])))
        tiles.append(((2, "w1", l, 0), rows(w["nsa_w1_k_2"][l])))
        tiles.append(((2, "w1", l, 1), rows(w["nsa_w1_v_2"][l])))
        for name, key, n in (("out", "w_out_2", 4), ("kv", "xa_wkv_2", 8), ("xq", "xa_wq_2", 4),
                             ("xo", "xa_wo_2", 4)):
            for k in range(n):
                tiles.append(((2, name, l, k), rows(w[key][l])[:, :, k * TC:(k + 1) * TC]))
        up = rows(w["ffn_w_up_2"][l])
        ffn(2, l, up[:, :, FF:2 * FF], up[:, :, 0:FF], rows(w["ffn_w_down_2"][l]))
    return tiles, {key: c for c, (key, _) in enumerate(tiles)}


def plan_units():
    units = []
    for l in range(L):
        units += [(1, l, kind, t) for kind in (SWA, DSA) for t in range(NT)]
    for l in range(L):
        units += [(2, l, kind, t) for kind in (SLC, WIN, MLA) for t in range(NT)]
    chunk0, m = [], 0
    for _, _, _, t in units:
        for _ in range(2):
            chunk0.append(m)
            m += t + 1
    chunk0.append(m)
    return units, chunk0


def build(nc, w, c, out):
    tiles, ti = plan_tiles(w)
    units, chunk0 = plan_units()
    n_tiles = len(tiles)

    def unit0(block, l):
        return next(u for u, x in enumerate(units) if x[0] == block and x[1] == l)

    with ExitStack() as ctx:
        def sb(name, shape, dt=F32):
            return ctx.enter_context(nc.sbuf_tensor(name, [P] + shape, dt))

        def sem(name):
            return ctx.enter_context(nc.semaphore(name))

        raw = sb("raw", [NRAW, 2048])
        whi = sb("whi", [NW, 2048], F32R)
        wlo = sb("wlo", [NW, 2048], F32R)
        xtok = sb("xtok", [NT, D])
        sy = sb("sy", [2, 2048])
        xhi = sb("xhi", [KD, S], F32R)
        xlo = sb("xlo", [KD, S], F32R)
        gb = sb("gb", [2, D])
        r1 = sb("r1", [4096])
        r2 = sb("r2", [4608])
        r3 = sb("r3", [4096])
        rt = sb("rt", [2048])
        pt = sb("pt", [4, 512])
        rr = sb("rr", [2560], F32R)
        ident = sb("ident", [P])
        causal = sb("causal", [S])
        band = sb("band", [S])
        inv = sb("inv", [32])
        pos_i = sb("pos_i", [NT], I32)
        pos_f = sb("pos_f", [NT])
        cos64 = sb("cos64", [NT, 64])
        sin64 = sb("sin64", [NT, 64])
        cos32 = sb("cos32", [NT, 32])
        sin32 = sb("sin32", [NT, 32])
        pcol = sb("pcol", [7, P])
        stats = sb("stats", [NT, 2, 6])
        meanvar = sb("meanvar", [NT, 2])
        vare = sb("vare", [4])
        rstd = sb("rstd", [4])
        mhalf = sb("mhalf", [4])
        sinkb = sb("sinkb", [L, H])
        ikg = sb("ikg", [L, 2, 32])
        wi_s = sb("wi_s", [NT, H])
        top8 = sb("top8", [8])
        mx = sb("mx", [2, H])
        nmx = sb("nmx", [2, H])
        den = sb("den", [2, H])
        rden = sb("rden", [2, H])
        esink = sb("esink", [2, 2, H])
        memhi = sb("memhi", [KD, S], F32R)
        memlo = sb("memlo", [KD, S], F32R)
        cmpbias = sb("cmpbias", [NT, H * 16])
        valid = sb("valid", [NT])
        mcos = sb("mcos", [NT, 16])
        msin = sb("msin", [NT, 16])
        w2s = sb("w2s", [L, 2, DH])
        hcmp = sb("hcmp", [2, 2 * NC])
        kct = sb("kct", [16])
        vbd = sb("vbd", [2, 4 * DH])
        krope = sb("krope", [NT, 32])
        gates = sb("gates", [NT, 3 * H])
        varc = sb("varc", [4])
        rstdc = sb("rstdc", [4])
        cmx = sb("cmx", [NT * H])
        cden = sb("cden", [NT * H])
        coef = sb("coef", [NT * H])
        otmp = sb("otmp", [H * DH])
        xmx = sb("xmx", [NT, 4])
        xden = sb("xden", [NT, 4])
        psw = ctx.enter_context(nc.psum_tensor("psw", [P, 4, 512], F32))
        psa = ctx.enter_context(nc.psum_tensor("psa", [P, 4, 512], F32))

        tile_loaded = [sem(f"tile_loaded{i}") for i in range(NRAW)]
        hi_ready = sem("hi_ready")
        lo_ready = sem("lo_ready")
        tile_done = sem("tile_done")
        consts_loaded = sem("consts_loaded")
        params_loaded = sem("params_loaded")
        x_loaded = sem("x_loaded")
        p_loaded = sem("p_loaded")
        gb_loaded = sem("gb_loaded")
        params_turned = sem("params_turned")
        params_ready = sem("params_ready")
        mhalf_ready = sem("mhalf_ready")
        angles_ready = sem("angles_ready")
        sines_ready = sem("sines_ready")
        tables_ready = sem("tables_ready")
        ln_var = sem("ln_var")
        ln_rstd = sem("ln_rstd")
        ln_xn = sem("ln_xn")
        ln_turned = sem("ln_turned")
        ln_v = sem("ln_v")
        xT_ready = sem("xT_ready")
        x_ready = sem("x_ready")
        p_turned = sem("p_turned")
        p_hi = sem("p_hi")
        p_ready = sem("p_ready")
        pp_ready = sem("pp_ready")
        proj_ready = sem("proj_ready")
        ki_var = sem("ki_var")
        ki_rstd = sem("ki_rstd")
        qki_roped = sem("qki_roped")
        qkb_roped = sem("qkb_roped")
        qka_roped = sem("qka_roped")
        heads_turned = sem("heads_turned")
        heads_ready = sem("heads_ready")
        iscores_done = sem("iscores_done")
        relu_done = sem("relu_done")
        icomb_done = sem("icomb_done")
        scores_done = sem("scores_done")
        smax_done = sem("smax_done")
        exp_done = sem("exp_done")
        pt_done = sem("pt_done")
        pt_ready = sem("pt_ready")
        pv_done = sem("pv_done")
        o_ready = sem("o_ready")
        opT_turned = sem("opT_turned")
        opT_hi = sem("opT_hi")
        opT_ready = sem("opT_ready")
        pg_exp = sem("pg_exp")
        ple_used = sem("ple_used")
        gate_ready = sem("gate_ready")
        hid_ready = sem("hid_ready")
        stored = sem("stored")
        alibi_loaded = sem("alibi_loaded")
        mem_loaded = sem("mem_loaded")
        proj2_ready = sem("proj2_ready")
        c_var = sem("c_var")
        c_rstd = sem("c_rstd")
        c_normed = sem("c_normed")
        c_turned = sem("c_turned")
        c_v = sem("c_v")
        cT_ready = sem("cT_ready")
        gate_exp = sem("gate_exp")
        qm_ready = sem("qm_ready")
        qm_roped = sem("qm_roped")
        kd_ready = sem("kd_ready")
        nsa_turned = sem("nsa_turned")
        nsa_ready = sem("nsa_ready")
        kvm_ready = sem("kvm_ready")
        km_roped = sem("km_roped")
        mla_turned = sem("mla_turned")
        mla_ready = sem("mla_ready")
        cmp_x = sem("cmp_x")
        cmp_gelu = sem("cmp_gelu")
        cmp_kv = sem("cmp_kv")
        cmp_kv_ready = sem("cmp_kv_ready")
        cmp_scores = sem("cmp_scores")
        cmp_shifted = sem("cmp_shifted")
        cmp_exp = sem("cmp_exp")
        cmp_turned = sem("cmp_turned")
        cmp_pT = sem("cmp_pT")
        cmp_pv = sem("cmp_pv")
        cmp_o = sem("cmp_o")
        kv_ready = sem("kv_ready")
        xq_ready = sem("xq_ready")
        xs_done = sem("xs_done")
        xmax_done = sem("xmax_done")
        xexp_done = sem("xexp_done")
        xp_ready = sem("xp_ready")
        xp_turned = sem("xp_turned")
        xpT_ready = sem("xpT_ready")
        conv_first = sem("conv_first")
        conv_done = sem("conv_done")

        prow = r1[:, 0:7 * P].rearrange("p (j c) -> p j c", j=7)
        angs = r1[:, 1024:1024 + 6 * NT * 32].rearrange("p (j c) -> p j c", j=6)
        iscore = r3[:, 13 * S:13 * S + NT * S].rearrange("p (t k) -> p t k", t=NT)
        dmask = r2[:, NT * 13 * P:NT * 13 * P + NT * S].rearrange("p (t k) -> p t k", t=NT)
        xv = sy[:, 0, :].rearrange("p (k s) -> p k s", k=KD)
        y = sy[:, 1, :].rearrange("p (t d) -> p t d", t=NT)
        soft = sy[:].rearrange("p b (h k) -> p b h k", h=H)
        proj1 = r1[:, 0:NT * IN1].rearrange("p (t c) -> p t c", t=NT)
        roped = r2[:, 0:NT * 13 * P].rearrange("p (t c) -> p t c", t=NT)
        omix = r2[:, 0:NT * D].rearrange("p (t c) -> p t c", t=NT)
        headT = r3[:, 0:13 * S].rearrange("p (b s) -> p b s", b=13)
        relu = sy[:, 1, :].rearrange("p (h k) -> p h k", h=H)
        ple = rt[:].rearrange("p (t d) -> p t d", t=NT)
        ptok = pt[:, 0, :].rearrange("p (t d) -> p t d", t=NT)
        pT_hi = rr[:, 0:512].rearrange("p (k s) -> p k s", k=2)
        pT_lo = rr[:, 512:1024].rearrange("p (k s) -> p k s", k=2)
        hidh = rr[:, 0:1024].rearrange("p (b c s) -> p b c s", b=2, c=2)
        hidl = rr[:, 1024:2048].rearrange("p (b c s) -> p b c s", b=2, c=2)
        alibi = rt[:].rearrange("p (h k) -> p h k", h=H)
        proj2 = r1[:, 0:NT * IN2].rearrange("p (t c) -> p t c", t=NT)
        qm = r2[:, 0:NT * H * MD].rearrange("p (t c) -> p t c", t=NT)
        kvm = r2[:, 2048:2048 + NT * H * KVW].rearrange("p (t h c) -> p t h c", t=NT, h=H)
        ctmp = r3[:, 0:5 * S].rearrange("p (k s) -> p k s", k=5)
        mqT = r3[:, 0:H * S].rearrange("p (h s) -> p h s", h=H)
        mkT = r3[:, H * S:2 * H * S].rearrange("p (h s) -> p h s", h=H)
        nsaT = gb[:].rearrange("p a b -> p (a b)")[:, 0:6 * S].rearrange("p (b s) -> p b s", b=6)
        cT_hi = rr[:, 0:5 * S].rearrange("p (k s) -> p k s", k=5)
        cT_lo = rr[:, 5 * S:10 * S].rearrange("p (k s) -> p k s", k=5)
        kdup = sy[:, 0, 0:1024].rearrange("p (t q e d) -> p t q e d", t=NT, q=4, e=2)
        nqp = sy[:, 1, 0:1024].rearrange("p (t c) -> p t c", t=NT)
        mtmp = sy[:, 0, 1024:2048].rearrange("p (i c) -> p i c", i=4)
        pcmp = pt[:, 0, :].rearrange("p (t h n) -> p t h n", t=NT, h=H)
        cx = pt[:, 1:3, :].rearrange("p a b -> p (a b)").rearrange("p (q s) -> p q s", q=4)
        cf = pt[:, 3, 0:16 * 2 * NC].rearrange("p (j g n) -> p j g n", j=16, g=2)
        scmp = pt[:, 3, 0:NT * H * 16].rearrange("p (t c) -> p t c", t=NT)
        pcT = pt[:, 1, :].rearrange("p (j q) -> p j q", j=4)
        cx_hi = [rr[:, 1000 * i:1000 * i + 480].rearrange("p (j c) -> p j c", j=16) for i in range(2)]
        cx_lo = [rr[:, 1000 * i + 500:1000 * i + 980].rearrange("p (j c) -> p j c", j=16) for i in range(2)]
        xkT = r1[:, 0:2048].rearrange("p (k s) -> p k s", k=KD)
        xvt = r1[:, 2048:4096].rearrange("p (t d) -> p t d", t=NT)
        xqT = r3[:, 0:2048].rearrange("p (k s) -> p k s", k=KD)
        xsoft = sy[:, 0, :].rearrange("p (t h k) -> p t h k", t=NT, h=4)
        hidf = r1[:, 0:512]
        conv_a = r1[:, 1536:2560].rearrange("p (b c s) -> p b c s", b=2, c=2)
        conv_g = r1[:, 2560:3584].rearrange("p (b c s) -> p b c s", b=2, c=2)
        gact = r1[:, 512:1536].rearrange("p (b c) -> p b c", b=2)
        egate = r1[:, 1536:3584].rearrange("p (b c) -> p b c", b=4)

        def tile_view(buf, n, i):
            ap = tiles[i][1]
            kt, cols = ap.shape[1], ap.shape[2]
            return buf[:, i % n, 0:kt * cols].rearrange("p (k c) -> p k c", k=kt)

        def tile_flat(buf, n, i):
            ap = tiles[i][1]
            return buf[:, i % n, 0:ap.shape[1] * ap.shape[2]]

        def bank2(ps, b):
            return ps[:, b, :].rearrange("p (t c) -> p t c", t=2)

        def bc(ap, n):
            return ap.unsqueeze(1).broadcast_to([P, n, ap.shape[1]])

        def bci(ap, n):
            return ap.unsqueeze(2).broadcast_to([P, ap.shape[1], n])

        norms = {}

        def add_norm(key, g, b, turned, tok, pc):
            norms[key] = dict(n=len(norms), g=g, b=b, turned=turned, tok=tok, pc=pc,
                              nt=sum(x["turned"] for x in norms.values()),
                              nx=sum(x["tok"] for x in norms.values()))
        add_norm((1, "in", 0), w["ln_in_g"], w["ln_in_b"], True, True, (0, 0))
        for l in range(L):
            add_norm((1, "1", l), w["ln1_g"][l], w["ln1_b"][l], True, True, (0, 16 + 32 * l))
            add_norm((1, "2", l), w["ln2_g"][l], w["ln2_b"][l], l + 1 < L, True, (0, 32 + 32 * l))
        add_norm((2, "in", 0), w["ln_in_g_2"], w["ln_in_b_2"], True, True, (1, 0))
        add_norm((2, "mem", 0), w["ln_mem_g_2"], w["ln_mem_b_2"], True, False, (1, 16))
        for l in range(L):
            add_norm((2, "1", l), w["ln1_g_2"][l], w["ln1_b_2"][l], True, True, (1, 32 + 48 * l))
            add_norm((2, "2", l), w["ln2_g_2"][l], w["ln2_b_2"][l], True, True, (1, 48 + 48 * l))
            add_norm((2, "3", l), w["ln3_g_2"][l], w["ln3_b_2"][l], l + 1 < L, True, (1, 64 + 48 * l))

        tok_norms = [x for x in norms.values() if x["tok"]]
        gb_before = {ti[(1, "in", 0, IN1_ORDER[6])]: 1, ti[(1, "g", 0, 2)]: 2, ti[(1, "in", 1, IN1_ORDER[6])]: 3,
                     ti[(1, "g", 1, 2)]: 4}
        gb_before[ti[(2, "in", 0, 5)]] = 5
        for l in range(L):
            gb_before[ti[(2, "kv", l, 1)]] = 6 + 3 * l
            gb_before[ti[(2, "xo", l, 0)]] = 7 + 3 * l
            gb_before[ti[(2, "g", l, 3)]] = 8 + 3 * l

        const_dmas = [(ident[:], c["ident"]), (inv[:], c["inv"]),
                      (causal[:], c["causal"]), (band[:], c["band"])]
        const_dmas += [(pos_i[:, t:t + 1], w["positions"][0, t * P:(t + 1) * P].rearrange("(p o) -> p o", o=1))
                       for t in range(NT)]
        for l in range(L):
            const_dmas += [(sinkb[:, l, :], w["attn_sinks"][l].partition_broadcast(P)),
                           (ikg[:, l, 0, :], w["idx_k_g"][l].partition_broadcast(P)),
                           (ikg[:, l, 1, :], w["idx_k_b"][l].partition_broadcast(P))]
        param_dmas = []
        param_rows = [0] * 7

        def add_param(j, row, vec):
            n = vec.shape[0] // P
            param_dmas.append((prow[row:row + n, j, :], vec.rearrange("(r c) -> r c", c=P)))
            param_rows[j] = max(param_rows[j], row + n)
        for x in norms.values():
            if x["pc"]:
                add_param(x["pc"][0], x["pc"][1], x["g"])
                add_param(x["pc"][0], x["pc"][1] + KD, x["b"])
        const_dmas += [(cmpbias[:].rearrange("p t c -> p (t c)"), c["cmpbias"]), (valid[:], c["valid"]),
                       (mcos[:].rearrange("p t c -> p (t c)"), c["mcos"]),
                       (msin[:].rearrange("p t c -> p (t c)"), c["msin"])]
        def cqg_row(l): return 3 * l
        def ckvg_row(l): return 6 + 2 * l
        def b1_row(l, i): return 10 + 2 * l + i
        def pe_row(l, i): return 14 + 16 * (2 * l + i)
        for l in range(L):
            const_dmas += [(w2s[:, l, 0, :], w["nsa_w2_k_2"][l]), (w2s[:, l, 1, :], w["nsa_w2_v_2"][l])]
            add_param(2, cqg_row(l), w["mla_cq_g_2"][l])
            add_param(2, ckvg_row(l), w["mla_ckv_g_2"][l])
            for i, kv in enumerate("kv"):
                add_param(2, b1_row(l, i), w[f"nsa_b1_{kv}_2"][l])
                add_param(2, pe_row(l, i), w[f"nsa_pe_{kv}_2"][l].rearrange("c d -> (c d)"))
            for j in range(3):
                add_param(3 + 2 * l + j // 2, 44 * (j % 2), w["ffn_conv_w_2"][l, j])
            add_param(4 + 2 * l, 44, w["ffn_conv_b_2"][l])
        param_rows = [n for n in param_rows if n]
        n_const_dmas, n_param_dmas = len(const_dmas), len(param_dmas)
        block = ctx.enter_context(nc.Block())

        @block.sync
        def _(sp):
            for t in range(NT):
                sp.dma_start(y[:, t, :], w["x"][0, t * P:(t + 1) * P, :]).then_inc(x_loaded, 16)

            def load_gb(m):
                x = tok_norms[m]
                if m >= 1:
                    sp.wait_ge(x_ready, m)
                sp.dma_start(gb[:, 0, :], x["g"].partition_broadcast(P)).then_inc(gb_loaded, 16)
                sp.dma_start(gb[:, 1, :], x["b"].partition_broadcast(P)).then_inc(gb_loaded, 16)

            for i in range(n_tiles):
                if i == NRAW:
                    load_gb(0)
                if i in gb_before:
                    if tiles[i][0][1] == "kv":
                        sp.wait_ge(o_ready, unit0(2, tiles[i][0][2]) + 6)
                    load_gb(gb_before[i])
                if i >= NRAW:
                    sp.wait_ge(lo_ready, i - NRAW + 1)
                key = tiles[i][0]
                if key == (1, "d", 1, FS - 1):
                    sp.wait_ge(hid_ready, FS + 5)
                    sp.dma_start(rt[:], c["alibi"]).then_inc(alibi_loaded, 16)
                if key == (2, "in", 0, 6):
                    sp.wait_ge(x_ready, norms[(2, "in", 0)]["nx"] + 1)
                    for t in range(NT):
                        sp.dma_start(y[:, t, :], w["mem_2"][0, t * P:(t + 1) * P, :]).then_inc(mem_loaded, 16)
                if key[1] == "pp" and key[2] >= 1:
                    sp.wait_ge(x_ready, 2 * key[2])
                if key[1] == "pp":
                    sp.dma_start(ptok, w["p"][key[2], 0].rearrange("(t p) d -> p t d", p=P)).then_inc(p_loaded, 16)
                sp.dma_start(tile_view(raw, NRAW, i), tiles[i][1]).then_inc(tile_loaded[i % NRAW], 16)
            sp.wait_ge(stored, 16 * NT)

        @block.tensor
        def _(pe):
            def take(key):
                pe.wait_ge(lo_ready, ti[key] + 1)
                return tile_view(whi, NW, ti[key]), tile_view(wlo, NW, ti[key])

            def product(o, lh, ll, rh, rl, first, last):
                pe.matmul(o, lh, rh, start=first, stop=False)
                pe.matmul(o, lh, rl, start=False, stop=False)
                return pe.matmul(o, ll, rh, start=False, stop=last)

            def by_tokens(key, outs, ah, al):
                wh, wl = take(key)
                kt = wh.shape[1]
                for t in range(NT):
                    for k in range(kt):
                        tok = slice(t * P, (t + 1) * P)
                        ins = product(outs[t], ah[:, k, tok], al[:, k, tok], wh[:, k, :], wl[:, k, :],
                                      k == 0, k == kt - 1)
                ins.then_inc(tile_done, 1)

            def by_features(key, bank, ah, al):
                wh, wl = take(key)
                kt = wh.shape[1]
                for ch in range(TC // P):
                    for k in range(kt):
                        cols = slice(ch * P, (ch + 1) * P)
                        ins = product(bank[:, ch, :], wh[:, k, cols], wl[:, k, cols], ah[:, k, :], al[:, k, :],
                                      k == 0, k == kt - 1)
                ins.then_inc(tile_done, 1)

            def norm_turns(key, ps=psw):
                x = norms[key]
                for b in range(4):
                    for kk in range(2):
                        for t in range(NT):
                            if b == 0 and kk == 0:
                                pe.wait_ge(ln_xn, NT * x["n"] + t + 1)
                            k = 2 * b + kk
                            ins = pe.transpose(ps[:, b, kk * S + t * P:kk * S + (t + 1) * P],
                                               y[:, t, k * P:(k + 1) * P], ident[:])
                    ins.then_inc(ln_turned, 1)

            def wait_norm(key):
                pe.wait_ge(xT_ready, 4 * (norms[key]["nt"] + 1))

            def attention(block, l, qT, kT, v, ready=lambda kind, t: None):
                first = 2 * unit0(block, l)
                count = 2 * sum(1 for x in units if x[0] == block and x[1] == l)
                for i in range(first, first + count + 2):
                    if i < first + count:
                        u, hf = divmod(i, 2)
                        kind, t = units[u][2:]
                        nk = (t + 1) * P
                        ready(kind, t)
                        if i >= 2:
                            pe.wait_ge(smax_done, i - 1)
                        for b in range(2):
                            for a in range(2):
                                h = a * 4 + hf * 2 + b
                                ins = pe.matmul(psw[:, 2 * (i % 2) + a, b * S:b * S + nk],
                                                qT(kind, h, t), kT(kind, h, nk), start=True, stop=True)
                        ins.then_inc(scores_done, 1)
                    if i - 2 >= first:
                        n = i - 2
                        u, hf = divmod(n, 2)
                        kind, t = units[u][2:]
                        pe.wait_ge(pt_ready, chunk0[n + 1])
                        if hf == 0 and u >= 2:
                            pe.wait_ge(o_ready, u - 1)
                        blk = [(b, a, kb) for b in range(2) for a in range(2) for kb in range(t + 1)]
                        for q, (b, a, kb) in enumerate(blk):
                            h = a * 4 + hf * 2 + b
                            m = chunk0[n] + q // 4
                            ins = pe.matmul(psa[:, 2 + u % 2, h * DH:(h + 1) * DH],
                                            pt[:, m % 4, (q % 4) * P:(q % 4 + 1) * P], v(kind, h, kb),
                                            start=(kb == 0), stop=(kb == t))
                        ins.then_inc(pv_done, 1)
                    if first <= i - 1 < first + count:
                        n = i - 1
                        u, hf = divmod(n, 2)
                        kind, t = units[u][2:]
                        pe.wait_ge(exp_done, n + 1)
                        blk = [(b, a, kb) for b in range(2) for a in range(2) for kb in range(t + 1)]
                        for q, (b, a, kb) in enumerate(blk):
                            h = a * 4 + hf * 2 + b
                            m = chunk0[n] + q // 4
                            if q % 4 == 0 and m >= 2:
                                pe.wait_ge(pt_ready, m - 1)
                            ins = pe.transpose(psa[:, m % 2, (q % 4) * P:(q % 4 + 1) * P],
                                               soft[:, u % 2, h, kb * P:(kb + 1) * P], ident[:])
                            if q % 4 == 3:
                                ins.then_inc(pt_done, 1)

            def mix_turns(e):
                for b in range(4):
                    for kk in range(2):
                        for t in range(NT):
                            k = 2 * b + kk
                            ins = pe.transpose(psw[:, b, kk * S + t * P:kk * S + (t + 1) * P],
                                               omix[:, t, k * P:(k + 1) * P], ident[:])
                    ins.then_inc(opT_turned, 1)

            def ffn(block, l, f0):
                for s in range(FS + 1):
                    f = f0 + s
                    if s < FS:
                        if f >= 2:
                            pe.wait_ge(hid_ready, f - 1)
                        by_features((block, "g", l, s), bank2(psw, 2 * (f % 2)), xhi, xlo)
                        by_features((block, "u", l, s), bank2(psw, 2 * (f % 2) + 1), xhi, xlo)
                    if s >= 1:
                        g = f - 1
                        pe.wait_ge(hid_ready, g + 1)
                        wh, wl = take((block, "d", l, s - 1))
                        for t in range(NT):
                            for half in range(2):
                                for kk in range(2):
                                    tok = slice(t * P, (t + 1) * P)
                                    col = slice(half * 512, (half + 1) * 512)
                                    ins = product(psa[:, 2 * t + half, :], hidh[:, g % 2, kk, tok],
                                                  hidl[:, g % 2, kk, tok], wh[:, kk, col], wl[:, kk, col],
                                                  s == 1 and kk == 0, s == FS and kk == 1)
                        ins.then_inc(tile_done, 1)

            pe.wait_ge(consts_loaded, 16 * n_const_dmas)
            pe.wait_ge(params_loaded, 16 * n_param_dmas)
            for j, n in enumerate(param_rows):
                ins = pe.transpose(psa[:, j // 4, (j % 4) * P:(j % 4) * P + n], prow[0:n, j, :], ident[0:n, 0:n])
            ins.then_inc(params_turned, 1)
            norm_turns((1, "in", 0))

            for l in range(L):
                pe.wait_ge(p_loaded, 16 * (l + 1))
                if l == 0:
                    pe.wait_ge(params_ready, 1)
                for kk in range(2):
                    for t in range(NT):
                        ins = pe.transpose(psa[:, 0, kk * S + t * P:kk * S + (t + 1) * P],
                                           ptok[:, t, kk * P:(kk + 1) * P], ident[:])
                ins.then_inc(p_turned, 1)
                pe.wait_ge(p_ready, l + 1)
                wh, wl = take((1, "pp", l, 0))
                for k4 in range(4):
                    for t in range(NT):
                        for kk in range(2):
                            tok = slice(t * P, (t + 1) * P)
                            col = slice(k4 * TC, (k4 + 1) * TC)
                            ins = product(bank2(psa, k4)[:, t, :], pT_hi[:, kk, tok], pT_lo[:, kk, tok],
                                          wh[:, kk, col], wl[:, kk, col], kk == 0, kk == 1)
                ins.then_inc(tile_done, 1)
                wait_norm((1, "in", 0) if l == 0 else (1, "2", l - 1))
                for q, k in enumerate(IN1_ORDER):
                    if q >= 4:
                        pe.wait_ge(proj_ready, 7 * l + q - 3)
                    cols = min(TC, IN1 - k * TC)
                    bank = bank2(psw, q % 4)
                    by_tokens((1, "in", l, k), [bank[:, t, 0:cols] for t in range(NT)], xhi, xlo)
                groups = [(10, 11), (12,), (5, 6), (7, 8), (9,), (0, 1), (2, 3), (4,)]
                pe.wait_ge(pp_ready, 4 * (l + 1))
                for q, grp in enumerate(groups):
                    g = 8 * l + q
                    if q == 0:
                        pe.wait_ge(qki_roped, NT * (l + 1))
                    if q == 2:
                        pe.wait_ge(heads_ready, 8 * l + 2)
                        pe.wait_ge(proj_ready, 7 * (l + 1))
                        for t in range(NT):
                            nk = (t + 1) * P
                            if t == 1:
                                pe.wait_ge(relu_done, NT * l + 1)
                            for h in range(H):
                                pr = slice(32 * (h % 4), 32 * (h % 4) + 32)
                                ins = pe.matmul(psw[:, h % 4, (h // 4) * S:(h // 4) * S + nk],
                                                headT[pr, 10 + h // 4, t * P:(t + 1) * P], headT[pr, 12, 0:nk],
                                                start=True, stop=True)
                            ins.then_inc(iscores_done, 1)
                        pe.wait_ge(qkb_roped, NT * (l + 1))
                    if q == 5:
                        pe.wait_ge(qka_roped, NT * (l + 1))
                    if q >= 4:
                        pe.wait_ge(heads_ready, g - 3)
                    for j, b in enumerate(grp):
                        for t in range(NT):
                            ins = pe.transpose(psa[:, q % 4, j * S + t * P:j * S + (t + 1) * P],
                                               roped[:, t, b * P:(b + 1) * P], ident[:])
                    ins.then_inc(heads_turned, 1)
                pe.wait_ge(heads_ready, 8 * (l + 1))
                pe.wait_ge(relu_done, NT * (l + 1))
                b0 = {SWA: 0, DSA: 5}
                attention(
                    1, l,
                    lambda kind, h, t: headT[64 * (h // 4):64 * (h // 4) + 64, b0[kind] + h % 4, t * P:(t + 1) * P],
                    lambda kind, h, nk: headT[64 * (h // 4):64 * (h // 4) + 64, b0[kind] + 4, 0:nk],
                    lambda kind, h, kb: (proj1[:, kb, VA + DH * (h // 4):VA + DH * (h // 4) + DH] if kind == SWA
                                         else proj1[:, kb, VB:VB + DH]))
                pe.wait_ge(o_ready, unit0(1, l) + 4)
                mix_turns(l)
                pe.wait_ge(opT_ready, 4 * (l + 1))
                for k in range(4):
                    bank = bank2(psw, k)
                    by_tokens((1, "o", l, k), [bank[:, t, :] for t in range(NT)], xhi, xlo)
                norm_turns((1, "1", l))
                wait_norm((1, "1", l))
                for k in range(4):
                    bank = bank2(psw, k)
                    by_tokens((1, "pg", l, k), [bank[:, t, :] for t in range(NT)], xhi, xlo)
                pe.wait_ge(pg_exp, 4 * (l + 1))
                ffn(1, l, FS * l)
                if l + 1 < L:
                    norm_turns((1, "2", l))

            norm_turns((2, "in", 0))
            for l in range(L):
                wait_norm((2, "in", 0) if l == 0 else (2, "3", l - 1))
                for k in range(8):
                    if k >= 4:
                        pe.wait_ge(proj2_ready, 8 * l + k - 3)
                    cols = min(TC, IN2 - k * TC)
                    bank = bank2(psw, k % 4)
                    by_tokens((2, "in", l, k), [bank[:, t, 0:cols] for t in range(NT)], xhi, xlo)
                    if l == 0 and k == 5:
                        norm_turns((2, "mem", 0), psa)
                pe.wait_ge(c_normed, l + 1)
                if l == 0:
                    wait_norm((2, "mem", 0))
                for b in range(3):
                    for kk in range(2 if b < 2 else 1):
                        for t in range(NT):
                            k = 2 * b + kk
                            ins = pe.transpose(psa[:, b, kk * S + t * P:kk * S + (t + 1) * P],
                                               proj2[:, t, k * P:(k + 1) * P], ident[:])
                    ins.then_inc(c_turned, 1)
                pe.wait_ge(cT_ready, 3 * (l + 1))
                pe.wait_ge(proj2_ready, 8 * (l + 1))
                for j in range(2):
                    by_tokens((2, "uq", l, j), [psw[:, 2 * j + t, 0:384] for t in range(NT)],
                              cT_hi[:, 0:3, :], cT_lo[:, 0:3, :])
                for q in range(5):
                    if q == 0:
                        pe.wait_ge(kd_ready, 2 * l + 1)
                    if q == 3:
                        pe.wait_ge(kd_ready, 2 * l + 2)
                    if q == 4:
                        pe.wait_ge(nsa_ready, 5 * l + 1)
                    for kk in range(2):
                        for t in range(NT):
                            if q < 2:
                                src = nqp[:, t, (2 * q + kk) * P:(2 * q + kk + 1) * P]
                            elif q == 2:
                                c0 = (KSL, KWN)[kk]
                                src = proj2[:, t, c0:c0 + P]
                            else:
                                src = kdup[:, t, 2 * (q - 3) + kk, :, :].rearrange("p e d -> p (e d)")
                            ins = pe.transpose(psa[:, q % 4, kk * S + t * P:kk * S + (t + 1) * P], src, ident[:])
                    ins.then_inc(nsa_turned, 1)
                pe.wait_ge(qm_ready, 2 * (l + 1))
                wh, wl = take((2, "ukv", l, 0))
                for t in range(NT):
                    for half in range(2):
                        for kk in range(2):
                            tok = slice(t * P, (t + 1) * P)
                            col = slice(half * 512, (half + 1) * 512)
                            ins = product(psw[:, 2 * t + half, :], cT_hi[:, 3 + kk, tok], cT_lo[:, 3 + kk, tok],
                                          wh[:, kk, col], wl[:, kk, col], kk == 0, kk == 1)
                ins.then_inc(tile_done, 1)
                pe.wait_ge(qm_roped, l + 1)
                pe.wait_ge(nsa_ready, 5 * (l + 1))
                for b in range(4):
                    for kk in range(2):
                        for t in range(NT):
                            h = 2 * b + kk
                            ins = pe.transpose(psa[0:MD, b, kk * S + t * P:kk * S + (t + 1) * P],
                                               qm[:, t, h * MD:(h + 1) * MD], ident[:])
                    ins.then_inc(mla_turned, 1)
                pe.wait_ge(kvm_ready, l + 1)
                for i in range(2):
                    pe.wait_ge(cmp_x, 2 * l + i + 1)
                    wh, wl = take((2, "w1", l, i))
                    for j in range(16):
                        ins = product(psw[:, i, 0:2 * NC], wh[:, j, :], wl[:, j, :], cx_hi[i][:, j, :],
                                      cx_lo[i][:, j, :], j == 0, j == 15)
                    ins.then_inc(tile_done, 1)
                pe.wait_ge(km_roped, l + 1)
                for b in range(4):
                    pe.wait_ge(mla_ready, 8 * l + b + 1)
                    for kk in range(2):
                        for t in range(NT):
                            h = 2 * b + kk
                            ins = pe.transpose(psa[0:MD, b, kk * S + t * P:kk * S + (t + 1) * P],
                                               kvm[:, t, h, DH:KVW], ident[:])
                    ins.then_inc(mla_turned, 1)
                pe.wait_ge(cmp_gelu, 2 * (l + 1))
                for gr in range(2):
                    pe.matmul(psw[64 * gr:64 * gr + 64, 2, 0:NC], w2s[:, l, 0, :],
                              hcmp[:, 0, gr * NC:(gr + 1) * NC], start=True, stop=True)
                for gr in range(2):
                    for i in range(4):
                        ins = pe.matmul(psw[32 * i:32 * i + NC, 3, gr * DH:(gr + 1) * DH],
                                        hcmp[:, 1, gr * NC:(gr + 1) * NC], w2s[:, l, 1, :], start=True, stop=True)
                ins.then_inc(cmp_kv, 1)
                pe.wait_ge(cmp_kv_ready, l + 1)
                for t in range(NT):
                    for r in range(4):
                        for a in range(2):
                            ins = pe.matmul(psw[:, a, t * 64 + r * 16:t * 64 + (r + 1) * 16],
                                            nsaT[64 * a:64 * a + 64, r, t * P:(t + 1) * P],
                                            kct[64 * a:64 * a + 64, :], start=True, stop=True)
                ins.then_inc(cmp_scores, 1)
                pe.wait_ge(cmp_exp, l + 1)
                pe.wait_ge(mla_ready, 8 * (l + 1))
                for t in range(NT):
                    for gr in range(2):
                        ins = pe.transpose(psa[:, 0, (2 * t + gr) * P:(2 * t + gr + 1) * P],
                                           pcmp[:, t, 4 * gr:4 * gr + 4, :].rearrange("p h n -> p (h n)"), ident[:])
                ins.then_inc(cmp_turned, 1)
                pe.wait_ge(cmp_pT, l + 1)
                for t in range(NT):
                    for gr in range(2):
                        ins = pe.matmul(psw[:, 2 + t, gr * S:(gr + 1) * S], pcT[:, 2 * t + gr, :], vbd[:, gr, :],
                                        start=True, stop=True)
                ins.then_inc(cmp_pv, 1)
                pe.wait_ge(cmp_o, l + 1)
                kblock = {SLC: 4, WIN: 5}
                vcol = {SLC: VSL, WIN: VWN}
                attention(
                    2, l,
                    lambda kind, h, t: (mqT[0:MD, h, t * P:(t + 1) * P] if kind == MLA else
                                        nsaT[64 * (h // 4):64 * (h // 4) + 64, h % 4, t * P:(t + 1) * P]),
                    lambda kind, h, nk: (mkT[0:MD, h, 0:nk] if kind == MLA else
                                         nsaT[64 * (h // 4):64 * (h // 4) + 64, kblock[kind], 0:nk]),
                    lambda kind, h, kb: (kvm[:, kb, h, 0:DH] if kind == MLA else
                                         proj2[:, kb, vcol[kind] + DH * (h // 4):vcol[kind] + DH * (h // 4) + DH]))
                pe.wait_ge(o_ready, unit0(2, l) + 6)
                mix_turns(2 + 2 * l)
                pe.wait_ge(opT_ready, 4 * (3 + 2 * l))
                for k in range(4):
                    bank = bank2(psw, k)
                    by_tokens((2, "out", l, k), [bank[:, t, :] for t in range(NT)], xhi, xlo)

                def memory_product(k):
                    if k >= 4:
                        pe.wait_ge(kv_ready, 8 * l + k - 3)
                    bank = bank2(psa, k % 4)
                    if k < 4:
                        by_features((2, "kv", l, k), bank, memhi, memlo)
                    else:
                        by_tokens((2, "kv", l, k), [bank[:, t, :] for t in range(NT)], memhi, memlo)
                for k in range(2):
                    memory_product(k)
                norm_turns((2, "1", l))
                for k in range(2, 8):
                    memory_product(k)
                wait_norm((2, "1", l))
                for k in range(4):
                    by_features((2, "xq", l, k), bank2(psw, k), xhi, xlo)
                pe.wait_ge(xq_ready, 4 * (l + 1))
                pe.wait_ge(kv_ready, 8 * (l + 1))
                for t in range(NT):
                    for h in range(4):
                        for kk in range(2):
                            ins = pe.matmul(psw[:, 2 * t + h // 2, (h % 2) * S:(h % 2 + 1) * S],
                                            xqT[:, 2 * h + kk, t * P:(t + 1) * P], xkT[:, 2 * h + kk, :],
                                            start=(kk == 0), stop=(kk == 1))
                    ins.then_inc(xs_done, 1)
                for t in range(NT):
                    pe.wait_ge(xp_ready, NT * l + t + 1)
                    for h in range(4):
                        for m in range(2):
                            ins = pe.transpose(psa[:, h, m * S + t * P:m * S + (t + 1) * P],
                                               xsoft[:, t, h, m * P:(m + 1) * P], ident[:])
                        if t == 1:
                            ins.then_inc(xp_turned, 1)
                for h in range(4):
                    pe.wait_ge(xpT_ready, 4 * l + h + 1)
                    for ch in range(2):
                        for m in range(2):
                            f = 2 * h + ch
                            ins = pe.matmul(psw[:, h, ch * S:(ch + 1) * S], xvt[:, m, f * P:(f + 1) * P],
                                            pt[:, h, m * S:(m + 1) * S], start=(m == 0), stop=(m == 1))
                    ins.then_inc(opT_turned, 1)
                pe.wait_ge(opT_ready, 4 * (4 + 2 * l))
                for k in range(4):
                    bank = bank2(psw, k)
                    by_tokens((2, "xo", l, k), [bank[:, t, :] for t in range(NT)], xhi, xlo)
                norm_turns((2, "2", l))
                wait_norm((2, "2", l))
                ffn(2, l, FS * (L + l))
                if l + 1 < L:
                    norm_turns((2, "3", l))

        @block.scalar
        def _(act):
            nxt = [0]

            def split(i):
                act.wait_ge(tile_loaded[i % NRAW], 16 * (i // NRAW + 1))
                if i >= NW:
                    act.wait_ge(tile_done, i - NW + 1)
                nc.scalar.activation(tile_flat(whi, NW, i), tile_flat(raw, NRAW, i), ACT.Copy).then_inc(hi_ready, 1)

            def serve(key):
                while nxt[0] <= min(ti[key] + NW, n_tiles - 1):
                    split(nxt[0])
                    nxt[0] += 1

            def norm_evac(key, ps=psw):
                x = norms[key]
                j, c0 = x["pc"]
                for b in range(4):
                    act.wait_ge(ln_turned, 4 * x["nt"] + b + 1)
                    for kk in range(2):
                        k = 2 * b + kk
                        ins = nc.scalar.activation(xv[:, k, :], ps[:, b, kk * S:(kk + 1) * S], ACT.Identity,
                                                   bias=pcol[:, j, c0 + KD + k:c0 + KD + k + 1],
                                                   scale=pcol[:, j, c0 + k:c0 + k + 1])
                    ins.then_inc(ln_v, 1)

            def attention(block, l):
                first = 2 * unit0(block, l)
                count = 2 * sum(1 for x in units if x[0] == block and x[1] == l)
                for i in range(first, first + count + 1):
                    if i < first + count:
                        u, hf = divmod(i, 2)
                        kind, t = units[u][2:]
                        nk = (t + 1) * P
                        act.wait_ge(smax_done, i + 1)
                        if kind == SWA:
                            hs = esink[:, u % 2, 1, :].rearrange("p (a q) -> p a q", a=2)[:, :, 2 * hf:2 * hf + 2]
                            nc.scalar.activation(hs, esink[:, u % 2, 0, :].rearrange(
                                "p (a q) -> p a q", a=2)[:, :, 2 * hf:2 * hf + 2], ACT.Exp)
                        for b in range(2):
                            for a in range(2):
                                h = a * 4 + hf * 2 + b
                                ins = nc.scalar.activation(soft[:, u % 2, h, 0:nk], soft[:, u % 2, h, 0:nk], ACT.Exp,
                                                           bias=nmx[:, u % 2, h:h + 1], scale=1.0,
                                                           accum_out=den[:, u % 2, h:h + 1])
                        ins.then_inc(exp_done, 1)
                    if i - 1 >= first:
                        n = i - 1
                        for m in range(chunk0[n], chunk0[n + 1]):
                            act.wait_ge(pt_done, m + 1)
                            if m >= 4:
                                owner = max(x for x in range(len(chunk0) - 1) if chunk0[x] <= m - 4)
                                act.wait_ge(pv_done, owner + 1)
                            nc.scalar.activation(pt[:, m % 4, :], psa[:, m % 2, :], ACT.Copy).then_inc(pt_ready, 1)

            def opT_evac(e):
                for b in range(4):
                    act.wait_ge(opT_turned, 4 * e + b + 1)
                    nc.scalar.activation(xhi[:, 2 * b:2 * b + 2, :], bank2(psw, b), ACT.Copy).then_inc(opT_hi, 1)

            for dst, src in const_dmas:
                act.dma_start(dst, src).then_inc(consts_loaded, 16)
            for dst, src in param_dmas:
                act.dma_start(dst, src).then_inc(params_loaded, 16)
            act.wait_ge(angles_ready, 1)
            nc.scalar.activation(angs[:, 4:6, :], angs[:, 4:6, :], ACT.Sin).then_inc(sines_ready, 1)
            for i in range(NW):
                split(i)
            nxt[0] = NW
            act.wait_ge(params_turned, 1)
            for j, n in enumerate(param_rows):
                ins = nc.scalar.activation(pcol[:, j, 0:n], psa[:, j // 4, (j % 4) * P:(j % 4) * P + n], ACT.Copy)
            ins.then_inc(params_ready, 1)
            act.wait_ge(params_ready, 1)
            norm_evac((1, "in", 0))

            for l in range(L):
                act.wait_ge(p_turned, l + 1)
                nc.scalar.activation(pT_hi, bank2(psa, 0), ACT.Copy).then_inc(p_hi, 1)
                act.wait_ge(tile_done, ti[(1, "pp", l, 0)] + 1)
                for k4 in range(4):
                    nc.scalar.activation(ple[:, :, k4 * TC:(k4 + 1) * TC], bank2(psa, k4),
                                         ACT.Copy).then_inc(pp_ready, 1)
                serve((1, "pp", l, 0))
                for q, k in enumerate(IN1_ORDER):
                    cols = min(TC, IN1 - k * TC)
                    act.wait_ge(tile_done, ti[(1, "in", l, k)] + 1)
                    nc.scalar.activation(proj1[:, :, k * TC:k * TC + cols], bank2(psw, q % 4)[:, :, 0:cols],
                                         ACT.Copy).then_inc(proj_ready, 1)
                    serve((1, "in", l, k))
                for q, grp in enumerate([(10, 11), (12,), (5, 6), (7, 8), (9,), (0, 1), (2, 3), (4,)]):
                    if q == 2:
                        act.wait_ge(x_ready, norms[(1, "in", 0) if l == 0 else (1, "2", l - 1)]["nx"] + 1)
                        for t in range(NT):
                            nk = (t + 1) * P
                            act.wait_ge(iscores_done, NT * l + t + 1)
                            if t == 1:
                                act.wait_ge(icomb_done, NT * l + 1)
                            for j in range(4):
                                ins = nc.scalar.activation(relu[:, j:8:4, 0:nk], bank2(psw, j)[:, :, 0:nk], ACT.Relu)
                            ins.then_inc(relu_done, 1)
                    act.wait_ge(heads_turned, 8 * l + q + 1)
                    nb = len(grp)
                    nc.scalar.activation(headT[:, grp[0]:grp[0] + nb, :], bank2(psa, q % 4)[:, 0:nb, :],
                                         ACT.Copy).then_inc(heads_ready, 1)
                attention(1, l)
                opT_evac(l)
                for k in range(4):
                    serve((1, "o", l, k))
                norm_evac((1, "1", l))
                for k in range(4):
                    act.wait_ge(tile_done, ti[(1, "pg", l, k)] + 1)
                    if k == 0:
                        act.wait_ge(o_ready, unit0(1, l) + 4)
                    nc.scalar.activation(egate[:, k, :], psw[:, k, :], ACT.Exp, scale=-1.0).then_inc(pg_exp, 1)
                    serve((1, "pg", l, k))
                for s in range(FS + 1):
                    f = FS * l + s
                    if s < FS:
                        serve((1, "g", l, s))
                        if f >= 2:
                            act.wait_ge(hid_ready, f - 1)
                        act.wait_ge(tile_done, ti[(1, "g", l, s)] + 1)
                        nc.scalar.activation(gact[:, f % 2, :], psw[:, 2 * (f % 2), :],
                                             ACT.Silu).then_inc(gate_ready, 1)
                        serve((1, "u", l, s))
                    if s >= 1:
                        serve((1, "d", l, s - 1))
                if l + 1 < L:
                    norm_evac((1, "2", l))

            norm_evac((2, "in", 0))
            for l in range(L):
                x_in = norms[(2, "in", 0) if l == 0 else (2, "3", l - 1)]["nx"]
                for k in range(8):
                    cols = min(TC, IN2 - k * TC)
                    act.wait_ge(tile_done, ti[(2, "in", l, k)] + 1)
                    nc.scalar.activation(proj2[:, :, k * TC:k * TC + cols], bank2(psw, k % 4)[:, :, 0:cols],
                                         ACT.Copy).then_inc(proj2_ready, 1)
                    serve((2, "in", l, k))
                    if l == 0 and k == 5:
                        norm_evac((2, "mem", 0), psa)
                for b in range(3):
                    act.wait_ge(c_turned, 3 * l + b + 1)
                    for kk in range(2 if b < 2 else 1):
                        k = 2 * b + kk
                        row = cqg_row(l) + k if k < 3 else ckvg_row(l) + k - 3
                        ins = nc.scalar.activation(ctmp[:, k, :], psa[:, b, kk * S:(kk + 1) * S], ACT.Copy,
                                                   scale=pcol[:, 2, row:row + 1])
                    ins.then_inc(c_v, 1)
                act.wait_ge(proj2_ready, 8 * (l + 1))
                nc.scalar.activation(gates[:], proj2[:, :, GL:IN2], ACT.Exp, scale=-1.0).then_inc(gate_exp, 1)
                for j in range(2):
                    act.wait_ge(tile_done, ti[(2, "uq", l, j)] + 1)
                    nc.scalar.activation(qm[:, :, j * 384:(j + 1) * 384], psw[:, 2 * j:2 * j + 2, 0:384],
                                         ACT.Copy).then_inc(qm_ready, 1)
                    serve((2, "uq", l, j))
                act.wait_ge(x_ready, x_in + 1)
                for q in range(5):
                    act.wait_ge(nsa_turned, 5 * l + q + 1)
                    if q < 3:
                        nc.scalar.activation(nsaT[:, 2 * q:2 * q + 2, :], bank2(psa, q), ACT.Copy).then_inc(nsa_ready, 1)
                    else:
                        i = 2 * (q - 3)
                        nc.scalar.activation(cx[0:64, i:i + 2, :], bank2(psa, q % 4)[0:64], ACT.Copy)
                        nc.scalar.activation(cx[64:128, i:i + 2, 0:S - 1], bank2(psa, q % 4)[64:128, :, 1:S],
                                             ACT.Copy).then_inc(nsa_ready, 1)
                act.wait_ge(tile_done, ti[(2, "ukv", l, 0)] + 1)
                for t in range(NT):
                    kv = psw[:, 2 * t:2 * t + 2, :].rearrange("p b (h c) -> p (b h) c", h=4)
                    nc.scalar.activation(kvm[:, t, :, 0:DH], kv[:, :, DH:P], ACT.Copy)
                    ins = nc.scalar.activation(kvm[:, t, :, DH:P], kv[:, :, 0:DH], ACT.Copy)
                ins.then_inc(kvm_ready, 1)
                serve((2, "ukv", l, 0))
                for b in range(4):
                    act.wait_ge(mla_turned, 8 * l + b + 1)
                    nc.scalar.activation(mqT[0:MD, 2 * b:2 * b + 2, :], bank2(psa, b)[0:MD], ACT.Copy).then_inc(mla_ready, 1)
                for i in range(2):
                    act.wait_ge(tile_done, ti[(2, "w1", l, i)] + 1)
                    row = b1_row(l, i)
                    nc.scalar.activation(hcmp[:, i, :], psw[:, i, 0:2 * NC], ACT.Gelu_apprx_tanh,
                                         bias=pcol[:, 2, row:row + 1]).then_inc(cmp_gelu, 1)
                    serve((2, "w1", l, i))
                for b in range(4):
                    act.wait_ge(mla_turned, 8 * l + b + 5)
                    nc.scalar.activation(mkT[0:MD, 2 * b:2 * b + 2, :], bank2(psa, b)[0:MD], ACT.Copy).then_inc(mla_ready, 1)
                act.wait_ge(cmp_shifted, l + 1)
                nc.scalar.activation(pcmp[:, :, :, 0:16].rearrange("p t h n -> p (t h) n"),
                                     scmp.rearrange("p t (h n) -> p (t h) n", h=H), ACT.Exp).then_inc(cmp_exp, 1)
                act.wait_ge(cmp_turned, l + 1)
                nc.scalar.activation(pcT, psa[:, 0, :].rearrange("p (j q) -> p j q", j=4), ACT.Copy).then_inc(cmp_pT, 1)
                attention(2, l)
                opT_evac(2 + 2 * l)
                for k in range(4):
                    serve((2, "out", l, k))

                def memory_evac(k):
                    act.wait_ge(tile_done, ti[(2, "kv", l, k)] + 1)
                    if k < 4:
                        nc.scalar.activation(xkT[:, 2 * k:2 * k + 2, :], bank2(psa, k % 4), ACT.Copy).then_inc(kv_ready, 1)
                    else:
                        nc.scalar.activation(xvt[:, :, (k - 4) * TC:(k - 3) * TC], bank2(psa, k % 4),
                                             ACT.Copy).then_inc(kv_ready, 1)
                    serve((2, "kv", l, k))
                for k in range(2):
                    memory_evac(k)
                norm_evac((2, "1", l))
                for k in range(2, 8):
                    memory_evac(k)
                for k in range(4):
                    act.wait_ge(tile_done, ti[(2, "xq", l, k)] + 1)
                    nc.scalar.activation(xqT[:, 2 * k:2 * k + 2, :], bank2(psw, k), ACT.Copy).then_inc(xq_ready, 1)
                    serve((2, "xq", l, k))
                for t in range(NT):
                    act.wait_ge(xmax_done, NT * l + t + 1)
                    for h in range(4):
                        ins = nc.scalar.activation(xsoft[:, t, h, :], psw[:, 2 * t + h // 2, (h % 2) * S:(h % 2 + 1) * S],
                                                   ACT.Exp, bias=xmx[:, t, h:h + 1], scale=1 / 16,
                                                   accum_out=xden[:, t, h:h + 1])
                    ins.then_inc(xexp_done, 1)
                for h in range(4):
                    act.wait_ge(xp_turned, 4 * l + h + 1)
                    nc.scalar.activation(pt[:, h, :], psa[:, h, :], ACT.Copy).then_inc(xpT_ready, 1)
                opT_evac(3 + 2 * l)
                for k in range(4):
                    serve((2, "xo", l, k))
                norm_evac((2, "2", l))
                for s in range(FS + 1):
                    f = FS * (L + l) + s
                    if s < FS:
                        for name, buf, bank, ch0 in (("g", conv_g, 2 * (f % 2), 22 + 2 * s),
                                                     ("u", conv_a, 2 * (f % 2) + 1, 2 * s)):
                            act.wait_ge(tile_done, ti[(2, name, l, s)] + 1)
                            if f >= 2:
                                act.wait_ge(hid_ready, f - 1)
                            for ch in range(2):
                                cc = ch0 + ch
                                ins = nc.scalar.activation(buf[:, f % 2, ch, :], bank2(psw, bank)[:, ch, :],
                                                           ACT.Identity, scale=pcol[:, 4 + 2 * l, cc:cc + 1],
                                                           bias=pcol[:, 4 + 2 * l, 44 + cc:45 + cc])
                            ins.then_inc(conv_first, 1)
                            serve((2, name, l, s))
                        act.wait_ge(conv_done, FS * l + s + 1)
                        nc.scalar.activation(gact[:, f % 2, :], conv_g[:, f % 2].rearrange("p c s -> p (c s)"),
                                             ACT.Silu).then_inc(gate_ready, 1)
                    if s >= 1:
                        serve((2, "d", l, s - 1))
                if l + 1 < L:
                    norm_evac((2, "3", l))
            for t in range(NT):
                act.wait_ge(x_ready, len(tok_norms) + t)
                act.dma_start(out[0, t * P:(t + 1) * P, :], y[:, t, :]).then_inc(stored, 16)
            act.wait_ge(stored, 16 * NT)

        @block.vector
        def _(dve):
            nxt = [0]
            v = nc.vector

            def split(i):
                dve.wait_ge(hi_ready, i + 1)
                v.tensor_tensor(tile_flat(wlo, NW, i), tile_flat(raw, NRAW, i), tile_flat(whi, NW, i).bitcast(F32),
                                ALU.subtract).then_inc(lo_ready, 1)

            def serve(key):
                while nxt[0] <= min(ti[key] + NW, n_tiles - 1):
                    split(nxt[0])
                    nxt[0] += 1

            def norm_rows(key):
                x = norms[key]
                dve.drain()
                for t in range(NT):
                    for half in range(2):
                        v.bn_stats(stats[:, t, half, :], y[:, t, half * 512:(half + 1) * 512])
                dve.drain()
                for t in range(NT):
                    v.bn_aggr(meanvar[:, t, :], stats[:, t, :, :])
                dve.drain()
                v.tensor_scalar(vare[:, 0:NT], meanvar[:, :, 1], LN_EPS, None, ALU.add).then_inc(ln_var, 1)
                dve.wait_ge(ln_rstd, x["n"] + 1)
                for t in range(NT):
                    v.tensor_scalar(y[:, t, :], y[:, t, :], meanvar[:, t, 0:1], rstd[:, t:t + 1],
                                    ALU.subtract, ALU.mult).then_inc(ln_xn, 1)

            def norm_split(key, hi, lo):
                x = norms[key]
                for b in range(4):
                    ks = slice(2 * b, 2 * b + 2)
                    dve.wait_ge(ln_v, 4 * x["nt"] + b + 1)
                    v.tensor_copy(hi[:, ks, :], xv[:, ks, :])
                    dve.drain()
                    v.tensor_tensor(lo[:, ks, :], xv[:, ks, :], hi[:, ks, :].bitcast(F32),
                                    ALU.subtract).then_inc(xT_ready, 1)

            def norm_tokens(key):
                x = norms[key]
                dve.wait_ge(gb_loaded, 32 * (x["nx"] + 1))
                dve.drain()
                for t in range(NT):
                    v.tensor_tensor(y[:, t, :], y[:, t, :], gb[:, 0, :], ALU.mult)
                dve.drain()
                for t in range(NT):
                    ins = v.tensor_tensor(y[:, t, :], y[:, t, :], gb[:, 1, :], ALU.add)
                    if x["n"] == len(norms) - 1:
                        ins.then_inc(x_ready, 1)
                if x["n"] < len(norms) - 1:
                    ins.then_inc(x_ready, 1)

            def rope(x, cos, sin, t1, t2, writes):
                nh, wd = x.shape[1], x.shape[2]
                hw = wd // 2
                v.tensor_tensor(t1, x, bc(cos, nh), ALU.mult)
                v.tensor_tensor(t2[:, :, 0:hw], x[:, :, hw:wd], bc(sin[:, 0:hw], nh), ALU.mult)
                v.tensor_tensor(t2[:, :, hw:wd], x[:, :, 0:hw], bc(sin[:, hw:wd], nh), ALU.mult)
                dve.drain()
                for o, sel in writes:
                    ins = v.tensor_tensor(o, sel(t1), sel(t2), ALU.add)
                return ins

            def attention(block, l, mask, scale, finish, before=lambda kind, t, hf: None):
                first = 2 * unit0(block, l)
                count = 2 * sum(1 for x in units if x[0] == block and x[1] == l)
                for i in range(first, first + count + 2):
                    if i < first + count:
                        u, hf = divmod(i, 2)
                        kind, t = units[u][2:]
                        nk = (t + 1) * P
                        before(kind, t, hf)
                        dve.wait_ge(scores_done, i + 1)
                        if u >= 2:
                            dve.wait_ge(pt_done, chunk0[2 * (u - 1)])
                        for b in range(2):
                            for a in range(2):
                                h = a * 4 + hf * 2 + b
                                v.tensor_tensor_reduce(
                                    out=soft[:, u % 2, h, 0:nk], in0=psw[:, 2 * (i % 2) + a, b * S:b * S + nk],
                                    in1=mask(kind, h, t), scale=scale[kind], scalar=LOWEST, op0=ALU.add, op1=ALU.max,
                                    accum_out=mx[:, u % 2, h:h + 1])
                        dve.drain()

                        def hs(x):
                            return x.rearrange("p (a q) -> p a q", a=2)[:, :, 2 * hf:2 * hf + 2]
                        m, nm = hs(mx[:, u % 2, :]), hs(nmx[:, u % 2, :])
                        if kind == SWA:
                            v.tensor_tensor(m, m, hs(sinkb[:, l, :]), ALU.max)
                            dve.drain()
                            v.tensor_tensor(hs(esink[:, u % 2, 0, :]), hs(sinkb[:, l, :]), m, ALU.subtract)
                        v.tensor_scalar(nm, m, -1.0, None, ALU.mult).then_inc(smax_done, 1)
                    if i - 2 >= first and (i - 2) % 2 == 1:
                        u = (i - 2) // 2
                        dve.wait_ge(pv_done, 2 * u + 2)
                        finish(u, units[u][2], units[u][3])

            def opT_split(e):
                for b in range(4):
                    dve.wait_ge(opT_hi, 4 * e + b + 1)
                    ks = slice(2 * b, 2 * b + 2)
                    v.tensor_tensor(xlo[:, ks, :], bank2(psw, b), xhi[:, ks, :].bitcast(F32),
                                    ALU.subtract).then_inc(opT_ready, 1)

            def residual(keys):
                for k, key in enumerate(keys):
                    dve.wait_ge(tile_done, ti[key] + 1)
                    cols = slice(k * TC, (k + 1) * TC)
                    v.scalar_tensor_tensor(out=y[:, :, cols], in0=xtok[:, :, cols], scalar=ALPHA, in1=bank2(psw, k),
                                           op0=ALU.mult, op1=ALU.add)
                    serve(key)

            v.memset(mhalf[:], -0.5).then_inc(mhalf_ready, 1)
            v.memset(kct[:], 0.0)
            v.memset(vbd[:], 0.0)
            dve.wait_ge(consts_loaded, 16 * n_const_dmas)
            v.tensor_copy(pos_f[:], pos_i[:])
            dve.drain()
            for t in range(NT):
                v.tensor_scalar(angs[:, 0, t * 32:(t + 1) * 32], inv[:], pos_f[:, t:t + 1], None, ALU.mult)
            dve.drain()
            whole = float(np.float32(1 / (2 * math.pi)))
            magic = 1.5 * 2.0 ** 23
            c1 = 6.28125
            c2 = float(np.float32(np.round((2 * math.pi - c1) * 2 ** 20) / 2 ** 20))
            c3 = float(np.float32(2 * math.pi - c1 - c2))
            v.tensor_scalar(angs[:, 1, :], angs[:, 0, :], whole, magic, ALU.mult, ALU.add)
            v.tensor_scalar(angs[:, 2, :], angs[:, 0, :], whole, 0.25, ALU.mult, ALU.add)
            dve.drain()
            v.tensor_scalar(angs[:, 2, :], angs[:, 2, :], magic, -magic, ALU.add, ALU.add)
            v.tensor_scalar(angs[:, 1, :], angs[:, 1, :], -magic, None, ALU.add)
            dve.drain()
            for j in range(2):
                src = angs[:, 0, :]
                for cc in (c1, c2, c3):
                    v.scalar_tensor_tensor(out=angs[:, 4 + j, :], in0=angs[:, 1 + j, :], scalar=-cc, in1=src,
                                           op0=ALU.mult, op1=ALU.add)
                    src = angs[:, 4 + j, :]
                    dve.drain()
            v.tensor_scalar(angs[:, 5, :], angs[:, 5, :], math.pi / 2, None, ALU.add)
            dve.drain()
            v.tensor_scalar(angs[:, 4:6, :], angs[:, 4:6, :], 3.1415925, -3.1415925, ALU.min,
                            ALU.max).then_inc(angles_ready, 1)
            dve.wait_ge(x_loaded, 16 * NT)
            norm_rows((1, "in", 0))
            dve.wait_ge(sines_ready, 1)
            sn = angs[:, 4, :].rearrange("p (t c) -> p t c", t=NT)
            cs = angs[:, 5, :].rearrange("p (t c) -> p t c", t=NT)
            for half in range(2):
                v.tensor_copy(cos64[:, :, 32 * half:32 * half + 32], cs)
                v.tensor_copy(cos32[:, :, 16 * half:16 * half + 16], cs[:, :, 0:32:2])
                v.tensor_scalar(sin64[:, :, 32 * half:32 * half + 32], sn, 2.0 * half - 1, None, ALU.mult)
                ins = v.tensor_scalar(sin32[:, :, 16 * half:16 * half + 16], sn[:, :, 0:32:2], 2.0 * half - 1, None,
                                      ALU.mult)
            ins.then_inc(tables_ready, 1)
            dve.drain()
            for i in range(NW):
                split(i)
            nxt[0] = NW
            norm_split((1, "in", 0), xhi, xlo)

            for l in range(L):
                dve.wait_ge(p_hi, l + 1)
                v.tensor_tensor(pT_lo, bank2(psa, 0), pT_hi.bitcast(F32), ALU.subtract).then_inc(p_ready, 1)
                serve((1, "pp", l, 0))
                t1 = sy[:, 0, 0:640]
                t2 = sy[:, 0, 640:1280]
                for q, k in enumerate(IN1_ORDER):
                    serve((1, "in", l, k))
                    if q == 1:
                        dve.wait_ge(proj_ready, 7 * l + 2)
                        for t in range(NT):
                            v.bn_stats(stats[:, t, 0, :], proj1[:, t, KI:KI + 32])
                        dve.drain()
                        for t in range(NT):
                            v.bn_aggr(meanvar[:, t, :], stats[:, t, 0:1, :])
                        dve.drain()
                        v.tensor_scalar(vare[:, 0:NT], meanvar[:, :, 1], LN_EPS, None, ALU.add).then_inc(ki_var, 1)
                        v.tensor_scalar(wi_s[:], proj1[:, :, WI:WI + H], 8 ** -0.5 * 32 ** -0.5, None, ALU.mult)
                        dve.wait_ge(ki_rstd, l + 1)
                        ki = proj1[:, :, KI:KI + 32]
                        for t in range(NT):
                            v.tensor_scalar(ki[:, t, :], ki[:, t, :], meanvar[:, t, 0:1], rstd[:, t:t + 1],
                                            ALU.subtract, ALU.mult)
                        dve.drain()
                        v.tensor_tensor(ki, ki, bc(ikg[:, l, 0, :], NT), ALU.mult)
                        dve.drain()
                        v.tensor_tensor(ki, ki, bc(ikg[:, l, 1, :], NT), ALU.add)
                        dve.drain()
                    if q == 2:
                        for t in range(NT):
                            x = proj1[:, t, QI:QI + 288].rearrange("p (h d) -> p h d", h=9)
                            a = t1[:, 0:288].rearrange("p (h d) -> p h d", h=9)
                            b = t2[:, 0:288].rearrange("p (h d) -> p h d", h=9)
                            rope(x, cos32[:, t, :], sin32[:, t, :], a, b, [
                                (roped[:, t, 10 * P:12 * P].rearrange("p (h d) -> p h d", h=8), lambda z: z[:, 0:8, :]),
                                (roped[:, t, 12 * P:13 * P].rearrange("p (h d) -> p h d", h=4),
                                 lambda z: z[:, 8:9, :].broadcast_to([P, 4, 32]))]).then_inc(qki_roped, 1)
                            dve.drain()
                    if q == 4:
                        dve.wait_ge(proj_ready, 7 * l + 4)
                        for t in range(NT):
                            x = proj1[:, t, QB:QB + 576].rearrange("p (h d) -> p h d", h=9)
                            a = t1[:, 0:576].rearrange("p (h d) -> p h d", h=9)
                            b = t2[:, 0:576].rearrange("p (h d) -> p h d", h=9)
                            rope(x, cos64[:, t, :], sin64[:, t, :], a, b, [
                                (roped[:, t, 5 * P:9 * P].rearrange("p (r a d) -> p a r d", a=2, d=DH),
                                 lambda z: z[:, 0:8, :].rearrange("p (a r) d -> p a r d", a=2)),
                                (roped[:, t, 9 * P:10 * P].rearrange("p (h d) -> p h d", h=2),
                                 lambda z: z[:, 8:9, :].broadcast_to([P, 2, DH]))]).then_inc(qkb_roped, 1)
                            dve.drain()
                for t in range(NT):
                    nk = (t + 1) * P
                    dve.wait_ge(relu_done, NT * l + t + 1)
                    sc = iscore[:, t, 0:nk]
                    cm = causal[:, S - nk:S]
                    for h in range(H):
                        ins = v.scalar_tensor_tensor(out=sc, in0=relu[:, h, 0:nk], scalar=wi_s[:, t, h:h + 1],
                                                     in1=cm if h == 0 else sc, op0=ALU.mult, op1=ALU.add)
                        if h < H - 1:
                            dve.drain()
                    ins.then_inc(icomb_done, 1)
                dve.drain()

                def top(kind, t, hf):
                    if kind != DSA or hf:
                        return
                    nk = (t + 1) * P
                    sc = iscore[:, t, 0:nk]
                    for _ in range(TOPK // 8):
                        v.max(out=top8[:], in_=sc)
                        dve.drain()
                        v.match_replace(out=sc, in_to_replace=top8[:], in_values=sc, imm_value=TAKEN)
                        dve.drain()
                    v.tensor_scalar(dmask[:, t, 0:nk], sc, TAKEN / 2, MASKED, ALU.is_gt, ALU.mult)
                    dve.drain()
                    v.tensor_tensor(dmask[:, t, 0:nk], dmask[:, t, 0:nk], causal[:, S - nk:S], ALU.add)
                    dve.drain()

                def mask(kind, h, t):
                    nk = (t + 1) * P
                    return band[:, S - nk:S] if kind == SWA else dmask[:, t, 0:nk]

                def finish(u, kind, t):
                    if kind == SWA:
                        v.tensor_tensor(den[:, u % 2, :], den[:, u % 2, :], esink[:, u % 2, 1, :], ALU.add)
                        dve.drain()
                    v.reciprocal(rden[:, u % 2, :], den[:, u % 2, :])
                    dve.drain()
                    c0 = 0 if kind == SWA else H * DH
                    v.tensor_tensor(omix[:, t, c0:c0 + H * DH].rearrange("p (h d) -> p h d", h=H),
                                    psa[:, 2 + u % 2, :].rearrange("p (h d) -> p h d", h=H),
                                    bci(rden[:, u % 2, :], DH), ALU.mult).then_inc(o_ready, 1)
                sc = DH ** -0.5
                attention(1, l, mask, {SWA: sc, DSA: sc}, finish, top)
                opT_split(l)
                dve.wait_ge(x_ready, norms[(1, "in", 0) if l == 0 else (1, "2", l - 1)]["nx"] + 1)
                residual([(1, "o", l, k) for k in range(4)])
                norm_rows((1, "1", l))
                norm_split((1, "1", l), xhi, xlo)
                for k in range(4):
                    dve.wait_ge(pg_exp, 4 * l + k + 1)
                    e = egate[:, k, :]
                    v.tensor_scalar(e, e, 1.0, None, ALU.add)
                    dve.drain()
                    v.reciprocal(e, e)
                    dve.drain()
                    cols = slice(k * TC, (k + 1) * TC)
                    e2 = e.rearrange("p (t c) -> p t c", t=NT)
                    v.tensor_tensor(ple[:, :, cols], ple[:, :, cols], e2, ALU.mult)
                    serve((1, "pg", l, k))
                x_in = norms[(1, "1", l)]["nx"] + 1
                for s in range(FS + 1):
                    f = FS * l + s
                    if s < FS:
                        serve((1, "g", l, s))
                        serve((1, "u", l, s))
                        dve.wait_ge(gate_ready, f + 1)
                        dve.wait_ge(tile_done, ti[(1, "u", l, s)] + 1)
                        dve.drain()
                        v.tensor_tensor(hidf, gact[:, f % 2, :], psw[:, 2 * (f % 2) + 1, :], ALU.mult)
                        dve.drain()
                        hh = hidh[:, f % 2, :, :].rearrange("p c s -> p (c s)")
                        hl = hidl[:, f % 2, :, :].rearrange("p c s -> p (c s)")
                        if s >= 2:
                            dve.wait_ge(tile_done, ti[(1, "d", l, s - 2)] + 1)
                        v.tensor_copy(hh, hidf)
                        dve.drain()
                        v.tensor_tensor(hl, hidf, hh.bitcast(F32), ALU.subtract).then_inc(hid_ready, 1)
                    if s >= 1:
                        serve((1, "d", l, s - 1))
                    if s == 2:
                        dve.wait_ge(x_ready, x_in)
                        for t in range(NT):
                            v.scalar_tensor_tensor(out=y[:, t, :], in0=xtok[:, t, :], scalar=ALPHA, in1=ple[:, t, :],
                                                   op0=ALU.mult, op1=ALU.add)
                dve.wait_ge(tile_done, ti[(1, "d", l, FS - 1)] + 1)
                for t in range(NT):
                    for half in range(2):
                        cols = slice(half * 512, (half + 1) * 512)
                        v.tensor_tensor(y[:, t, cols], y[:, t, cols], psa[:, 2 * t + half, :], ALU.add)
                norm_rows((1, "2", l))
                if l + 1 < L:
                    norm_split((1, "2", l), xhi, xlo)
                else:
                    norm_tokens((1, "2", l))

            norm_rows((2, "in", 0))
            norm_split((2, "in", 0), xhi, xlo)
            for l in range(L):
                x_in = norms[(2, "in", 0) if l == 0 else (2, "3", l - 1)]["nx"]
                for k in range(8):
                    serve((2, "in", l, k))
                    if k == 2:
                        dve.wait_ge(proj2_ready, 8 * l + 3)
                        for j, (c0, n) in enumerate(((CQ, QR), (CKV, KVR))):
                            for t in range(NT):
                                src = proj2[:, t, c0:c0 + n]
                                v.tensor_tensor_reduce(out=mtmp[:, :, :].rearrange("p i c -> p (i c)")[:, 0:n], in0=src,
                                                       in1=src, scale=1.0 / n, scalar=RMS_EPS, op0=ALU.mult,
                                                       op1=ALU.add, accum_out=varc[:, 2 * j + t:2 * j + t + 1])
                                dve.drain()
                        v.tensor_scalar(varc[:], varc[:], 1.0, None, ALU.mult).then_inc(c_var, 1)
                        dve.wait_ge(c_rstd, l + 1)
                        for j, (c0, n) in enumerate(((CQ, QR), (CKV, KVR))):
                            for t in range(NT):
                                src = proj2[:, t, c0:c0 + n]
                                ins = v.tensor_scalar(src, src, rstdc[:, 2 * j + t:2 * j + t + 1], None, ALU.mult)
                        ins.then_inc(c_normed, 1)
                        kx = proj2[:, :, KR:KR + 32]
                        tm = [mtmp[:, i, 0:32].rearrange("p (t c) -> p t c", t=NT) for i in range(4)]
                        v.tensor_tensor(tm[0], kx[:, :, 0:16], mcos[:], ALU.mult)
                        v.tensor_tensor(tm[1], kx[:, :, 16:32], msin[:], ALU.mult)
                        v.tensor_tensor(tm[2], kx[:, :, 0:16], msin[:], ALU.mult)
                        v.tensor_tensor(tm[3], kx[:, :, 16:32], mcos[:], ALU.mult)
                        dve.drain()
                        v.tensor_tensor(krope[:, :, 0:16], tm[0], tm[1], ALU.subtract)
                        v.tensor_tensor(krope[:, :, 16:32], tm[2], tm[3], ALU.add)
                    if l == 0 and k == 3:
                        dve.wait_ge(mem_loaded, 16 * NT)
                        norm_rows((2, "mem", 0))
                    if l == 0 and k == 5:
                        norm_split((2, "mem", 0), memhi, memlo)
                for b in range(3):
                    dve.wait_ge(c_v, 3 * l + b + 1)
                    ks = slice(2 * b, min(2 * b + 2, 5))
                    v.tensor_copy(cT_hi[:, ks, :], ctmp[:, ks, :])
                    dve.drain()
                    v.tensor_tensor(cT_lo[:, ks, :], ctmp[:, ks, :], cT_hi[:, ks, :].bitcast(F32),
                                    ALU.subtract).then_inc(cT_ready, 1)
                for j in range(2):
                    serve((2, "uq", l, j))
                dve.wait_ge(qm_ready, 2 * (l + 1))
                qh = qm.rearrange("p t (h c) -> p t h c", h=H)
                cb = mcos[:].unsqueeze(2).broadcast_to([P, NT, H, 16])
                sb_ = msin[:].unsqueeze(2).broadcast_to([P, NT, H, 16])
                tm = [mtmp[:, i, :].rearrange("p (t h c) -> p t h c", t=NT, h=H) for i in range(4)]
                q1, q2 = qh[:, :, :, DH:DH + 16], qh[:, :, :, DH + 16:MD]
                dve.drain()
                v.tensor_tensor(tm[0], q1, cb, ALU.mult)
                v.tensor_tensor(tm[1], q2, sb_, ALU.mult)
                v.tensor_tensor(tm[2], q1, sb_, ALU.mult)
                v.tensor_tensor(tm[3], q2, cb, ALU.mult)
                dve.drain()
                v.tensor_tensor(q1, tm[0], tm[1], ALU.subtract)
                v.tensor_tensor(q2, tm[2], tm[3], ALU.add).then_inc(qm_roped, 1)
                dve.wait_ge(gate_exp, l + 1)
                v.tensor_scalar(gates[:], gates[:], 1.0, None, ALU.add)
                dve.drain()
                v.reciprocal(gates[:], gates[:])
                dve.wait_ge(tile_done, ti[(2, "ukv", l, 0)] + 1)
                for i in range(2):
                    dve.wait_ge(nsa_ready, 5 * l + 4 + i)
                    dve.drain()
                    for gr in range(2):
                        for jh in range(2):
                            src = cx[:, 2 * i + gr, :].rearrange("p (n r) -> p r n", r=16)[:, 0:16:2, jh:jh + NC]
                            row = pe_row(l, i) + 8 * jh
                            v.tensor_tensor(cf[:, 8 * jh:8 * jh + 8, gr, :], src,
                                            pcol[:, 2, row:row + 8].unsqueeze(2).broadcast_to([P, 8, NC]), ALU.add)
                    dve.drain()
                    cff = cf.rearrange("p j g n -> p j (g n)")
                    v.tensor_copy(cx_hi[i], cff)
                    dve.drain()
                    v.tensor_tensor(cx_lo[i], cff, cx_hi[i].bitcast(F32), ALU.subtract).then_inc(cmp_x, 1)
                dve.wait_ge(kvm_ready, l + 1)
                v.tensor_copy(kvm[:, :, :, P:KVW],
                              krope[:].unsqueeze(2).broadcast_to([P, NT, H, 32])).then_inc(km_roped, 1)
                serve((2, "ukv", l, 0))
                for i in range(2):
                    serve((2, "w1", l, i))
                dve.wait_ge(cmp_kv, l + 1)
                dve.drain()
                v.memset(pcmp, 0.0)
                v.tensor_copy(kct[:, 0:NC], psw[:, 2, 0:NC])
                for i in range(4):
                    ins = v.tensor_copy(vbd[32 * i:32 * i + NC, :, i * DH:(i + 1) * DH],
                                        psw[32 * i:32 * i + NC, 3, 0:2 * DH].rearrange("p (g d) -> p g d", g=2))
                ins.then_inc(cmp_kv_ready, 1)
                dve.wait_ge(cmp_scores, l + 1)
                for a in range(2):
                    v.scalar_tensor_tensor(out=scmp[:, :, a * 64:(a + 1) * 64],
                                           in0=psw[:, a, 0:128].rearrange("p (t c) -> p t c", t=NT), scalar=DH ** -0.5,
                                           in1=cmpbias[:, :, a * 64:(a + 1) * 64], op0=ALU.mult, op1=ALU.add)
                dve.drain()
                s3 = scmp.rearrange("p t (h n) -> p (t h) n", h=H)
                v.tensor_reduce(cmx[:], s3, AX.X, ALU.max)
                dve.drain()
                v.tensor_tensor(s3, s3, bci(cmx[:], 16), ALU.subtract).then_inc(cmp_shifted, 1)
                dve.wait_ge(cmp_exp, l + 1)
                v.tensor_reduce(cden[:], pcmp[:, :, :, 0:16].rearrange("p t h n -> p (t h) n"), AX.X, ALU.add)
                dve.drain()
                v.reciprocal(cden[:], cden[:])
                dve.drain()
                g4 = gates[:].rearrange("p t (h b) -> p b t h", b=3)
                cf3 = coef[:].rearrange("p (t h) -> p t h", t=NT)
                v.tensor_tensor(cf3, cden[:].rearrange("p (t h) -> p t h", t=NT), g4[:, 0], ALU.mult)
                dve.drain()
                v.tensor_tensor(cf3, cf3, bci(valid[:], H), ALU.mult)
                dve.drain()
                dve.wait_ge(cmp_pv, l + 1)
                for t in range(NT):
                    ins = v.tensor_tensor(omix[:, t, 512:1024].rearrange("p (h d) -> p h d", h=H),
                                          psw[:, 2 + t, :].rearrange("p (h d) -> p h d", h=H),
                                          bci(coef[:, t * H:(t + 1) * H], DH), ALU.mult)
                ins.then_inc(cmp_o, 1)
                if l == 0:
                    dve.wait_ge(alibi_loaded, 16)

                def mask2(kind, h, t):
                    nk = (t + 1) * P
                    return causal[:, S - nk:S] if kind == MLA else alibi[:, h, S - nk:S]

                def finish2(u, kind, t):
                    rd = rden[:, u % 2, :]
                    v.reciprocal(rd, den[:, u % 2, :])
                    dve.drain()
                    ps = psa[:, 2 + u % 2, :].rearrange("p (h d) -> p h d", h=H)
                    if kind == MLA:
                        v.tensor_tensor(omix[:, t, 0:512].rearrange("p (h d) -> p h d", h=H), ps, bci(rd, DH),
                                        ALU.mult).then_inc(o_ready, 1)
                        return
                    v.tensor_tensor(rd, rd, g4[:, 1 if kind == SLC else 2, t, :], ALU.mult)
                    dve.drain()
                    v.tensor_tensor(otmp[:].rearrange("p (h d) -> p h d", h=H), ps, bci(rd, DH), ALU.mult)
                    dve.drain()
                    v.tensor_tensor(omix[:, t, 512:1024], omix[:, t, 512:1024], otmp[:], ALU.add).then_inc(o_ready, 1)
                dve.wait_ge(x_ready, x_in + 1)
                attention(2, l, mask2, {SLC: DH ** -0.5, WIN: DH ** -0.5, MLA: MD ** -0.5}, finish2)
                opT_split(2 + 2 * l)
                residual([(2, "out", l, k) for k in range(4)])
                norm_rows((2, "1", l))
                for k in range(2):
                    serve((2, "kv", l, k))
                norm_split((2, "1", l), xhi, xlo)
                for k in range(2, 8):
                    serve((2, "kv", l, k))
                for k in range(4):
                    serve((2, "xq", l, k))
                for t in range(NT):
                    dve.wait_ge(xs_done, NT * l + t + 1)
                    v.tensor_reduce(xmx[:, t, :], psw[:, 2 * t:2 * t + 2, :].rearrange("p b (h k) -> p (b h) k", h=2),
                                    AX.X, ALU.max)
                    dve.drain()
                    v.tensor_scalar(xmx[:, t, :], xmx[:, t, :], -1 / 16, None, ALU.mult).then_inc(xmax_done, 1)
                for t in range(NT):
                    dve.wait_ge(xexp_done, NT * l + t + 1)
                    v.reciprocal(xden[:, t, :], xden[:, t, :])
                    dve.drain()
                    v.tensor_tensor(xsoft[:, t], xsoft[:, t], bci(xden[:, t, :], S), ALU.mult).then_inc(xp_ready, 1)
                opT_split(3 + 2 * l)
                dve.wait_ge(x_ready, norms[(2, "1", l)]["nx"] + 1)
                residual([(2, "xo", l, k) for k in range(4)])
                norm_rows((2, "2", l))
                norm_split((2, "2", l), xhi, xlo)
                for s in range(FS + 1):
                    f = FS * (L + l) + s
                    if s < FS:
                        serve((2, "g", l, s))
                        serve((2, "u", l, s))
                        dve.wait_ge(conv_first, 2 * (FS * l + s + 1))
                        for tap, lag in ((1, 1), (0, 2)):
                            j = 3 + 2 * l
                            for buf, bank, ch0 in ((conv_g, 2 * (f % 2), 22 + 2 * s), (conv_a, 2 * (f % 2) + 1, 2 * s)):
                                for ch in range(2):
                                    cc = 44 * tap + ch0 + ch
                                    o = buf[:, f % 2, ch, lag:S]
                                    ins = v.scalar_tensor_tensor(out=o, in0=bank2(psw, bank)[:, ch, 0:S - lag],
                                                                 scalar=pcol[:, j, cc:cc + 1], in1=o, op0=ALU.mult,
                                                                 op1=ALU.add)
                            if tap:
                                dve.drain()
                        ins.then_inc(conv_done, 1)
                        dve.wait_ge(gate_ready, f + 1)
                        dve.drain()
                        v.tensor_tensor(hidf, gact[:, f % 2, :], conv_a[:, f % 2].rearrange("p c s -> p (c s)"),
                                        ALU.mult)
                        dve.drain()
                        hh = hidh[:, f % 2, :, :].rearrange("p c s -> p (c s)")
                        hl = hidl[:, f % 2, :, :].rearrange("p c s -> p (c s)")
                        if s >= 2:
                            dve.wait_ge(tile_done, ti[(2, "d", l, s - 2)] + 1)
                        v.tensor_copy(hh, hidf)
                        dve.drain()
                        v.tensor_tensor(hl, hidf, hh.bitcast(F32), ALU.subtract).then_inc(hid_ready, 1)
                    if s >= 1:
                        serve((2, "d", l, s - 1))
                dve.wait_ge(x_ready, norms[(2, "2", l)]["nx"] + 1)
                dve.wait_ge(tile_done, ti[(2, "d", l, FS - 1)] + 1)
                for t in range(NT):
                    for half in range(2):
                        cols = slice(half * 512, (half + 1) * 512)
                        v.scalar_tensor_tensor(out=y[:, t, cols], in0=xtok[:, t, cols], scalar=ALPHA,
                                               in1=psa[:, 2 * t + half, :], op0=ALU.mult, op1=ALU.add)
                norm_rows((2, "3", l))
                if l + 1 < L:
                    norm_split((2, "3", l), xhi, xlo)
                else:
                    norm_tokens((2, "3", l))

        @block.gpsimd
        def _(pool):
            g = nc.gpsimd

            def norm_scale(key):
                x = norms[key]
                pool.wait_ge(ln_var, x["n"] + 1)
                g.tensor_tensor(rstd[:, 0:NT], vare[:, 0:NT], mhalf[:, 0:NT], ALU.pow).then_inc(ln_rstd, 1)

            def norm_tokens(key):
                x = norms[key]
                pool.wait_ge(ln_xn, NT * (x["n"] + 1))
                pool.wait_ge(gb_loaded, 32 * (x["nx"] + 1))
                g.tensor_tensor(xtok[:], y, bc(gb[:, 0, :], NT), ALU.mult)
                pool.drain()
                g.tensor_tensor(xtok[:], xtok[:], bc(gb[:, 1, :], NT), ALU.add).then_inc(x_ready, 1)

            pool.wait_ge(mhalf_ready, 1)
            norm_scale((1, "in", 0))
            norm_tokens((1, "in", 0))
            pool.wait_ge(tables_ready, 1)
            for l in range(L):
                pool.wait_ge(ki_var, l + 1)
                g.tensor_tensor(rstd[:, 0:NT], vare[:, 0:NT], mhalf[:, 0:NT], ALU.pow).then_inc(ki_rstd, 1)
                pool.wait_ge(proj_ready, 7 * (l + 1))
                pool.wait_ge(p_ready, l + 1)
                t1 = pt[:, 1:3, :].rearrange("p a b -> p (a b)")[:, 0:640].rearrange("p (h d) -> p h d", h=10)
                t2 = pt[:, 2:4, :].rearrange("p a b -> p (a b)")[:, 384:1024].rearrange("p (h d) -> p h d", h=10)
                for t in range(NT):
                    x = proj1[:, t, QA:QA + 640].rearrange("p (h d) -> p h d", h=10)
                    g.tensor_tensor(t1, x, bc(cos64[:, t, :], 10), ALU.mult)
                    g.tensor_tensor(t2[:, :, 0:32], x[:, :, 32:64], bc(sin64[:, t, 0:32], 10), ALU.mult)
                    g.tensor_tensor(t2[:, :, 32:64], x[:, :, 0:32], bc(sin64[:, t, 32:64], 10), ALU.mult)
                    pool.drain()
                    g.tensor_tensor(roped[:, t, 0:4 * P].rearrange("p (r a d) -> p a r d", a=2, d=DH),
                                    t1[:, 0:8, :].rearrange("p (a r) d -> p a r d", a=2),
                                    t2[:, 0:8, :].rearrange("p (a r) d -> p a r d", a=2), ALU.add)
                    g.tensor_tensor(roped[:, t, 4 * P:5 * P].rearrange("p (h d) -> p h d", h=2),
                                    t1[:, 8:10, :], t2[:, 8:10, :], ALU.add).then_inc(qka_roped, 1)
                    pool.drain()
                norm_scale((1, "1", l))
                norm_tokens((1, "1", l))
                norm_scale((1, "2", l))
                if l + 1 < L:
                    norm_tokens((1, "2", l))

            norm_scale((2, "in", 0))
            norm_tokens((2, "in", 0))
            for l in range(L):
                pool.wait_ge(c_var, l + 1)
                g.tensor_tensor(rstdc[:], varc[:], mhalf[:], ALU.pow).then_inc(c_rstd, 1)
                if l == 0:
                    norm_scale((2, "mem", 0))
                    pool.wait_ge(xT_ready, 4 * (norms[(2, "mem", 0)]["nt"] + 1))
                pool.wait_ge(proj2_ready, 8 * l + 5)
                for t in range(NT):
                    ins = g.tensor_copy(nqp[:, t, :].rearrange("p (r g d) -> p g r d", r=4, g=2),
                                        proj2[:, t, NQ:NQ + 512].rearrange("p (g r d) -> p g r d", g=2, r=4))
                ins.then_inc(kd_ready, 1)
                pool.wait_ge(proj2_ready, 8 * l + 6)
                for e in range(2):
                    ins = g.tensor_copy(kdup[:, :, :, e, :],
                                        proj2[:, :, KC:KC + 256].rearrange("p t (q d) -> p t q d", q=4))
                ins.then_inc(kd_ready, 1)
                norm_scale((2, "1", l))
                norm_tokens((2, "1", l))
                norm_scale((2, "2", l))
                norm_tokens((2, "2", l))
                norm_scale((2, "3", l))
                if l + 1 < L:
                    norm_tokens((2, "3", l))


_NAMES = [
    "x", "p", "positions", "ln_in_g", "ln_in_b", "w_in", "attn_sinks", "idx_k_g", "idx_k_b", "w_o", "ln1_g", "ln1_b",
    "w_gu", "w_down", "w_pg", "w_pp", "ln2_g", "ln2_b", "mem_2", "ln_in_g_2", "ln_in_b_2", "ln_mem_g_2",
    "ln_mem_b_2", "w_in_2", "mla_cq_g_2", "mla_w_uq_2", "mla_ckv_g_2", "mla_w_ukv_2", "nsa_pe_k_2", "nsa_w1_k_2",
    "nsa_b1_k_2", "nsa_w2_k_2", "nsa_pe_v_2", "nsa_w1_v_2", "nsa_b1_v_2", "nsa_w2_v_2", "w_out_2", "ln1_g_2",
    "ln1_b_2", "xa_wq_2", "xa_wkv_2", "xa_wo_2", "ln2_g_2", "ln2_b_2", "ffn_w_up_2", "ffn_conv_w_2",
    "ffn_conv_b_2", "ffn_w_down_2", "ln3_g_2", "ln3_b_2",
]


def kernel(**inputs):
    import concourse.bacc as bacc
    from concourse.bass_utils import run_bass_kernel_spmd

    nc = bacc.Bacc("TRN2", target_bir_lowering=False, num_devices=1, dynamic_dma_scratch_size=1024)
    arrays, w, c = {}, {}, {}
    for name in _NAMES:
        a = np.ascontiguousarray(inputs[name])
        arrays[f"in_{name}"] = a
        w[name] = nc.dram_tensor(f"in_{name}", a.shape, mybir.dt.from_np(a.dtype), kind="ExternalInput").ap()
    for name, a in constants().items():
        arrays[f"table_{name}"] = a
        c[name] = nc.dram_tensor(f"table_{name}", a.shape, F32, kind="ExternalInput").ap()
    out = nc.dram_tensor("out_0", (1, S, D), F32, kind="ExternalOutput").ap()
    build(nc, w, c, out)
    r = run_bass_kernel_spmd(nc, [arrays], core_ids=[0])
    return r.results[0]["out_0"]
```

```python
from contextlib import ExitStack
import math

import numpy as np

import concourse.bass as bass
from concourse import mybir

F32 = mybir.dt.float32
F32R = mybir.dt.float32r
I32 = mybir.dt.int32
ALU = mybir.AluOpType
ACT = mybir.ActivationFunctionType
AX = mybir.AxisListType

P = 128
S = 256
NT = S // P
D = 1024
KD = D // P
L = 2
TC = 256
FF = 2816
FS = FF // TC
H = 8
DH = 64
LN_EPS = 1e-5
RMS_EPS = 1e-6
ALPHA = (2 * L) ** 0.25
MASKED = -1e31
NEG = -1e30
TAKEN = -3e38
TOPK = min(256, S // 4)
LOWEST = -3.4e38

QA, KA, VA, QB, KB, VB, QI, KI, WI, IN1 = 0, 512, 640, 768, 1280, 1344, 1408, 1664, 1696, 1704
IN1_ORDER = (6, 5, 3, 4, 0, 1, 2)
CQ, CKV, KR, NQ, KC, KSL, VSL, KWN, VWN, GL, IN2 = 0, 384, 640, 672, 1184, 1440, 1568, 1696, 1824, 1952, 1976
QR, KVR = 384, 256
NC = 15
MD = 96
KVW = 160

NL = 5
NW = 3

SWA, DSA, SLC, WIN, MLA = "swa", "dsa", "slc", "win", "mla"


def constants():
    i = np.arange(P)[:, None]
    j = np.arange(S)[None, :]
    diag = (j - P) > i
    causal = np.where(diag, MASKED, 0.0)
    band = np.where(diag | ((j < P) & (j <= i)), MASKED, 0.0)
    slope = 2.0 ** -np.arange(1, H + 1)
    dist = P + i - j
    alibi = np.where(dist[:, None, :] < 0, MASKED, -slope[None, :, None] * dist[:, None, :] * DH ** 0.5)
    t = np.arange(NT)[None, :, None, None] * P + i[:, :, None, None]
    end = np.arange(NC + 1)[None, None, None, :] * 16 + 31
    ok = (end <= t) & (end < NC * 16 + 31)
    cmp = np.where(ok, -slope[None, None, :, None] * (t - end), NEG)
    valid = (np.arange(NT)[None, :] * P + i >= 31).astype(np.float64)
    inv = (10000.0 ** -(np.arange(32) / 32)).astype(np.float32)
    ang = (np.arange(S, dtype=np.float32)[:, None] * inv[None, ::2]).astype(np.float32)
    ang = ang.reshape(NT, P, 16).transpose(1, 0, 2).reshape(P, NT * 16)
    out = {
        "ident": np.eye(P), "causal": causal, "band": band, "alibi": alibi.reshape(P, H * S),
        "cmpbias": cmp.reshape(P, NT * H * (NC + 1)), "valid": valid,
        "inv": np.broadcast_to(inv, (P, 32)), "mcos": np.cos(ang), "msin": np.sin(ang),
    }
    return {k: np.ascontiguousarray(v, dtype=np.float32) for k, v in out.items()}


def plan_tiles(w):
    tiles = []

    def rows(a):
        return a.rearrange("(k p) n -> p k n", p=P)

    def ffn(block, l, gate, up, down):
        def gu(s):
            tiles.append(((block, "g", l, s), gate[:, :, s * TC:(s + 1) * TC]))
            tiles.append(((block, "u", l, s), up[:, :, s * TC:(s + 1) * TC]))

        def d(s):
            tiles.append(((block, "d", l, s), down[:, 2 * s:2 * s + 2, :]))
        gu(0)
        for s in range(1, FS):
            gu(s)
            d(s - 1)
        d(FS - 1)

    for l in range(L):
        tiles.append(((1, "pp", l, 0), rows(w["w_pp"][l])))
        for k in IN1_ORDER:
            tiles.append(((1, "in", l, k), rows(w["w_in"][l])[:, :, k * TC:min((k + 1) * TC, IN1)]))
        for k in range(4):
            tiles.append(((1, "o", l, k), rows(w["w_o"][l])[:, :, k * TC:(k + 1) * TC]))
        for k in range(4):
            tiles.append(((1, "pg", l, k), rows(w["w_pg"][l])[:, :, k * TC:(k + 1) * TC]))
        gu = rows(w["w_gu"][l])
        ffn(1, l, gu[:, :, 0:FF], gu[:, :, FF:2 * FF], rows(w["w_down"][l]))
    for l in range(L):
        for k in range(8):
            tiles.append(((2, "in", l, k), rows(w["w_in_2"][l])[:, :, k * TC:min((k + 1) * TC, IN2)]))
        for k in range(2):
            tiles.append(((2, "uq", l, k), rows(w["mla_w_uq_2"][l])[:, :, k * 384:(k + 1) * 384]))
        tiles.append(((2, "ukv", l, 0), rows(w["mla_w_ukv_2"][l])))
        tiles.append(((2, "w1", l, 0), rows(w["nsa_w1_k_2"][l])))
        tiles.append(((2, "w1", l, 1), rows(w["nsa_w1_v_2"][l])))
        for name, key, n in (("out", "w_out_2", 4), ("kv", "xa_wkv_2", 8), ("xq", "xa_wq_2", 4),
                             ("xo", "xa_wo_2", 4)):
            for k in range(n):
                tiles.append(((2, name, l, k), rows(w[key][l])[:, :, k * TC:(k + 1) * TC]))
        up = rows(w["ffn_w_up_2"][l])
        ffn(2, l, up[:, :, FF:2 * FF], up[:, :, 0:FF], rows(w["ffn_w_down_2"][l]))
    return tiles, {key: c for c, (key, _) in enumerate(tiles)}


def plan_units():
    units = []
    for l in range(L):
        units += [(1, l, kind, t) for kind in (SWA, DSA) for t in range(NT)]
    for l in range(L):
        units += [(2, l, kind, t) for kind in (SLC, WIN, MLA) for t in range(NT)]
    chunk0, m = [], 0
    for _, _, _, t in units:
        for _ in range(2):
            chunk0.append(m)
            m += t + 1
    chunk0.append(m)
    return units, chunk0


def build(nc, w, c, out):
    tiles, ti = plan_tiles(w)
    units, chunk0 = plan_units()
    n_tiles = len(tiles)

    def unit0(block, l):
        return next(u for u, x in enumerate(units) if x[0] == block and x[1] == l)

    with ExitStack() as ctx:
        def sb(name, shape, dt=F32):
            return ctx.enter_context(nc.sbuf_tensor(name, [P] + shape, dt))

        def sem(name):
            return ctx.enter_context(nc.semaphore(name))

        with nc.sbuf_tensor("raw", [P, NL, 2048], F32) as raw:
            pass
        wlo = sb("wlo", [NL, 2048], F32R)
        whi = sb("whi", [NW, 2048], F32R)
        xtok = sb("xtok", [NT, D])
        sy = sb("sy", [2, 2048])
        xhi = sb("xhi", [KD, S], F32R)
        xlo = sb("xlo", [KD, S], F32R)
        gb = sb("gb", [2, D])
        r1 = sb("r1", [4096])
        r2 = sb("r2", [4608])
        r3 = sb("r3", [4096])
        rt = sb("rt", [2048])
        pt = sb("pt", [4, 512])
        rr = sb("rr", [2560], F32R)
        ident = sb("ident", [P])
        causal = sb("causal", [S])
        band = sb("band", [S])
        inv = sb("inv", [32])
        pos_i = sb("pos_i", [NT], I32)
        pos_f = sb("pos_f", [NT])
        cos64 = sb("cos64", [NT, 64])
        sin64 = sb("sin64", [NT, 64])
        cos32 = sb("cos32", [NT, 32])
        sin32 = sb("sin32", [NT, 32])
        pcol = sb("pcol", [5, P])
        stats = sb("stats", [NT, 4, 6])
        meanvar = sb("meanvar", [NT, 2])
        vare = sb("vare", [4])
        rstd = sb("rstd", [4])
        mhalf = sb("mhalf", [4])
        sinkb = sb("sinkb", [L, H])
        ikg = sb("ikg", [L, 2, 32])
        wi_s = sb("wi_s", [NT, H])
        top8 = sb("top8", [8])
        mx = sb("mx", [2, H])
        nmx = sb("nmx", [2, H])
        den = sb("den", [2, H])
        rden = sb("rden", [2, H])
        esink = sb("esink", [2, 2, H])
        memhi = sb("memhi", [KD, S], F32R)
        memlo = sb("memlo", [KD, S], F32R)
        cmpbias = sb("cmpbias", [NT, H * 16])
        valid = sb("valid", [NT])
        mcos = sb("mcos", [NT, 16])
        msin = sb("msin", [NT, 16])
        w2s = sb("w2s", [L, 2, DH])
        hcmp = sb("hcmp", [2, 2 * NC])
        kct = sb("kct", [16])
        vbd = sb("vbd", [2, 4 * DH])
        krope = sb("krope", [NT, 32])
        gates = sb("gates", [NT, 3 * H])
        varc = sb("varc", [4])
        rstdc = sb("rstdc", [4])
        cmx = sb("cmx", [NT * H])
        cden = sb("cden", [NT * H])
        coef = sb("coef", [NT * H])
        otmp = sb("otmp", [H * DH])
        xmx = sb("xmx", [NT, 4])
        xden = sb("xden", [NT, 4])
        psw = ctx.enter_context(nc.psum_tensor("psw", [P, 4, 512], F32))
        psa = ctx.enter_context(nc.psum_tensor("psa", [P, 4, 512], F32))

        tile_loaded = [sem(f"tile_loaded{i}") for i in range(NL)]
        hi_ready = sem("hi_ready")
        lo_ready = sem("lo_ready")
        tile_done = sem("tile_done")
        ident_loaded = sem("ident_loaded")
        angles_loaded = sem("angles_loaded")
        consts_loaded = sem("consts_loaded")
        params_loaded = sem("params_loaded")
        x_loaded = sem("x_loaded")
        p_loaded = sem("p_loaded")
        gb_loaded = sem("gb_loaded")
        params_turned = sem("params_turned")
        params_ready = sem("params_ready")
        mhalf_ready = sem("mhalf_ready")
        angles_ready = sem("angles_ready")
        sines_ready = sem("sines_ready")
        tables_ready = sem("tables_ready")
        ln_var = sem("ln_var")
        ln_rstd = sem("ln_rstd")
        lo_pool = sem("lo_pool")
        part_done = sem("part_done")
        x_ready = sem("x_ready")
        act_turned = sem("act_turned")
        act_hi = sem("act_hi")
        act_ready = sem("act_ready")
        p_turned = sem("p_turned")
        p_hi = sem("p_hi")
        p_ready = sem("p_ready")
        pp_part = sem("pp_part")
        pp_ready = sem("pp_ready")
        proj_ready = sem("proj_ready")
        ki_var = sem("ki_var")
        ki_rstd = sem("ki_rstd")
        qki_roped = sem("qki_roped")
        qkb_roped = sem("qkb_roped")
        qka_roped = sem("qka_roped")
        heads_turned = sem("heads_turned")
        heads_ready = sem("heads_ready")
        iscores_done = sem("iscores_done")
        relu_done = sem("relu_done")
        icomb_done = sem("icomb_done")
        scores_done = sem("scores_done")
        smax_done = sem("smax_done")
        exp_done = sem("exp_done")
        pt_done = sem("pt_done")
        pt_ready = sem("pt_ready")
        pv_done = sem("pv_done")
        o_ready = sem("o_ready")
        pg_exp = sem("pg_exp")
        ple_used = sem("ple_used")
        gate_ready = sem("gate_ready")
        hid_ready = sem("hid_ready")
        stored = sem("stored")
        alibi_loaded = sem("alibi_loaded")
        mem_loaded = sem("mem_loaded")
        proj2_ready = sem("proj2_ready")
        c_var = sem("c_var")
        c_rstd = sem("c_rstd")
        c_normed = sem("c_normed")
        c_turned = sem("c_turned")
        c_v = sem("c_v")
        cT_ready = sem("cT_ready")
        gate_exp = sem("gate_exp")
        qm_ready = sem("qm_ready")
        qm_roped = sem("qm_roped")
        kd_ready = sem("kd_ready")
        nsa_turned = sem("nsa_turned")
        nsa_ready = sem("nsa_ready")
        kvm_ready = sem("kvm_ready")
        km_roped = sem("km_roped")
        mla_turned = sem("mla_turned")
        mla_ready = sem("mla_ready")
        cmp_x = sem("cmp_x")
        cmp_gelu = sem("cmp_gelu")
        cmp_kv = sem("cmp_kv")
        cmp_kv_ready = sem("cmp_kv_ready")
        cmp_scores = sem("cmp_scores")
        cmp_shifted = sem("cmp_shifted")
        cmp_exp = sem("cmp_exp")
        cmp_turned = sem("cmp_turned")
        cmp_pT = sem("cmp_pT")
        cmp_pv = sem("cmp_pv")
        cmp_o = sem("cmp_o")
        kv_ready = sem("kv_ready")
        xq_ready = sem("xq_ready")
        xs_done = sem("xs_done")
        xmax_done = sem("xmax_done")
        xexp_done = sem("xexp_done")
        xp_ready = sem("xp_ready")
        xp_turned = sem("xp_turned")
        xpT_ready = sem("xpT_ready")
        conv_first = sem("conv_first")
        conv_done = sem("conv_done")

        prow = r3[:, 0:5 * P].rearrange("p (j c) -> p j c", j=5)
        angs = r3[:, 1024:1024 + 6 * NT * 32].rearrange("p (j c) -> p j c", j=6)
        iscore = r3[:, 13 * S:13 * S + NT * S].rearrange("p (t k) -> p t k", t=NT)
        dmask = r2[:, NT * 13 * P:NT * 13 * P + NT * S].rearrange("p (t k) -> p t k", t=NT)
        memory = r2[:, 0:NT * D].rearrange("p (t d) -> p t d", t=NT)
        gb2 = r3[:, 0:2 * D].rearrange("p (i d) -> p i d", i=2)
        gbm = r3[:, 2 * D:4 * D].rearrange("p (i d) -> p i d", i=2)
        soft = sy[:].rearrange("p b (h k) -> p b h k", h=H)
        proj1 = r1[:, 0:NT * IN1].rearrange("p (t c) -> p t c", t=NT)
        roped = r2[:, 0:NT * 13 * P].rearrange("p (t c) -> p t c", t=NT)
        omix = r2[:, 0:NT * D].rearrange("p (t c) -> p t c", t=NT)
        headT = r3[:, 0:13 * S].rearrange("p (b s) -> p b s", b=13)
        relu = sy[:, 1, :].rearrange("p (h k) -> p h k", h=H)
        ple = rt[:].rearrange("p (t d) -> p t d", t=NT)
        ptok = pt[:, 0, :].rearrange("p (t d) -> p t d", t=NT)
        pT_hi, pT_lo = memhi[:, 0:2, :], memlo[:, 0:2, :]
        hidh = rr[:, 0:1024].rearrange("p (b c s) -> p b c s", b=2, c=2)
        hidl = rr[:, 1024:2048].rearrange("p (b c s) -> p b c s", b=2, c=2)
        alibi = rt[:].rearrange("p (h k) -> p h k", h=H)
        proj2 = r1[:, 0:NT * IN2].rearrange("p (t c) -> p t c", t=NT)
        qm = r2[:, 0:NT * H * MD].rearrange("p (t c) -> p t c", t=NT)
        kvm = r2[:, 2048:2048 + NT * H * KVW].rearrange("p (t h c) -> p t h c", t=NT, h=H)
        ctmp = r3[:, 0:5 * S].rearrange("p (k s) -> p k s", k=5)
        mqT = r3[:, 0:H * S].rearrange("p (h s) -> p h s", h=H)
        mkT = r3[:, H * S:2 * H * S].rearrange("p (h s) -> p h s", h=H)
        nsaT = gb[:].rearrange("p a b -> p (a b)")[:, 0:6 * S].rearrange("p (b s) -> p b s", b=6)
        cT_hi = rr[:, 0:5 * S].rearrange("p (k s) -> p k s", k=5)
        cT_lo = rr[:, 5 * S:10 * S].rearrange("p (k s) -> p k s", k=5)
        kdup = sy[:, 0, 0:1024].rearrange("p (t q e d) -> p t q e d", t=NT, q=4, e=2)
        nqp = sy[:, 1, 0:1024].rearrange("p (t c) -> p t c", t=NT)
        mtmp = sy[:, 0, 1024:2048].rearrange("p (i c) -> p i c", i=4)
        pcmp = pt[:, 0, :].rearrange("p (t h n) -> p t h n", t=NT, h=H)
        cx = pt[:, 1:3, :].rearrange("p a b -> p (a b)").rearrange("p (q s) -> p q s", q=4)
        cf = pt[:, 3, 0:16 * 2 * NC].rearrange("p (j g n) -> p j g n", j=16, g=2)
        scmp = pt[:, 3, 0:NT * H * 16].rearrange("p (t c) -> p t c", t=NT)
        pcT = pt[:, 1, :].rearrange("p (j q) -> p j q", j=4)
        cx_hi = [rr[:, 1000 * i:1000 * i + 480].rearrange("p (j c) -> p j c", j=16) for i in range(2)]
        cx_lo = [rr[:, 1000 * i + 500:1000 * i + 980].rearrange("p (j c) -> p j c", j=16) for i in range(2)]
        xkT = r1[:, 0:2048].rearrange("p (k s) -> p k s", k=KD)
        xvt = r1[:, 2048:4096].rearrange("p (t d) -> p t d", t=NT)
        xqT = r3[:, 0:2048].rearrange("p (k s) -> p k s", k=KD)
        xsoft = sy[:, 0, :].rearrange("p (t h k) -> p t h k", t=NT, h=4)
        hidf = r1[:, 0:512]
        conv_a = r1[:, 1536:2560].rearrange("p (b c s) -> p b c s", b=2, c=2)
        conv_g = r1[:, 2560:3584].rearrange("p (b c s) -> p b c s", b=2, c=2)
        gact = r1[:, 512:1536].rearrange("p (b c) -> p b c", b=2)
        egate = r1[:, 1536:3584].rearrange("p (b c) -> p b c", b=4)

        def tile_view(buf, n, i):
            ap = tiles[i][1]
            kt, cols = ap.shape[1], ap.shape[2]
            return buf[:, i % n, 0:kt * cols].rearrange("p (k c) -> p k c", k=kt)

        def tile_flat(buf, n, i):
            ap = tiles[i][1]
            return buf[:, i % n, 0:ap.shape[1] * ap.shape[2]]

        def bank2(ps, b):
            return ps[:, b, :].rearrange("p (t c) -> p t c", t=2)

        def residual_banks(key):
            k = key[3]
            split_tile = k == 3 and key in part
            return [bank2(psw, k)[:, 0, :], bank2(psa, 0)[:, 1, :] if split_tile else bank2(psw, k)[:, 1, :]]

        def bc(ap, n):
            return ap.unsqueeze(1).broadcast_to([P, n, ap.shape[1]])

        def bci(ap, n):
            return ap.unsqueeze(2).broadcast_to([P, ap.shape[1], n])

        norms = {}

        def add_norm(key, g, b, place=gb):
            norms[key] = dict(n=len(norms), g=g, b=b, place=place)
        add_norm((1, "in", 0), w["ln_in_g"], w["ln_in_b"])
        for l in range(L):
            add_norm((1, "1", l), w["ln1_g"][l], w["ln1_b"][l])
            add_norm((1, "2", l), w["ln2_g"][l], w["ln2_b"][l])
        add_norm((2, "in", 0), w["ln_in_g_2"], w["ln_in_b_2"], gb2)
        add_norm((2, "mem", 0), w["ln_mem_g_2"], w["ln_mem_b_2"], gbm)
        for l in range(L):
            add_norm((2, "1", l), w["ln1_g_2"][l], w["ln1_b_2"][l])
            add_norm((2, "2", l), w["ln2_g_2"][l], w["ln2_b_2"][l])
            add_norm((2, "3", l), w["ln3_g_2"][l], w["ln3_b_2"][l])

        gb_before = {0: [(1, "in", 0)]}
        for l in range(L):
            gb_before[ti[(1, "in", l, IN1_ORDER[6])]] = [(1, "1", l)]
            gb_before[ti[(1, "g", l, 2)]] = [(1, "2", l)]
            gb_before[ti[(2, "kv", l, 1)]] = [(2, "1", l)]
            gb_before[ti[(2, "xo", l, 0)]] = [(2, "2", l)]
            gb_before[ti[(2, "g", l, 3)]] = [(2, "3", l)]
        gb_before[ti[(1, "g", 1, 4)]] = [(2, "in", 0), (2, "mem", 0)]

        turn_keys = [(1, "in", 0)]
        for l in range(L):
            turn_keys += [(1, "mix", l), (1, "1", l)] + ([(1, "2", l)] if l + 1 < L else [])
        turn_keys += [(2, "in", 0), (2, "mem", 0)]
        for l in range(L):
            turn_keys += [(2, "mix", l), (2, "1", l), (2, "xa", l), (2, "2", l)] + ([(2, "3", l)] if l + 1 < L else [])
        turn = {key: e for e, key in enumerate(turn_keys)}

        last_tiles = []
        for l in range(L):
            last_tiles += [(1, "o", l, 3), (1, "d", l, FS - 1)]
        for l in range(L):
            last_tiles += [(2, "out", l, 3), (2, "xo", l, 3), (2, "d", l, FS - 1)]
        part = {key: q + 1 for q, key in enumerate(x for x in last_tiles if x[1] != "out")}
        pool_tiles = [1, 2] + [ti[key] + q for key in last_tiles if key[1] != "out" for q in (2, 3)]
        pool_tiles = [i for i in pool_tiles if i < n_tiles]

        angle_dmas = [(inv[:], c["inv"])]
        angle_dmas += [(pos_i[:, t:t + 1], w["positions"][0, t * P:(t + 1) * P].rearrange("(p o) -> p o", o=1))
                       for t in range(NT)]
        const_dmas = [(causal[:], c["causal"]), (band[:], c["band"])]
        for l in range(L):
            const_dmas += [(sinkb[:, l, :], w["attn_sinks"][l].partition_broadcast(P)),
                           (ikg[:, l, 0, :], w["idx_k_g"][l].partition_broadcast(P)),
                           (ikg[:, l, 1, :], w["idx_k_b"][l].partition_broadcast(P))]
        param_dmas = []
        param_rows = [0] * 5

        def add_param(j, row, vec):
            n = vec.shape[0] // P
            param_dmas.append((prow[row:row + n, j, :], vec.rearrange("(r c) -> r c", c=P)))
            param_rows[j] = max(param_rows[j], row + n)
        const_dmas += [(cmpbias[:].rearrange("p t c -> p (t c)"), c["cmpbias"]), (valid[:], c["valid"]),
                       (mcos[:].rearrange("p t c -> p (t c)"), c["mcos"]),
                       (msin[:].rearrange("p t c -> p (t c)"), c["msin"])]
        def cqg_row(l): return 3 * l
        def ckvg_row(l): return 6 + 2 * l
        def b1_row(l, i): return 10 + 2 * l + i
        def pe_row(l, i): return 14 + 16 * (2 * l + i)
        for l in range(L):
            const_dmas += [(w2s[:, l, 0, :], w["nsa_w2_k_2"][l]), (w2s[:, l, 1, :], w["nsa_w2_v_2"][l])]
            add_param(0, cqg_row(l), w["mla_cq_g_2"][l])
            add_param(0, ckvg_row(l), w["mla_ckv_g_2"][l])
            for i, kv in enumerate("kv"):
                add_param(0, b1_row(l, i), w[f"nsa_b1_{kv}_2"][l])
                add_param(0, pe_row(l, i), w[f"nsa_pe_{kv}_2"][l].rearrange("c d -> (c d)"))
            for j in range(3):
                add_param(1 + 2 * l + j // 2, 44 * (j % 2), w["ffn_conv_w_2"][l, j])
            add_param(2 + 2 * l, 44, w["ffn_conv_b_2"][l])
        n_const_dmas, n_param_dmas = len(const_dmas), len(param_dmas)
        block = ctx.enter_context(nc.Block())

        @block.sync
        def _(sp):
            for t in range(NT):
                sp.dma_start(xtok[:, t, :], w["x"][0, t * P:(t + 1) * P, :]).then_inc(x_loaded, 16)
            sp.dma_start(ident[:], c["ident"]).then_inc(ident_loaded, 16)

            def load_gb(key):
                x = norms[key]
                if x["place"] is not gb:
                    sp.wait_ge(x_ready, NT * (norms[(1, "1", 1)]["n"] + 1))
                elif x["n"]:
                    sp.wait_ge(x_ready, NT * x["n"])
                sp.dma_start(x["place"][:, 0, :], x["g"].partition_broadcast(P)).then_inc(gb_loaded, 16)
                sp.dma_start(x["place"][:, 1, :], x["b"].partition_broadcast(P)).then_inc(gb_loaded, 16)

            small = [(dst, src, consts_loaded) for dst, src in const_dmas]
            small += [(dst, src, params_loaded) for dst, src in param_dmas]
            for i in range(n_tiles):
                for norm_key in gb_before.get(i, []):
                    if tiles[i][0][1] == "kv":
                        sp.wait_ge(o_ready, unit0(2, tiles[i][0][2]) + 6)
                    load_gb(norm_key)
                if i >= NL:
                    sp.wait_ge(tile_done, i - NL + 1)
                key = tiles[i][0]
                if key == (1, "d", 1, FS - 1):
                    sp.wait_ge(hid_ready, FS + 5)
                    sp.dma_start(rt[:], c["alibi"]).then_inc(alibi_loaded, 16)
                if key == (1, "g", 1, 5):
                    for t in range(NT):
                        sp.dma_start(memory[:, t, :], w["mem_2"][0, t * P:(t + 1) * P, :]).then_inc(mem_loaded, 16)
                if key[1] == "pp":
                    if key[2] >= 1:
                        sp.wait_ge(x_ready, NT * 2 * key[2])
                    sp.dma_start(ptok, w["p"][key[2], 0].rearrange("(t p) d -> p t d", p=P)).then_inc(p_loaded, 16)
                sp.dma_start(tile_view(raw, NL, i), tiles[i][1]).then_inc(tile_loaded[i % NL], 16)
                if i == 0:
                    for dst, src in angle_dmas:
                        sp.dma_start(dst, src).then_inc(angles_loaded, 16)
                if i >= 2:
                    for dst, src, loaded in small[0:8]:
                        sp.dma_start(dst, src).then_inc(loaded, 16)
                    small = small[8:]
            sp.wait_ge(stored, 16 * NT)

        @block.tensor
        def _(pe):
            def take(key):
                i = ti[key]
                if i in pool_tiles:
                    pe.wait_ge(lo_pool, sum(1 for x in pool_tiles if x <= i))
                else:
                    pe.wait_ge(lo_ready, i + 1 - sum(1 for x in pool_tiles if x <= i))
                return tile_view(whi, NW, ti[key]), tile_view(wlo, NL, ti[key])

            def product(o, lh, ll, rh, rl, first, last):
                pe.matmul(o, lh, rh, start=first, stop=False)
                pe.matmul(o, lh, rl, start=False, stop=False)
                return pe.matmul(o, ll, rh, start=False, stop=last)

            def by_tokens(key, outs, ah, al, ready=None):
                wh, wl = take(key)
                kt = wh.shape[1]
                for t in range(NT):
                    for k in range(kt):
                        if ready is not None and t == 0 and k % 2 == 0:
                            pe.wait_ge(act_ready, 4 * turn[ready] + k // 2 + 1)
                        tok = slice(t * P, (t + 1) * P)
                        ins = product(outs[t], ah[:, k, tok], al[:, k, tok], wh[:, k, :], wl[:, k, :],
                                      k == 0, k == kt - 1)
                    if key in part and t == 0:
                        ins.then_inc(part_done, 1)
                ins.then_inc(tile_done, 1)

            def by_features(key, bank, ah, al, ready=None):
                wh, wl = take(key)
                kt = wh.shape[1]
                for ch in range(TC // P):
                    for k in range(kt):
                        if ready is not None and ch == 0 and k % 2 == 0:
                            pe.wait_ge(act_ready, 4 * turn[ready] + k // 2 + 1)
                        cols = slice(ch * P, (ch + 1) * P)
                        ins = product(bank[:, ch, :], wh[:, k, cols], wl[:, k, cols], ah[:, k, :], al[:, k, :],
                                      k == 0, k == kt - 1)
                ins.then_inc(tile_done, 1)

            def turns(src, ps):
                for b in range(4):
                    for kk in range(2):
                        for t in range(NT):
                            k = 2 * b + kk
                            ins = pe.transpose(ps[:, b, kk * S + t * P:kk * S + (t + 1) * P],
                                               src[:, t, k * P:(k + 1) * P], ident[:])
                    ins.then_inc(act_turned, 1)

            def norm_turns(key, ps, src=xtok):
                pe.wait_ge(x_ready, NT * (norms[key]["n"] + 1))
                turns(src, ps)

            def p_turns(l, bank):
                pe.wait_ge(p_loaded, 16 * (l + 1))
                for kk in range(2):
                    for t in range(NT):
                        ins = pe.transpose(psw[:, bank, kk * S + t * P:kk * S + (t + 1) * P],
                                           ptok[:, t, kk * P:(kk + 1) * P], ident[:])
                ins.then_inc(p_turned, 1)

            def attention(block, l, qT, kT, v, ready=lambda kind, t: None):
                first = 2 * unit0(block, l)
                count = 2 * sum(1 for x in units if x[0] == block and x[1] == l)
                for i in range(first, first + count + 2):
                    if i < first + count:
                        u, hf = divmod(i, 2)
                        kind, t = units[u][2:]
                        nk = (t + 1) * P
                        ready(kind, t)
                        if i >= 2:
                            pe.wait_ge(smax_done, i - 1)
                        for b in range(2):
                            for a in range(2):
                                h = a * 4 + hf * 2 + b
                                ins = pe.matmul(psw[:, 2 * (i % 2) + a, b * S:b * S + nk],
                                                qT(kind, h, t), kT(kind, h, nk), start=True, stop=True)
                        ins.then_inc(scores_done, 1)
                    if i - 2 >= first:
                        n = i - 2
                        u, hf = divmod(n, 2)
                        kind, t = units[u][2:]
                        pe.wait_ge(pt_ready, chunk0[n + 1])
                        if hf == 0 and u >= 2:
                            pe.wait_ge(o_ready, u - 1)
                        blk = [(b, a, kb) for b in range(2) for a in range(2) for kb in range(t + 1)]
                        for q, (b, a, kb) in enumerate(blk):
                            h = a * 4 + hf * 2 + b
                            m = chunk0[n] + q // 4
                            ins = pe.matmul(psa[:, 2 + u % 2, h * DH:(h + 1) * DH],
                                            pt[:, m % 4, (q % 4) * P:(q % 4 + 1) * P], v(kind, h, kb),
                                            start=(kb == 0), stop=(kb == t))
                        ins.then_inc(pv_done, 1)
                    if first <= i - 1 < first + count:
                        n = i - 1
                        u, hf = divmod(n, 2)
                        kind, t = units[u][2:]
                        pe.wait_ge(exp_done, n + 1)
                        blk = [(b, a, kb) for b in range(2) for a in range(2) for kb in range(t + 1)]
                        for q, (b, a, kb) in enumerate(blk):
                            h = a * 4 + hf * 2 + b
                            m = chunk0[n] + q // 4
                            if q % 4 == 0 and m >= 2:
                                pe.wait_ge(pt_ready, m - 1)
                            ins = pe.transpose(psa[:, m % 2, (q % 4) * P:(q % 4 + 1) * P],
                                               soft[:, u % 2, h, kb * P:(kb + 1) * P], ident[:])
                            if q % 4 == 3:
                                ins.then_inc(pt_done, 1)

            def ffn(block, l, f0, norm_key, before_last=lambda: None):
                for s in range(FS + 1):
                    f = f0 + s
                    if s < FS:
                        if f >= 2:
                            pe.wait_ge(hid_ready, f - 1)
                        by_features((block, "g", l, s), bank2(psw, 2 * (f % 2)), xhi, xlo,
                                    norm_key if s == 0 else None)
                        by_features((block, "u", l, s), bank2(psw, 2 * (f % 2) + 1), xhi, xlo)
                    if s >= 1:
                        g = f - 1
                        if s == FS:
                            before_last()
                        pe.wait_ge(hid_ready, g + 1)
                        wh, wl = take((block, "d", l, s - 1))
                        for t in range(NT):
                            for half in range(2):
                                for kk in range(2):
                                    tok = slice(t * P, (t + 1) * P)
                                    col = slice(half * 512, (half + 1) * 512)
                                    ins = product(psa[:, 2 * t + half, :], hidh[:, g % 2, kk, tok],
                                                  hidl[:, g % 2, kk, tok], wh[:, kk, col], wl[:, kk, col],
                                                  s == 1 and kk == 0, s == FS and kk == 1)
                            if s == FS and t == 0:
                                ins.then_inc(part_done, 1)
                        ins.then_inc(tile_done, 1)

            pe.wait_ge(ident_loaded, 16)
            p_turns(0, 0)
            for l in range(L):
                pe.wait_ge(p_ready, l + 1)
                wh, wl = take((1, "pp", l, 0))
                for k4 in range(4):
                    for t in range(NT):
                        for kk in range(2):
                            tok = slice(t * P, (t + 1) * P)
                            col = slice(k4 * TC, (k4 + 1) * TC)
                            ins = product(bank2(psw, k4)[:, t, :], pT_hi[:, kk, tok], pT_lo[:, kk, tok],
                                          wh[:, kk, col], wl[:, kk, col], kk == 0, kk == 1)
                    ins.then_inc(pp_part if k4 < 3 else tile_done, 1)
                x_in = (1, "in", 0) if l == 0 else (1, "2", l - 1)
                norm_turns(x_in, psa)
                for q, k in enumerate(IN1_ORDER):
                    if q < 4:
                        pe.wait_ge(pp_ready, 4 * l + q + 1)
                    else:
                        pe.wait_ge(proj_ready, 7 * l + q - 3)
                    cols = min(TC, IN1 - k * TC)
                    bank = bank2(psw, q % 4)
                    by_tokens((1, "in", l, k), [bank[:, t, 0:cols] for t in range(NT)], xhi, xlo,
                              x_in if q == 0 else None)
                if l == 0:
                    pe.wait_ge(params_loaded, 16 * n_param_dmas)
                    for j, n in enumerate(param_rows):
                        ins = pe.transpose(psa[:, 2 + j // 4, (j % 4) * P:(j % 4) * P + n], prow[0:n, j, :],
                                           ident[0:n, 0:n])
                    ins.then_inc(params_turned, 1)
                groups = [(10, 11), (12,), (5, 6), (7, 8), (9,), (0, 1), (2, 3), (4,)]
                for q, grp in enumerate(groups):
                    g = 8 * l + q
                    if q == 0:
                        pe.wait_ge(qki_roped, NT * (l + 1))
                    if q == 2:
                        pe.wait_ge(heads_ready, 8 * l + 2)
                        pe.wait_ge(proj_ready, 7 * (l + 1))
                        for t in range(NT):
                            nk = (t + 1) * P
                            if t == 1:
                                pe.wait_ge(relu_done, NT * l + 1)
                            for h in range(H):
                                pr = slice(32 * (h % 4), 32 * (h % 4) + 32)
                                ins = pe.matmul(psw[:, h % 4, (h // 4) * S:(h // 4) * S + nk],
                                                headT[pr, 10 + h // 4, t * P:(t + 1) * P], headT[pr, 12, 0:nk],
                                                start=True, stop=True)
                            ins.then_inc(iscores_done, 1)
                        pe.wait_ge(qkb_roped, NT * (l + 1))
                    if q == 5:
                        pe.wait_ge(qka_roped, NT * (l + 1))
                    if q >= 4:
                        pe.wait_ge(heads_ready, g - 3)
                    for j, b in enumerate(grp):
                        for t in range(NT):
                            ins = pe.transpose(psa[:, q % 4, j * S + t * P:j * S + (t + 1) * P],
                                               roped[:, t, b * P:(b + 1) * P], ident[:])
                    ins.then_inc(heads_turned, 1)
                pe.wait_ge(heads_ready, 8 * (l + 1))
                pe.wait_ge(relu_done, NT * (l + 1))
                b0 = {SWA: 0, DSA: 5}
                attention(
                    1, l,
                    lambda kind, h, t: headT[64 * (h // 4):64 * (h // 4) + 64, b0[kind] + h % 4, t * P:(t + 1) * P],
                    lambda kind, h, nk: headT[64 * (h // 4):64 * (h // 4) + 64, b0[kind] + 4, 0:nk],
                    lambda kind, h, kb: (proj1[:, kb, VA + DH * (h // 4):VA + DH * (h // 4) + DH] if kind == SWA
                                         else proj1[:, kb, VB:VB + DH]))
                pe.wait_ge(o_ready, unit0(1, l) + 4)
                turns(omix, psw)
                for k in range(4):
                    by_tokens((1, "o", l, k), residual_banks((1, "o", l, k)), xhi, xlo,
                              (1, "mix", l) if k == 0 else None)
                norm_turns((1, "1", l), psa)
                for k in range(4):
                    bank = bank2(psw, k)
                    by_tokens((1, "pg", l, k), [bank[:, t, :] for t in range(NT)], xhi, xlo,
                              (1, "1", l) if k == 0 else None)
                pe.wait_ge(pg_exp, 4 * (l + 1))
                if l + 1 < L:
                    ffn(1, l, FS * l, None, lambda: p_turns(l + 1, 2 * ((l + 1) * FS % 2)))
                else:
                    ffn(1, l, FS * l, None)

            norm_turns((2, "in", 0), psw)
            for l in range(L):
                x_in = (2, "in", 0) if l == 0 else (2, "3", l - 1)
                for k in range(8):
                    if k >= 4:
                        pe.wait_ge(proj2_ready, 8 * l + k - 3)
                    cols = min(TC, IN2 - k * TC)
                    bank = bank2(psw, k % 4)
                    by_tokens((2, "in", l, k), [bank[:, t, 0:cols] for t in range(NT)], xhi, xlo,
                              x_in if k == 0 else None)
                    if l == 0 and k == 5:
                        norm_turns((2, "mem", 0), psa, memory)
                pe.wait_ge(c_normed, l + 1)
                if l == 0:
                    pe.wait_ge(act_ready, 4 * (turn[(2, "mem", 0)] + 1))
                for b in range(3):
                    for kk in range(2 if b < 2 else 1):
                        for t in range(NT):
                            k = 2 * b + kk
                            ins = pe.transpose(psa[:, b, kk * S + t * P:kk * S + (t + 1) * P],
                                               proj2[:, t, k * P:(k + 1) * P], ident[:])
                    ins.then_inc(c_turned, 1)
                pe.wait_ge(cT_ready, 3 * (l + 1))
                pe.wait_ge(proj2_ready, 8 * (l + 1))
                for j in range(2):
                    by_tokens((2, "uq", l, j), [psw[:, 2 * j + t, 0:384] for t in range(NT)],
                              cT_hi[:, 0:3, :], cT_lo[:, 0:3, :])
                for q in range(5):
                    if q == 0:
                        pe.wait_ge(kd_ready, 2 * l + 1)
                    if q == 3:
                        pe.wait_ge(kd_ready, 2 * l + 2)
                    if q == 4:
                        pe.wait_ge(nsa_ready, 5 * l + 1)
                    for kk in range(2):
                        for t in range(NT):
                            if q < 2:
                                src = nqp[:, t, (2 * q + kk) * P:(2 * q + kk + 1) * P]
                            elif q == 2:
                                c0 = (KSL, KWN)[kk]
                                src = proj2[:, t, c0:c0 + P]
                            else:
                                src = kdup[:, t, 2 * (q - 3) + kk, :, :].rearrange("p e d -> p (e d)")
                            ins = pe.transpose(psa[:, q % 4, kk * S + t * P:kk * S + (t + 1) * P], src, ident[:])
                    ins.then_inc(nsa_turned, 1)
                pe.wait_ge(qm_ready, 2 * (l + 1))
                wh, wl = take((2, "ukv", l, 0))
                for t in range(NT):
                    for half in range(2):
                        for kk in range(2):
                            tok = slice(t * P, (t + 1) * P)
                            col = slice(half * 512, (half + 1) * 512)
                            ins = product(psw[:, 2 * t + half, :], cT_hi[:, 3 + kk, tok], cT_lo[:, 3 + kk, tok],
                                          wh[:, kk, col], wl[:, kk, col], kk == 0, kk == 1)
                ins.then_inc(tile_done, 1)
                pe.wait_ge(qm_roped, l + 1)
                pe.wait_ge(nsa_ready, 5 * (l + 1))
                for b in range(4):
                    for kk in range(2):
                        for t in range(NT):
                            h = 2 * b + kk
                            ins = pe.transpose(psa[0:MD, b, kk * S + t * P:kk * S + (t + 1) * P],
                                               qm[:, t, h * MD:(h + 1) * MD], ident[:])
                    ins.then_inc(mla_turned, 1)
                pe.wait_ge(kvm_ready, l + 1)
                for i in range(2):
                    pe.wait_ge(cmp_x, 2 * l + i + 1)
                    wh, wl = take((2, "w1", l, i))
                    for j in range(16):
                        ins = product(psw[:, i, 0:2 * NC], wh[:, j, :], wl[:, j, :], cx_hi[i][:, j, :],
                                      cx_lo[i][:, j, :], j == 0, j == 15)
                    ins.then_inc(tile_done, 1)
                pe.wait_ge(km_roped, l + 1)
                for b in range(4):
                    pe.wait_ge(mla_ready, 8 * l + b + 1)
                    for kk in range(2):
                        for t in range(NT):
                            h = 2 * b + kk
                            ins = pe.transpose(psa[0:MD, b, kk * S + t * P:kk * S + (t + 1) * P],
                                               kvm[:, t, h, DH:KVW], ident[:])
                    ins.then_inc(mla_turned, 1)
                pe.wait_ge(cmp_gelu, 2 * (l + 1))
                for gr in range(2):
                    pe.matmul(psw[64 * gr:64 * gr + 64, 2, 0:NC], w2s[:, l, 0, :],
                              hcmp[:, 0, gr * NC:(gr + 1) * NC], start=True, stop=True)
                for gr in range(2):
                    for i in range(4):
                        ins = pe.matmul(psw[32 * i:32 * i + NC, 3, gr * DH:(gr + 1) * DH],
                                        hcmp[:, 1, gr * NC:(gr + 1) * NC], w2s[:, l, 1, :], start=True, stop=True)
                ins.then_inc(cmp_kv, 1)
                pe.wait_ge(cmp_kv_ready, l + 1)
                for t in range(NT):
                    for r in range(4):
                        for a in range(2):
                            ins = pe.matmul(psw[:, a, t * 64 + r * 16:t * 64 + (r + 1) * 16],
                                            nsaT[64 * a:64 * a + 64, r, t * P:(t + 1) * P],
                                            kct[64 * a:64 * a + 64, :], start=True, stop=True)
                ins.then_inc(cmp_scores, 1)
                pe.wait_ge(cmp_exp, l + 1)
                pe.wait_ge(mla_ready, 8 * (l + 1))
                for t in range(NT):
                    for gr in range(2):
                        ins = pe.transpose(psa[:, 0, (2 * t + gr) * P:(2 * t + gr + 1) * P],
                                           pcmp[:, t, 4 * gr:4 * gr + 4, :].rearrange("p h n -> p (h n)"), ident[:])
                ins.then_inc(cmp_turned, 1)
                pe.wait_ge(cmp_pT, l + 1)
                for t in range(NT):
                    for gr in range(2):
                        ins = pe.matmul(psw[:, 2 + t, gr * S:(gr + 1) * S], pcT[:, 2 * t + gr, :], vbd[:, gr, :],
                                        start=True, stop=True)
                ins.then_inc(cmp_pv, 1)
                pe.wait_ge(cmp_o, l + 1)
                kblock = {SLC: 4, WIN: 5}
                vcol = {SLC: VSL, WIN: VWN}
                attention(
                    2, l,
                    lambda kind, h, t: (mqT[0:MD, h, t * P:(t + 1) * P] if kind == MLA else
                                        nsaT[64 * (h // 4):64 * (h // 4) + 64, h % 4, t * P:(t + 1) * P]),
                    lambda kind, h, nk: (mkT[0:MD, h, 0:nk] if kind == MLA else
                                         nsaT[64 * (h // 4):64 * (h // 4) + 64, kblock[kind], 0:nk]),
                    lambda kind, h, kb: (kvm[:, kb, h, 0:DH] if kind == MLA else
                                         proj2[:, kb, vcol[kind] + DH * (h // 4):vcol[kind] + DH * (h // 4) + DH]))
                pe.wait_ge(o_ready, unit0(2, l) + 6)
                turns(omix, psw)
                for k in range(4):
                    by_tokens((2, "out", l, k), residual_banks((2, "out", l, k)), xhi, xlo,
                              (2, "mix", l) if k == 0 else None)

                def memory_product(k):
                    if k >= 4:
                        pe.wait_ge(kv_ready, 8 * l + k - 3)
                    bank = bank2(psa, k % 4)
                    if k < 4:
                        by_features((2, "kv", l, k), bank, memhi, memlo)
                    else:
                        by_tokens((2, "kv", l, k), [bank[:, t, :] for t in range(NT)], memhi, memlo)
                for k in range(2):
                    memory_product(k)
                norm_turns((2, "1", l), psw)
                for k in range(2, 8):
                    memory_product(k)
                for k in range(4):
                    by_features((2, "xq", l, k), bank2(psw, k), xhi, xlo, (2, "1", l) if k == 0 else None)
                pe.wait_ge(xq_ready, 4 * (l + 1))
                pe.wait_ge(kv_ready, 8 * (l + 1))
                for t in range(NT):
                    for h in range(4):
                        for kk in range(2):
                            ins = pe.matmul(psw[:, 2 * t + h // 2, (h % 2) * S:(h % 2 + 1) * S],
                                            xqT[:, 2 * h + kk, t * P:(t + 1) * P], xkT[:, 2 * h + kk, :],
                                            start=(kk == 0), stop=(kk == 1))
                    ins.then_inc(xs_done, 1)
                for t in range(NT):
                    pe.wait_ge(xp_ready, NT * l + t + 1)
                    for h in range(4):
                        for m in range(2):
                            ins = pe.transpose(psa[:, h, m * S + t * P:m * S + (t + 1) * P],
                                               xsoft[:, t, h, m * P:(m + 1) * P], ident[:])
                        if t == 1:
                            ins.then_inc(xp_turned, 1)
                for h in range(4):
                    pe.wait_ge(xpT_ready, 4 * l + h + 1)
                    for ch in range(2):
                        for m in range(2):
                            f = 2 * h + ch
                            ins = pe.matmul(psw[:, h, ch * S:(ch + 1) * S], xvt[:, m, f * P:(f + 1) * P],
                                            pt[:, h, m * S:(m + 1) * S], start=(m == 0), stop=(m == 1))
                    ins.then_inc(act_turned, 1)
                for k in range(4):
                    by_tokens((2, "xo", l, k), residual_banks((2, "xo", l, k)), xhi, xlo,
                              (2, "xa", l) if k == 0 else None)
                norm_turns((2, "2", l), psa)
                ffn(2, l, FS * (L + l), (2, "2", l))
                if l + 1 < L:
                    norm_turns((2, "3", l), psw)

        @block.scalar
        def _(act):
            nxt = [0]

            def split(i):
                act.wait_ge(tile_loaded[i % NL], 16 * (i // NL + 1))
                if i >= NW:
                    act.wait_ge(tile_done, i - NW + 1)
                nc.scalar.activation(tile_flat(whi, NW, i), tile_flat(raw, NL, i), ACT.Copy).then_inc(hi_ready, 1)

            def serve(key):
                while nxt[0] <= min(ti[key] + NW, n_tiles - 1):
                    split(nxt[0])
                    nxt[0] += 1

            def turned_hi(key, ps, hi=xhi):
                for b in range(4):
                    act.wait_ge(act_turned, 4 * turn[key] + b + 1)
                    nc.scalar.activation(hi[:, 2 * b:2 * b + 2, :], bank2(ps, b), ACT.Copy).then_inc(act_hi, 1)

            def p_high(l, bank):
                act.wait_ge(p_turned, l + 1)
                nc.scalar.activation(pT_hi, bank2(psw, bank), ACT.Copy).then_inc(p_hi, 1)

            def attention(block, l):
                first = 2 * unit0(block, l)
                count = 2 * sum(1 for x in units if x[0] == block and x[1] == l)
                for i in range(first, first + count + 1):
                    if i < first + count:
                        u, hf = divmod(i, 2)
                        kind, t = units[u][2:]
                        nk = (t + 1) * P
                        act.wait_ge(smax_done, i + 1)
                        if kind == SWA:
                            hs = esink[:, u % 2, 1, :].rearrange("p (a q) -> p a q", a=2)[:, :, 2 * hf:2 * hf + 2]
                            nc.scalar.activation(hs, esink[:, u % 2, 0, :].rearrange(
                                "p (a q) -> p a q", a=2)[:, :, 2 * hf:2 * hf + 2], ACT.Exp)
                        for b in range(2):
                            for a in range(2):
                                h = a * 4 + hf * 2 + b
                                ins = nc.scalar.activation(soft[:, u % 2, h, 0:nk], soft[:, u % 2, h, 0:nk], ACT.Exp,
                                                           bias=nmx[:, u % 2, h:h + 1], scale=1.0,
                                                           accum_out=den[:, u % 2, h:h + 1])
                        ins.then_inc(exp_done, 1)
                    if i - 1 >= first:
                        n = i - 1
                        for m in range(chunk0[n], chunk0[n + 1]):
                            act.wait_ge(pt_done, m + 1)
                            if m >= 4:
                                owner = max(x for x in range(len(chunk0) - 1) if chunk0[x] <= m - 4)
                                act.wait_ge(pv_done, owner + 1)
                            nc.scalar.activation(pt[:, m % 4, :], psa[:, m % 2, :], ACT.Copy).then_inc(pt_ready, 1)

            split(0)
            p_high(0, 0)
            split(1)
            split(2)
            nxt[0] = 3

            for l in range(L):
                for k4 in range(4):
                    if k4 < 3:
                        act.wait_ge(pp_part, 3 * l + k4 + 1)
                    else:
                        act.wait_ge(tile_done, ti[(1, "pp", l, 0)] + 1)
                    nc.scalar.activation(ple[:, :, k4 * TC:(k4 + 1) * TC], bank2(psw, k4),
                                         ACT.Copy).then_inc(pp_ready, 1)
                turned_hi((1, "in", 0) if l == 0 else (1, "2", l - 1), psa)
                serve((1, "pp", l, 0))
                if l == 0:
                    act.wait_ge(angles_ready, 1)
                    nc.scalar.activation(angs[:, 4:6, :], angs[:, 4:6, :], ACT.Sin).then_inc(sines_ready, 1)
                for q, k in enumerate(IN1_ORDER):
                    cols = min(TC, IN1 - k * TC)
                    act.wait_ge(tile_done, ti[(1, "in", l, k)] + 1)
                    nc.scalar.activation(proj1[:, :, k * TC:k * TC + cols], bank2(psw, q % 4)[:, :, 0:cols],
                                         ACT.Copy).then_inc(proj_ready, 1)
                    serve((1, "in", l, k))
                if l == 0:
                    act.wait_ge(params_turned, 1)
                    for j, n in enumerate(param_rows):
                        nc.scalar.activation(pcol[:, j, 0:n], psa[:, 2 + j // 4, (j % 4) * P:(j % 4) * P + n], ACT.Copy)
                for q, grp in enumerate([(10, 11), (12,), (5, 6), (7, 8), (9,), (0, 1), (2, 3), (4,)]):
                    if q == 2:
                        for t in range(NT):
                            nk = (t + 1) * P
                            act.wait_ge(iscores_done, NT * l + t + 1)
                            if t == 1:
                                act.wait_ge(icomb_done, NT * l + 1)
                            for j in range(4):
                                ins = nc.scalar.activation(relu[:, j:8:4, 0:nk], bank2(psw, j)[:, :, 0:nk], ACT.Relu)
                            ins.then_inc(relu_done, 1)
                    act.wait_ge(heads_turned, 8 * l + q + 1)
                    nb = len(grp)
                    nc.scalar.activation(headT[:, grp[0]:grp[0] + nb, :], bank2(psa, q % 4)[:, 0:nb, :],
                                         ACT.Copy).then_inc(heads_ready, 1)
                attention(1, l)
                turned_hi((1, "mix", l), psw)
                for k in range(4):
                    serve((1, "o", l, k))
                turned_hi((1, "1", l), psa)
                for k in range(4):
                    act.wait_ge(tile_done, ti[(1, "pg", l, k)] + 1)
                    if k == 0:
                        act.wait_ge(o_ready, unit0(1, l) + 4)
                    nc.scalar.activation(egate[:, k, :], psw[:, k, :], ACT.Exp, scale=-1.0).then_inc(pg_exp, 1)
                    serve((1, "pg", l, k))
                for s in range(FS + 1):
                    f = FS * l + s
                    if s < FS:
                        serve((1, "g", l, s))
                        if f >= 2:
                            act.wait_ge(hid_ready, f - 1)
                        act.wait_ge(tile_done, ti[(1, "g", l, s)] + 1)
                        nc.scalar.activation(gact[:, f % 2, :], psw[:, 2 * (f % 2), :],
                                             ACT.Silu).then_inc(gate_ready, 1)
                        serve((1, "u", l, s))
                    if s == FS and l + 1 < L:
                        p_high(l + 1, 2 * ((l + 1) * FS % 2))
                    if s >= 1:
                        serve((1, "d", l, s - 1))

            for l in range(L):
                turned_hi((2, "in", 0) if l == 0 else (2, "3", l - 1), psw)
                for k in range(8):
                    cols = min(TC, IN2 - k * TC)
                    act.wait_ge(tile_done, ti[(2, "in", l, k)] + 1)
                    nc.scalar.activation(proj2[:, :, k * TC:k * TC + cols], bank2(psw, k % 4)[:, :, 0:cols],
                                         ACT.Copy).then_inc(proj2_ready, 1)
                    serve((2, "in", l, k))
                    if l == 0 and k == 5:
                        turned_hi((2, "mem", 0), psa, memhi)
                for b in range(3):
                    act.wait_ge(c_turned, 3 * l + b + 1)
                    for kk in range(2 if b < 2 else 1):
                        k = 2 * b + kk
                        row = cqg_row(l) + k if k < 3 else ckvg_row(l) + k - 3
                        ins = nc.scalar.activation(ctmp[:, k, :], psa[:, b, kk * S:(kk + 1) * S], ACT.Copy,
                                                   scale=pcol[:, 0, row:row + 1])
                    ins.then_inc(c_v, 1)
                act.wait_ge(proj2_ready, 8 * (l + 1))
                nc.scalar.activation(gates[:], proj2[:, :, GL:IN2], ACT.Exp, scale=-1.0).then_inc(gate_exp, 1)
                for j in range(2):
                    act.wait_ge(tile_done, ti[(2, "uq", l, j)] + 1)
                    nc.scalar.activation(qm[:, :, j * 384:(j + 1) * 384], psw[:, 2 * j:2 * j + 2, 0:384],
                                         ACT.Copy).then_inc(qm_ready, 1)
                    serve((2, "uq", l, j))
                for q in range(5):
                    act.wait_ge(nsa_turned, 5 * l + q + 1)
                    if q < 3:
                        nc.scalar.activation(nsaT[:, 2 * q:2 * q + 2, :], bank2(psa, q), ACT.Copy).then_inc(nsa_ready, 1)
                    else:
                        i = 2 * (q - 3)
                        nc.scalar.activation(cx[0:64, i:i + 2, :], bank2(psa, q % 4)[0:64], ACT.Copy)
                        nc.scalar.activation(cx[64:128, i:i + 2, 0:S - 1], bank2(psa, q % 4)[64:128, :, 1:S],
                                             ACT.Copy).then_inc(nsa_ready, 1)
                act.wait_ge(tile_done, ti[(2, "ukv", l, 0)] + 1)
                for t in range(NT):
                    kv = psw[:, 2 * t:2 * t + 2, :].rearrange("p b (h c) -> p (b h) c", h=4)
                    nc.scalar.activation(kvm[:, t, :, 0:DH], kv[:, :, DH:P], ACT.Copy)
                    ins = nc.scalar.activation(kvm[:, t, :, DH:P], kv[:, :, 0:DH], ACT.Copy)
                ins.then_inc(kvm_ready, 1)
                serve((2, "ukv", l, 0))
                for b in range(4):
                    act.wait_ge(mla_turned, 8 * l + b + 1)
                    nc.scalar.activation(mqT[0:MD, 2 * b:2 * b + 2, :], bank2(psa, b)[0:MD], ACT.Copy).then_inc(mla_ready, 1)
                for i in range(2):
                    act.wait_ge(tile_done, ti[(2, "w1", l, i)] + 1)
                    row = b1_row(l, i)
                    nc.scalar.activation(hcmp[:, i, :], psw[:, i, 0:2 * NC], ACT.Gelu_apprx_tanh,
                                         bias=pcol[:, 0, row:row + 1]).then_inc(cmp_gelu, 1)
                    serve((2, "w1", l, i))
                for b in range(4):
                    act.wait_ge(mla_turned, 8 * l + b + 5)
                    nc.scalar.activation(mkT[0:MD, 2 * b:2 * b + 2, :], bank2(psa, b)[0:MD], ACT.Copy).then_inc(mla_ready, 1)
                act.wait_ge(cmp_shifted, l + 1)
                nc.scalar.activation(pcmp[:, :, :, 0:16].rearrange("p t h n -> p (t h) n"),
                                     scmp.rearrange("p t (h n) -> p (t h) n", h=H), ACT.Exp).then_inc(cmp_exp, 1)
                act.wait_ge(cmp_turned, l + 1)
                nc.scalar.activation(pcT, psa[:, 0, :].rearrange("p (j q) -> p j q", j=4), ACT.Copy).then_inc(cmp_pT, 1)
                attention(2, l)
                turned_hi((2, "mix", l), psw)
                for k in range(4):
                    serve((2, "out", l, k))

                def memory_evac(k):
                    act.wait_ge(tile_done, ti[(2, "kv", l, k)] + 1)
                    if k < 4:
                        nc.scalar.activation(xkT[:, 2 * k:2 * k + 2, :], bank2(psa, k % 4), ACT.Copy).then_inc(kv_ready, 1)
                    else:
                        nc.scalar.activation(xvt[:, :, (k - 4) * TC:(k - 3) * TC], bank2(psa, k % 4),
                                             ACT.Copy).then_inc(kv_ready, 1)
                    serve((2, "kv", l, k))
                for k in range(2):
                    memory_evac(k)
                turned_hi((2, "1", l), psw)
                for k in range(2, 8):
                    memory_evac(k)
                for k in range(4):
                    act.wait_ge(tile_done, ti[(2, "xq", l, k)] + 1)
                    nc.scalar.activation(xqT[:, 2 * k:2 * k + 2, :], bank2(psw, k), ACT.Copy).then_inc(xq_ready, 1)
                    serve((2, "xq", l, k))
                for t in range(NT):
                    act.wait_ge(xmax_done, NT * l + t + 1)
                    for h in range(4):
                        ins = nc.scalar.activation(xsoft[:, t, h, :], psw[:, 2 * t + h // 2, (h % 2) * S:(h % 2 + 1) * S],
                                                   ACT.Exp, bias=xmx[:, t, h:h + 1], scale=1 / 16,
                                                   accum_out=xden[:, t, h:h + 1])
                    ins.then_inc(xexp_done, 1)
                for h in range(4):
                    act.wait_ge(xp_turned, 4 * l + h + 1)
                    nc.scalar.activation(pt[:, h, :], psa[:, h, :], ACT.Copy).then_inc(xpT_ready, 1)
                turned_hi((2, "xa", l), psw)
                for k in range(4):
                    serve((2, "xo", l, k))
                turned_hi((2, "2", l), psa)
                for s in range(FS + 1):
                    f = FS * (L + l) + s
                    if s < FS:
                        for name, buf, bank, ch0 in (("g", conv_g, 2 * (f % 2), 22 + 2 * s),
                                                     ("u", conv_a, 2 * (f % 2) + 1, 2 * s)):
                            act.wait_ge(tile_done, ti[(2, name, l, s)] + 1)
                            if f >= 2:
                                act.wait_ge(hid_ready, f - 1)
                            for ch in range(2):
                                cc = ch0 + ch
                                ins = nc.scalar.activation(buf[:, f % 2, ch, :], bank2(psw, bank)[:, ch, :],
                                                           ACT.Identity, scale=pcol[:, 2 + 2 * l, cc:cc + 1],
                                                           bias=pcol[:, 2 + 2 * l, 44 + cc:45 + cc])
                            ins.then_inc(conv_first, 1)
                            serve((2, name, l, s))
                        act.wait_ge(conv_done, FS * l + s + 1)
                        nc.scalar.activation(gact[:, f % 2, :], conv_g[:, f % 2].rearrange("p c s -> p (c s)"),
                                             ACT.Silu).then_inc(gate_ready, 1)
                    if s >= 1:
                        serve((2, "d", l, s - 1))
            for t in range(NT):
                act.wait_ge(x_ready, NT * (len(norms) - 1) + t + 1)
                act.dma_start(out[0, t * P:(t + 1) * P, :], xtok[:, t, :]).then_inc(stored, 16)
            act.wait_ge(stored, 16 * NT)

        @block.vector
        def _(dve):
            nxt = [0]
            v = nc.vector

            def split(i):
                dve.wait_ge(hi_ready, i + 1)
                v.tensor_tensor(tile_flat(wlo, NL, i), tile_flat(raw, NL, i),
                                tile_flat(whi, NW, i).bitcast(F32), ALU.subtract).then_inc(lo_ready, 1)

            def serve(key):
                while nxt[0] <= min(ti[key] + NW, n_tiles - 1):
                    if nxt[0] not in pool_tiles:
                        split(nxt[0])
                    nxt[0] += 1

            def norm(key, x, chunks, before=lambda t: None):
                nm = norms[key]
                for t in range(NT):
                    before(t)
                    dve.drain()
                    v.bn_aggr(meanvar[:, t, :], stats[:, t, 0:chunks, :])
                    dve.drain()
                    v.tensor_scalar(vare[:, t:t + 1], meanvar[:, t, 1:2], LN_EPS, None, ALU.add).then_inc(ln_var, 1)
                    if t == 0:
                        dve.wait_ge(gb_loaded, 32 * (nm["n"] + 1))
                    v.scalar_tensor_tensor(out=x[:, t, :], in0=x[:, t, :], scalar=meanvar[:, t, 0:1],
                                           in1=nm["place"][:, 0, :], op0=ALU.subtract, op1=ALU.mult)
                    dve.wait_ge(ln_rstd, NT * nm["n"] + t + 1)
                    dve.drain()
                    v.scalar_tensor_tensor(out=x[:, t, :], in0=x[:, t, :], scalar=rstd[:, t:t + 1],
                                           in1=nm["place"][:, 1, :], op0=ALU.mult, op1=ALU.add).then_inc(x_ready, 1)

            def half_stats(x, t):
                for half in range(2):
                    v.bn_stats(stats[:, t, half, :], x[:, t, half * 512:(half + 1) * 512])

            def turned_lo(key, ps, hi=xhi, lo=xlo):
                for b in range(4):
                    dve.wait_ge(act_hi, 4 * turn[key] + b + 1)
                    ks = slice(2 * b, 2 * b + 2)
                    v.tensor_tensor(lo[:, ks, :], bank2(ps, b), hi[:, ks, :].bitcast(F32),
                                    ALU.subtract).then_inc(act_ready, 1)

            def p_low(l, bank):
                dve.wait_ge(p_hi, l + 1)
                v.tensor_tensor(pT_lo, bank2(psw, bank), pT_hi.bitcast(F32), ALU.subtract).then_inc(p_ready, 1)

            def rope(x, cos, sin, t1, t2, writes):
                nh, wd = x.shape[1], x.shape[2]
                hw = wd // 2
                v.tensor_tensor(t1, x, bc(cos, nh), ALU.mult)
                v.tensor_tensor(t2[:, :, 0:hw], x[:, :, hw:wd], bc(sin[:, 0:hw], nh), ALU.mult)
                v.tensor_tensor(t2[:, :, hw:wd], x[:, :, 0:hw], bc(sin[:, hw:wd], nh), ALU.mult)
                dve.drain()
                for o, sel in writes:
                    ins = v.tensor_tensor(o, sel(t1), sel(t2), ALU.add)
                return ins

            def attention(block, l, mask, scale, finish, before=lambda kind, t, hf: None):
                first = 2 * unit0(block, l)
                count = 2 * sum(1 for x in units if x[0] == block and x[1] == l)
                for i in range(first, first + count + 2):
                    if i < first + count:
                        u, hf = divmod(i, 2)
                        kind, t = units[u][2:]
                        nk = (t + 1) * P
                        before(kind, t, hf)
                        dve.wait_ge(scores_done, i + 1)
                        if u >= 2:
                            dve.wait_ge(pt_done, chunk0[2 * (u - 1)])
                        for b in range(2):
                            for a in range(2):
                                h = a * 4 + hf * 2 + b
                                v.tensor_tensor_reduce(
                                    out=soft[:, u % 2, h, 0:nk], in0=psw[:, 2 * (i % 2) + a, b * S:b * S + nk],
                                    in1=mask(kind, h, t), scale=scale[kind], scalar=LOWEST, op0=ALU.add, op1=ALU.max,
                                    accum_out=mx[:, u % 2, h:h + 1])
                        dve.drain()

                        def hs(x):
                            return x.rearrange("p (a q) -> p a q", a=2)[:, :, 2 * hf:2 * hf + 2]
                        m, nm = hs(mx[:, u % 2, :]), hs(nmx[:, u % 2, :])
                        if kind == SWA:
                            v.tensor_tensor(m, m, hs(sinkb[:, l, :]), ALU.max)
                            dve.drain()
                            v.tensor_tensor(hs(esink[:, u % 2, 0, :]), hs(sinkb[:, l, :]), m, ALU.subtract)
                        v.tensor_scalar(nm, m, -1.0, None, ALU.mult).then_inc(smax_done, 1)
                    if i - 2 >= first and (i - 2) % 2 == 1:
                        u = (i - 2) // 2
                        dve.wait_ge(pv_done, 2 * u + 2)
                        finish(u, units[u][2], units[u][3])

            def residual_norm(keys, norm_key):
                def piece(k, ts, ps):
                    cols = slice(k * TC, (k + 1) * TC)
                    v.scalar_tensor_tensor(out=xtok[:, ts, cols], in0=xtok[:, ts, cols], scalar=ALPHA,
                                           in1=ps, op0=ALU.mult, op1=ALU.add)
                    dve.drain()
                    for t in range(ts.start, ts.stop):
                        v.bn_stats(stats[:, t, k, :], xtok[:, t, cols])
                for k in range(3):
                    dve.wait_ge(tile_done, ti[keys[k]] + 1)
                    piece(k, slice(0, NT), bank2(psw, k))
                    serve(keys[k])

                def last(t):
                    if t == 0 and keys[3] in part:
                        dve.wait_ge(part_done, part[keys[3]])
                    else:
                        dve.wait_ge(tile_done, ti[keys[3]] + 1)
                    piece(3, slice(t, t + 1), residual_banks(keys[3])[t].unsqueeze(1))
                norm(norm_key, xtok, 4, last)

            def ffn_norm(block, l, norm_key, join):
                key = (block, "d", l, FS - 1)

                def last(t):
                    if t == 0:
                        dve.wait_ge(part_done, part[key])
                    else:
                        dve.wait_ge(tile_done, ti[key] + 1)
                    for half in range(2):
                        join(t, slice(half * 512, (half + 1) * 512), psa[:, 2 * t + half, :])
                    dve.drain()
                    half_stats(xtok, t)
                norm(norm_key, xtok, 2, last)

            v.memset(mhalf[:], -0.5).then_inc(mhalf_ready, 1)
            v.memset(kct[:], 0.0)
            v.memset(vbd[:], 0.0)
            dve.wait_ge(x_loaded, 16 * NT)
            norm((1, "in", 0), xtok, 2, lambda t: half_stats(xtok, t))
            p_low(0, 0)
            split(0)
            nxt[0] = 1

            def angles():
                dve.wait_ge(angles_loaded, 16 * len(angle_dmas))
                v.tensor_copy(pos_f[:], pos_i[:])
                dve.drain()
                for t in range(NT):
                    v.tensor_scalar(angs[:, 0, t * 32:(t + 1) * 32], inv[:], pos_f[:, t:t + 1], None, ALU.mult)
                dve.drain()
                whole = float(np.float32(1 / (2 * math.pi)))
                magic = 1.5 * 2.0 ** 23
                c1 = 6.28125
                c2 = float(np.float32(np.round((2 * math.pi - c1) * 2 ** 20) / 2 ** 20))
                c3 = float(np.float32(2 * math.pi - c1 - c2))
                v.tensor_scalar(angs[:, 1, :], angs[:, 0, :], whole, magic, ALU.mult, ALU.add)
                v.tensor_scalar(angs[:, 2, :], angs[:, 0, :], whole, 0.25, ALU.mult, ALU.add)
                dve.drain()
                v.tensor_scalar(angs[:, 2, :], angs[:, 2, :], magic, -magic, ALU.add, ALU.add)
                v.tensor_scalar(angs[:, 1, :], angs[:, 1, :], -magic, None, ALU.add)
                dve.drain()
                for j in range(2):
                    src = angs[:, 0, :]
                    for cc in (c1, c2, c3):
                        v.scalar_tensor_tensor(out=angs[:, 4 + j, :], in0=angs[:, 1 + j, :], scalar=-cc, in1=src,
                                               op0=ALU.mult, op1=ALU.add)
                        src = angs[:, 4 + j, :]
                        dve.drain()
                v.tensor_scalar(angs[:, 5, :], angs[:, 5, :], math.pi / 2, None, ALU.add)
                dve.drain()
                v.tensor_scalar(angs[:, 4:6, :], angs[:, 4:6, :], 3.1415925, -3.1415925, ALU.min,
                                ALU.max).then_inc(angles_ready, 1)

            def tables():
                dve.wait_ge(sines_ready, 1)
                sn = angs[:, 4, :].rearrange("p (t c) -> p t c", t=NT)
                cs = angs[:, 5, :].rearrange("p (t c) -> p t c", t=NT)
                for half in range(2):
                    v.tensor_copy(cos64[:, :, 32 * half:32 * half + 32], cs)
                    v.tensor_copy(cos32[:, :, 16 * half:16 * half + 16], cs[:, :, 0:32:2])
                    v.tensor_scalar(sin64[:, :, 32 * half:32 * half + 32], sn, 2.0 * half - 1, None, ALU.mult)
                    ins = v.tensor_scalar(sin32[:, :, 16 * half:16 * half + 16], sn[:, :, 0:32:2], 2.0 * half - 1, None,
                                          ALU.mult)
                ins.then_inc(tables_ready, 1)

            for l in range(L):
                turned_lo((1, "in", 0) if l == 0 else (1, "2", l - 1), psa)
                if l == 0:
                    angles()
                serve((1, "pp", l, 0))
                t1 = sy[:, 0, 0:640]
                t2 = sy[:, 0, 640:1280]
                for q, k in enumerate(IN1_ORDER):
                    serve((1, "in", l, k))
                    if l == 0 and q == 0:
                        tables()
                        dve.wait_ge(consts_loaded, 16 * n_const_dmas)
                        dve.drain()
                    if q == 1:
                        dve.wait_ge(proj_ready, 7 * l + 2)
                        for t in range(NT):
                            v.bn_stats(stats[:, t, 0, :], proj1[:, t, KI:KI + 32])
                        dve.drain()
                        for t in range(NT):
                            v.bn_aggr(meanvar[:, t, :], stats[:, t, 0:1, :])
                        dve.drain()
                        v.tensor_scalar(vare[:, 0:NT], meanvar[:, :, 1], LN_EPS, None, ALU.add).then_inc(ki_var, 1)
                        v.tensor_scalar(wi_s[:], proj1[:, :, WI:WI + H], 8 ** -0.5 * 32 ** -0.5, None, ALU.mult)
                        dve.wait_ge(ki_rstd, l + 1)
                        ki = proj1[:, :, KI:KI + 32]
                        for t in range(NT):
                            v.tensor_scalar(ki[:, t, :], ki[:, t, :], meanvar[:, t, 0:1], rstd[:, t:t + 1],
                                            ALU.subtract, ALU.mult)
                        dve.drain()
                        v.tensor_tensor(ki, ki, bc(ikg[:, l, 0, :], NT), ALU.mult)
                        dve.drain()
                        v.tensor_tensor(ki, ki, bc(ikg[:, l, 1, :], NT), ALU.add)
                        dve.drain()
                    if q == 2:
                        for t in range(NT):
                            x = proj1[:, t, QI:QI + 288].rearrange("p (h d) -> p h d", h=9)
                            a = t1[:, 0:288].rearrange("p (h d) -> p h d", h=9)
                            b = t2[:, 0:288].rearrange("p (h d) -> p h d", h=9)
                            rope(x, cos32[:, t, :], sin32[:, t, :], a, b, [
                                (roped[:, t, 10 * P:12 * P].rearrange("p (h d) -> p h d", h=8), lambda z: z[:, 0:8, :]),
                                (roped[:, t, 12 * P:13 * P].rearrange("p (h d) -> p h d", h=4),
                                 lambda z: z[:, 8:9, :].broadcast_to([P, 4, 32]))]).then_inc(qki_roped, 1)
                            dve.drain()
                    if q == 4:
                        dve.wait_ge(proj_ready, 7 * l + 4)
                        for t in range(NT):
                            x = proj1[:, t, QB:QB + 576].rearrange("p (h d) -> p h d", h=9)
                            a = t1[:, 0:576].rearrange("p (h d) -> p h d", h=9)
                            b = t2[:, 0:576].rearrange("p (h d) -> p h d", h=9)
                            rope(x, cos64[:, t, :], sin64[:, t, :], a, b, [
                                (roped[:, t, 5 * P:9 * P].rearrange("p (r a d) -> p a r d", a=2, d=DH),
                                 lambda z: z[:, 0:8, :].rearrange("p (a r) d -> p a r d", a=2)),
                                (roped[:, t, 9 * P:10 * P].rearrange("p (h d) -> p h d", h=2),
                                 lambda z: z[:, 8:9, :].broadcast_to([P, 2, DH]))]).then_inc(qkb_roped, 1)
                            dve.drain()
                for t in range(NT):
                    nk = (t + 1) * P
                    dve.wait_ge(relu_done, NT * l + t + 1)
                    sc = iscore[:, t, 0:nk]
                    cm = causal[:, S - nk:S]
                    for h in range(H):
                        ins = v.scalar_tensor_tensor(out=sc, in0=relu[:, h, 0:nk], scalar=wi_s[:, t, h:h + 1],
                                                     in1=cm if h == 0 else sc, op0=ALU.mult, op1=ALU.add)
                        if h < H - 1:
                            dve.drain()
                    ins.then_inc(icomb_done, 1)
                dve.drain()

                def top(kind, t, hf):
                    if kind != DSA or hf:
                        return
                    nk = (t + 1) * P
                    sc = iscore[:, t, 0:nk]
                    for _ in range(TOPK // 8):
                        v.max(out=top8[:], in_=sc)
                        dve.drain()
                        v.match_replace(out=sc, in_to_replace=top8[:], in_values=sc, imm_value=TAKEN)
                        dve.drain()
                    v.tensor_scalar(dmask[:, t, 0:nk], sc, TAKEN / 2, MASKED, ALU.is_gt, ALU.mult)
                    dve.drain()
                    v.tensor_tensor(dmask[:, t, 0:nk], dmask[:, t, 0:nk], causal[:, S - nk:S], ALU.add)
                    dve.drain()

                def mask(kind, h, t):
                    nk = (t + 1) * P
                    return band[:, S - nk:S] if kind == SWA else dmask[:, t, 0:nk]

                def finish(u, kind, t):
                    if kind == SWA:
                        v.tensor_tensor(den[:, u % 2, :], den[:, u % 2, :], esink[:, u % 2, 1, :], ALU.add)
                        dve.drain()
                    v.reciprocal(rden[:, u % 2, :], den[:, u % 2, :])
                    dve.drain()
                    c0 = 0 if kind == SWA else H * DH
                    v.tensor_tensor(omix[:, t, c0:c0 + H * DH].rearrange("p (h d) -> p h d", h=H),
                                    psa[:, 2 + u % 2, :].rearrange("p (h d) -> p h d", h=H),
                                    bci(rden[:, u % 2, :], DH), ALU.mult).then_inc(o_ready, 1)
                sc = DH ** -0.5
                attention(1, l, mask, {SWA: sc, DSA: sc}, finish, top)
                turned_lo((1, "mix", l), psw)
                residual_norm([(1, "o", l, k) for k in range(4)], (1, "1", l))
                turned_lo((1, "1", l), psa)
                serve((1, "o", l, 3))
                for k in range(4):
                    dve.wait_ge(pg_exp, 4 * l + k + 1)
                    e = egate[:, k, :]
                    v.tensor_scalar(e, e, 1.0, None, ALU.add)
                    dve.drain()
                    v.reciprocal(e, e)
                    dve.drain()
                    cols = slice(k * TC, (k + 1) * TC)
                    e2 = e.rearrange("p (t c) -> p t c", t=NT)
                    v.tensor_tensor(ple[:, :, cols], ple[:, :, cols], e2, ALU.mult)
                    serve((1, "pg", l, k))
                for s in range(FS + 1):
                    f = FS * l + s
                    if s < FS:
                        serve((1, "g", l, s))
                        serve((1, "u", l, s))
                        dve.wait_ge(gate_ready, f + 1)
                        dve.wait_ge(tile_done, ti[(1, "u", l, s)] + 1)
                        dve.drain()
                        v.tensor_tensor(hidf, gact[:, f % 2, :], psw[:, 2 * (f % 2) + 1, :], ALU.mult)
                        dve.drain()
                        hh = hidh[:, f % 2, :, :].rearrange("p c s -> p (c s)")
                        hl = hidl[:, f % 2, :, :].rearrange("p c s -> p (c s)")
                        if s >= 2:
                            dve.wait_ge(tile_done, ti[(1, "d", l, s - 2)] + 1)
                        v.tensor_copy(hh, hidf)
                        dve.drain()
                        v.tensor_tensor(hl, hidf, hh.bitcast(F32), ALU.subtract).then_inc(hid_ready, 1)
                    if s == FS and l + 1 < L:
                        p_low(l + 1, 2 * ((l + 1) * FS % 2))
                    if 1 <= s < FS:
                        serve((1, "d", l, s - 1))
                    if s == 2:
                        for t in range(NT):
                            v.scalar_tensor_tensor(out=xtok[:, t, :], in0=xtok[:, t, :], scalar=ALPHA,
                                                   in1=ple[:, t, :], op0=ALU.mult, op1=ALU.add)

                def join(t, cols, ps):
                    v.tensor_tensor(xtok[:, t, cols], xtok[:, t, cols], ps, ALU.add)
                ffn_norm(1, l, (1, "2", l), join)

            norm((2, "in", 0), xtok, 2, lambda t: (dve.drain(), half_stats(xtok, t)))
            serve((1, "d", L - 1, FS - 1))
            for l in range(L):
                turned_lo((2, "in", 0) if l == 0 else (2, "3", l - 1), psw)
                for k in range(8):
                    serve((2, "in", l, k))
                    if k == 2:
                        dve.wait_ge(proj2_ready, 8 * l + 3)
                        for j, (c0, n) in enumerate(((CQ, QR), (CKV, KVR))):
                            for t in range(NT):
                                src = proj2[:, t, c0:c0 + n]
                                v.tensor_tensor_reduce(out=mtmp[:, :, :].rearrange("p i c -> p (i c)")[:, 0:n], in0=src,
                                                       in1=src, scale=1.0 / n, scalar=RMS_EPS, op0=ALU.mult,
                                                       op1=ALU.add, accum_out=varc[:, 2 * j + t:2 * j + t + 1])
                                dve.drain()
                        v.tensor_scalar(varc[:], varc[:], 1.0, None, ALU.mult).then_inc(c_var, 1)
                        dve.wait_ge(c_rstd, l + 1)
                        for j, (c0, n) in enumerate(((CQ, QR), (CKV, KVR))):
                            for t in range(NT):
                                src = proj2[:, t, c0:c0 + n]
                                ins = v.tensor_scalar(src, src, rstdc[:, 2 * j + t:2 * j + t + 1], None, ALU.mult)
                        ins.then_inc(c_normed, 1)
                        kx = proj2[:, :, KR:KR + 32]
                        tm = [mtmp[:, i, 0:32].rearrange("p (t c) -> p t c", t=NT) for i in range(4)]
                        v.tensor_tensor(tm[0], kx[:, :, 0:16], mcos[:], ALU.mult)
                        v.tensor_tensor(tm[1], kx[:, :, 16:32], msin[:], ALU.mult)
                        v.tensor_tensor(tm[2], kx[:, :, 0:16], msin[:], ALU.mult)
                        v.tensor_tensor(tm[3], kx[:, :, 16:32], mcos[:], ALU.mult)
                        dve.drain()
                        v.tensor_tensor(krope[:, :, 0:16], tm[0], tm[1], ALU.subtract)
                        v.tensor_tensor(krope[:, :, 16:32], tm[2], tm[3], ALU.add)
                    if l == 0 and k == 3:
                        dve.wait_ge(mem_loaded, 16 * NT)
                        norm((2, "mem", 0), memory, 2, lambda t: half_stats(memory, t))
                    if l == 0 and k == 5:
                        turned_lo((2, "mem", 0), psa, memhi, memlo)
                for b in range(3):
                    dve.wait_ge(c_v, 3 * l + b + 1)
                    ks = slice(2 * b, min(2 * b + 2, 5))
                    v.tensor_copy(cT_hi[:, ks, :], ctmp[:, ks, :])
                    dve.drain()
                    v.tensor_tensor(cT_lo[:, ks, :], ctmp[:, ks, :], cT_hi[:, ks, :].bitcast(F32),
                                    ALU.subtract).then_inc(cT_ready, 1)
                for j in range(2):
                    serve((2, "uq", l, j))
                dve.wait_ge(qm_ready, 2 * (l + 1))
                qh = qm.rearrange("p t (h c) -> p t h c", h=H)
                cb = mcos[:].unsqueeze(2).broadcast_to([P, NT, H, 16])
                sb_ = msin[:].unsqueeze(2).broadcast_to([P, NT, H, 16])
                tm = [mtmp[:, i, :].rearrange("p (t h c) -> p t h c", t=NT, h=H) for i in range(4)]
                q1, q2 = qh[:, :, :, DH:DH + 16], qh[:, :, :, DH + 16:MD]
                dve.drain()
                v.tensor_tensor(tm[0], q1, cb, ALU.mult)
                v.tensor_tensor(tm[1], q2, sb_, ALU.mult)
                v.tensor_tensor(tm[2], q1, sb_, ALU.mult)
                v.tensor_tensor(tm[3], q2, cb, ALU.mult)
                dve.drain()
                v.tensor_tensor(q1, tm[0], tm[1], ALU.subtract)
                v.tensor_tensor(q2, tm[2], tm[3], ALU.add).then_inc(qm_roped, 1)
                dve.wait_ge(gate_exp, l + 1)
                v.tensor_scalar(gates[:], gates[:], 1.0, None, ALU.add)
                dve.drain()
                v.reciprocal(gates[:], gates[:])
                dve.wait_ge(tile_done, ti[(2, "ukv", l, 0)] + 1)
                for i in range(2):
                    dve.wait_ge(nsa_ready, 5 * l + 4 + i)
                    dve.drain()
                    for gr in range(2):
                        for jh in range(2):
                            src = cx[:, 2 * i + gr, :].rearrange("p (n r) -> p r n", r=16)[:, 0:16:2, jh:jh + NC]
                            row = pe_row(l, i) + 8 * jh
                            v.tensor_tensor(cf[:, 8 * jh:8 * jh + 8, gr, :], src,
                                            pcol[:, 0, row:row + 8].unsqueeze(2).broadcast_to([P, 8, NC]), ALU.add)
                    dve.drain()
                    cff = cf.rearrange("p j g n -> p j (g n)")
                    v.tensor_copy(cx_hi[i], cff)
                    dve.drain()
                    v.tensor_tensor(cx_lo[i], cff, cx_hi[i].bitcast(F32), ALU.subtract).then_inc(cmp_x, 1)
                dve.wait_ge(kvm_ready, l + 1)
                v.tensor_copy(kvm[:, :, :, P:KVW],
                              krope[:].unsqueeze(2).broadcast_to([P, NT, H, 32])).then_inc(km_roped, 1)
                serve((2, "ukv", l, 0))
                for i in range(2):
                    serve((2, "w1", l, i))
                dve.wait_ge(cmp_kv, l + 1)
                dve.drain()
                v.memset(pcmp, 0.0)
                v.tensor_copy(kct[:, 0:NC], psw[:, 2, 0:NC])
                for i in range(4):
                    ins = v.tensor_copy(vbd[32 * i:32 * i + NC, :, i * DH:(i + 1) * DH],
                                        psw[32 * i:32 * i + NC, 3, 0:2 * DH].rearrange("p (g d) -> p g d", g=2))
                ins.then_inc(cmp_kv_ready, 1)
                dve.wait_ge(cmp_scores, l + 1)
                for a in range(2):
                    v.scalar_tensor_tensor(out=scmp[:, :, a * 64:(a + 1) * 64],
                                           in0=psw[:, a, 0:128].rearrange("p (t c) -> p t c", t=NT), scalar=DH ** -0.5,
                                           in1=cmpbias[:, :, a * 64:(a + 1) * 64], op0=ALU.mult, op1=ALU.add)
                dve.drain()
                s3 = scmp.rearrange("p t (h n) -> p (t h) n", h=H)
                v.tensor_reduce(cmx[:], s3, AX.X, ALU.max)
                dve.drain()
                v.tensor_tensor(s3, s3, bci(cmx[:], 16), ALU.subtract).then_inc(cmp_shifted, 1)
                dve.wait_ge(cmp_exp, l + 1)
                v.tensor_reduce(cden[:], pcmp[:, :, :, 0:16].rearrange("p t h n -> p (t h) n"), AX.X, ALU.add)
                dve.drain()
                v.reciprocal(cden[:], cden[:])
                dve.drain()
                g4 = gates[:].rearrange("p t (h b) -> p b t h", b=3)
                cf3 = coef[:].rearrange("p (t h) -> p t h", t=NT)
                v.tensor_tensor(cf3, cden[:].rearrange("p (t h) -> p t h", t=NT), g4[:, 0], ALU.mult)
                dve.drain()
                v.tensor_tensor(cf3, cf3, bci(valid[:], H), ALU.mult)
                dve.drain()
                dve.wait_ge(cmp_pv, l + 1)
                for t in range(NT):
                    ins = v.tensor_tensor(omix[:, t, 512:1024].rearrange("p (h d) -> p h d", h=H),
                                          psw[:, 2 + t, :].rearrange("p (h d) -> p h d", h=H),
                                          bci(coef[:, t * H:(t + 1) * H], DH), ALU.mult)
                ins.then_inc(cmp_o, 1)
                if l == 0:
                    dve.wait_ge(alibi_loaded, 16)

                def mask2(kind, h, t):
                    nk = (t + 1) * P
                    return causal[:, S - nk:S] if kind == MLA else alibi[:, h, S - nk:S]

                def finish2(u, kind, t):
                    rd = rden[:, u % 2, :]
                    v.reciprocal(rd, den[:, u % 2, :])
                    dve.drain()
                    ps = psa[:, 2 + u % 2, :].rearrange("p (h d) -> p h d", h=H)
                    if kind == MLA:
                        v.tensor_tensor(omix[:, t, 0:512].rearrange("p (h d) -> p h d", h=H), ps, bci(rd, DH),
                                        ALU.mult).then_inc(o_ready, 1)
                        return
                    v.tensor_tensor(rd, rd, g4[:, 1 if kind == SLC else 2, t, :], ALU.mult)
                    dve.drain()
                    v.tensor_tensor(otmp[:].rearrange("p (h d) -> p h d", h=H), ps, bci(rd, DH), ALU.mult)
                    dve.drain()
                    v.tensor_tensor(omix[:, t, 512:1024], omix[:, t, 512:1024], otmp[:], ALU.add).then_inc(o_ready, 1)
                attention(2, l, mask2, {SLC: DH ** -0.5, WIN: DH ** -0.5, MLA: MD ** -0.5}, finish2)
                turned_lo((2, "mix", l), psw)
                residual_norm([(2, "out", l, k) for k in range(4)], (2, "1", l))
                serve((2, "out", l, 3))
                for k in range(2):
                    serve((2, "kv", l, k))
                turned_lo((2, "1", l), psw)
                for k in range(2, 8):
                    serve((2, "kv", l, k))
                for k in range(4):
                    serve((2, "xq", l, k))
                for t in range(NT):
                    dve.wait_ge(xs_done, NT * l + t + 1)
                    v.tensor_reduce(xmx[:, t, :], psw[:, 2 * t:2 * t + 2, :].rearrange("p b (h k) -> p (b h) k", h=2),
                                    AX.X, ALU.max)
                    dve.drain()
                    v.tensor_scalar(xmx[:, t, :], xmx[:, t, :], -1 / 16, None, ALU.mult).then_inc(xmax_done, 1)
                for t in range(NT):
                    dve.wait_ge(xexp_done, NT * l + t + 1)
                    v.reciprocal(xden[:, t, :], xden[:, t, :])
                    dve.drain()
                    v.tensor_tensor(xsoft[:, t], xsoft[:, t], bci(xden[:, t, :], S), ALU.mult).then_inc(xp_ready, 1)
                turned_lo((2, "xa", l), psw)
                residual_norm([(2, "xo", l, k) for k in range(4)], (2, "2", l))
                turned_lo((2, "2", l), psa)
                serve((2, "xo", l, 3))
                for s in range(FS + 1):
                    f = FS * (L + l) + s
                    if s < FS:
                        serve((2, "g", l, s))
                        dve.wait_ge(conv_first, 2 * (FS * l + s + 1))
                        for tap, lag in ((1, 1), (0, 2)):
                            j = 1 + 2 * l
                            for buf, bank, ch0 in ((conv_g, 2 * (f % 2), 22 + 2 * s), (conv_a, 2 * (f % 2) + 1, 2 * s)):
                                for ch in range(2):
                                    cc = 44 * tap + ch0 + ch
                                    o = buf[:, f % 2, ch, lag:S]
                                    ins = v.scalar_tensor_tensor(out=o, in0=bank2(psw, bank)[:, ch, 0:S - lag],
                                                                 scalar=pcol[:, j, cc:cc + 1], in1=o, op0=ALU.mult,
                                                                 op1=ALU.add)
                            if tap:
                                dve.drain()
                        ins.then_inc(conv_done, 1)
                        serve((2, "u", l, s))
                        dve.wait_ge(gate_ready, f + 1)
                        dve.drain()
                        v.tensor_tensor(hidf, gact[:, f % 2, :], conv_a[:, f % 2].rearrange("p c s -> p (c s)"),
                                        ALU.mult)
                        dve.drain()
                        hh = hidh[:, f % 2, :, :].rearrange("p c s -> p (c s)")
                        hl = hidl[:, f % 2, :, :].rearrange("p c s -> p (c s)")
                        if s >= 2:
                            dve.wait_ge(tile_done, ti[(2, "d", l, s - 2)] + 1)
                        v.tensor_copy(hh, hidf)
                        dve.drain()
                        v.tensor_tensor(hl, hidf, hh.bitcast(F32), ALU.subtract).then_inc(hid_ready, 1)
                    if 1 <= s < FS:
                        serve((2, "d", l, s - 1))

                def join(t, cols, ps):
                    v.scalar_tensor_tensor(out=xtok[:, t, cols], in0=xtok[:, t, cols], scalar=ALPHA, in1=ps,
                                           op0=ALU.mult, op1=ALU.add)
                ffn_norm(2, l, (2, "3", l), join)

        @block.gpsimd
        def _(pool):
            g = nc.gpsimd

            def norm_scale(key):
                for t in range(NT):
                    pool.wait_ge(ln_var, NT * norms[key]["n"] + t + 1)
                    g.tensor_tensor(rstd[:, t:t + 1], vare[:, t:t + 1], mhalf[:, t:t + 1],
                                    ALU.pow).then_inc(ln_rstd, 1)

            def low_parts(c):
                for i in (c + 2, c + 3):
                    if i < n_tiles:
                        pool.wait_ge(hi_ready, i + 1)
                        g.tensor_tensor(tile_flat(wlo, NL, i), tile_flat(raw, NL, i),
                                        tile_flat(whi, NW, i).bitcast(F32), ALU.subtract).then_inc(lo_pool, 1)

            pool.wait_ge(mhalf_ready, 1)
            norm_scale((1, "in", 0))
            low_parts(-1)
            pool.wait_ge(tables_ready, 1)
            for l in range(L):
                pool.wait_ge(ki_var, l + 1)
                g.tensor_tensor(rstd[:, 0:NT], vare[:, 0:NT], mhalf[:, 0:NT], ALU.pow).then_inc(ki_rstd, 1)
                pool.wait_ge(proj_ready, 7 * (l + 1))
                pool.wait_ge(p_ready, l + 1)
                t1 = pt[:, 1:3, :].rearrange("p a b -> p (a b)")[:, 0:640].rearrange("p (h d) -> p h d", h=10)
                t2 = pt[:, 2:4, :].rearrange("p a b -> p (a b)")[:, 384:1024].rearrange("p (h d) -> p h d", h=10)
                for t in range(NT):
                    x = proj1[:, t, QA:QA + 640].rearrange("p (h d) -> p h d", h=10)
                    g.tensor_tensor(t1, x, bc(cos64[:, t, :], 10), ALU.mult)
                    g.tensor_tensor(t2[:, :, 0:32], x[:, :, 32:64], bc(sin64[:, t, 0:32], 10), ALU.mult)
                    g.tensor_tensor(t2[:, :, 32:64], x[:, :, 0:32], bc(sin64[:, t, 32:64], 10), ALU.mult)
                    pool.drain()
                    g.tensor_tensor(roped[:, t, 0:4 * P].rearrange("p (r a d) -> p a r d", a=2, d=DH),
                                    t1[:, 0:8, :].rearrange("p (a r) d -> p a r d", a=2),
                                    t2[:, 0:8, :].rearrange("p (a r) d -> p a r d", a=2), ALU.add)
                    g.tensor_tensor(roped[:, t, 4 * P:5 * P].rearrange("p (h d) -> p h d", h=2),
                                    t1[:, 8:10, :], t2[:, 8:10, :], ALU.add).then_inc(qka_roped, 1)
                    pool.drain()
                norm_scale((1, "1", l))
                low_parts(ti[(1, "o", l, 3)])
                norm_scale((1, "2", l))
                if l == L - 1:
                    norm_scale((2, "in", 0))
                low_parts(ti[(1, "d", l, FS - 1)])

            for l in range(L):
                pool.wait_ge(c_var, l + 1)
                g.tensor_tensor(rstdc[:], varc[:], mhalf[:], ALU.pow).then_inc(c_rstd, 1)
                if l == 0:
                    norm_scale((2, "mem", 0))
                pool.wait_ge(proj2_ready, 8 * l + 5)
                for t in range(NT):
                    ins = g.tensor_copy(nqp[:, t, :].rearrange("p (r g d) -> p g r d", r=4, g=2),
                                        proj2[:, t, NQ:NQ + 512].rearrange("p (g r d) -> p g r d", g=2, r=4))
                ins.then_inc(kd_ready, 1)
                pool.wait_ge(proj2_ready, 8 * l + 6)
                for e in range(2):
                    ins = g.tensor_copy(kdup[:, :, :, e, :],
                                        proj2[:, :, KC:KC + 256].rearrange("p t (q d) -> p t q d", q=4))
                ins.then_inc(kd_ready, 1)
                norm_scale((2, "1", l))
                norm_scale((2, "2", l))
                low_parts(ti[(2, "xo", l, 3)])
                norm_scale((2, "3", l))
                low_parts(ti[(2, "d", l, FS - 1)])


_NAMES = [
    "x", "p", "positions", "ln_in_g", "ln_in_b", "w_in", "attn_sinks", "idx_k_g", "idx_k_b", "w_o", "ln1_g", "ln1_b",
    "w_gu", "w_down", "w_pg", "w_pp", "ln2_g", "ln2_b", "mem_2", "ln_in_g_2", "ln_in_b_2", "ln_mem_g_2",
    "ln_mem_b_2", "w_in_2", "mla_cq_g_2", "mla_w_uq_2", "mla_ckv_g_2", "mla_w_ukv_2", "nsa_pe_k_2", "nsa_w1_k_2",
    "nsa_b1_k_2", "nsa_w2_k_2", "nsa_pe_v_2", "nsa_w1_v_2", "nsa_b1_v_2", "nsa_w2_v_2", "w_out_2", "ln1_g_2",
    "ln1_b_2", "xa_wq_2", "xa_wkv_2", "xa_wo_2", "ln2_g_2", "ln2_b_2", "ffn_w_up_2", "ffn_conv_w_2",
    "ffn_conv_b_2", "ffn_w_down_2", "ln3_g_2", "ln3_b_2",
]


def kernel(**inputs):
    import concourse.bacc as bacc
    from concourse.bass_utils import run_bass_kernel_spmd

    nc = bacc.Bacc("TRN2", target_bir_lowering=False, num_devices=1, dynamic_dma_scratch_size=1024)
    arrays, w, c = {}, {}, {}
    for name in _NAMES:
        a = np.ascontiguousarray(inputs[name])
        arrays[f"in_{name}"] = a
        w[name] = nc.dram_tensor(f"in_{name}", a.shape, mybir.dt.from_np(a.dtype), kind="ExternalInput").ap()
    for name, a in constants().items():
        arrays[f"table_{name}"] = a
        c[name] = nc.dram_tensor(f"table_{name}", a.shape, F32, kind="ExternalInput").ap()
    out = nc.dram_tensor("out_0", (1, S, D), F32, kind="ExternalOutput").ap()
    build(nc, w, c, out)
    r = run_bass_kernel_spmd(nc, [arrays], core_ids=[0])
    return r.results[0]["out_0"]
```

```python
from contextlib import ExitStack
import math

import numpy as np

import concourse.bass as bass
from concourse import mybir

F32 = mybir.dt.float32
F32R = mybir.dt.float32r
I32 = mybir.dt.int32
ALU = mybir.AluOpType
ACT = mybir.ActivationFunctionType
AX = mybir.AxisListType

P = 128
S = 256
NT = S // P
D = 1024
KD = D // P
L = 2
TC = 256
FF = 2816
FS = FF // TC
H = 8
DH = 64
LN_EPS = 1e-5
RMS_EPS = 1e-6
ALPHA = (2 * L) ** 0.25
MASKED = -1e31
NEG = -1e30
TAKEN = -3e38
TOPK = min(256, S // 4)
LOWEST = -3.4e38

QA, KA, VA, QB, KB, VB, QI, KI, WI, IN1 = 0, 512, 640, 768, 1280, 1344, 1408, 1664, 1696, 1704
IN1_ORDER = (6, 5, 3, 4, 0, 1, 2)
CQ, CKV, KR, NQ, KC, KSL, VSL, KWN, VWN, GL, IN2 = 0, 384, 640, 672, 1184, 1440, 1568, 1696, 1824, 1952, 1976
QR, KVR = 384, 256
XR = 2 * NT
NC = 15
MD = 96
KVW = 160

SLOTS1 = (0, 1, 2, 3, 4, 5, 6, 8)
SLOTS2 = (0, 2, 4, 6, 8, 10, 11, 12)
NL = 5
NW = 3

SWA, DSA, SLC, WIN, MLA = "swa", "dsa", "slc", "win", "mla"


def constants():
    i = np.arange(P)[:, None]
    j = np.arange(S)[None, :]
    diag = (j - P) > i
    causal = np.where(diag, MASKED, 0.0)
    band = np.where(diag | ((j < P) & (j <= i)), MASKED, 0.0)
    slope = 2.0 ** -np.arange(1, H + 1)
    dist = P + i - j
    alibi = np.where(dist[:, None, :] < 0, MASKED, -slope[None, :, None] * dist[:, None, :] * DH ** 0.5)
    t = np.arange(NT)[None, :, None, None] * P + i[:, :, None, None]
    end = np.arange(NC + 1)[None, None, None, :] * 16 + 31
    ok = (end <= t) & (end < NC * 16 + 31)
    cmp = np.where(ok, -slope[None, None, :, None] * (t - end), NEG)
    valid = (np.arange(NT)[None, :] * P + i >= 31).astype(np.float64)
    inv = (10000.0 ** -(np.arange(32) / 32)).astype(np.float32)
    ang = (np.arange(S, dtype=np.float32)[:, None] * inv[None, ::2]).astype(np.float32)
    ang = ang.reshape(NT, P, 16).transpose(1, 0, 2).reshape(P, NT * 16)
    out = {
        "ident": np.eye(P), "causal": causal, "band": band, "alibi": alibi.reshape(P, H * S),
        "cmpbias": cmp.reshape(P, NT * H * (NC + 1)), "valid": valid,
        "inv": np.broadcast_to(inv, (P, 32)), "mcos": np.cos(ang), "msin": np.sin(ang),
    }
    return {k: np.ascontiguousarray(v, dtype=np.float32) for k, v in out.items()}


def during_attention(block, l):
    return [(block - 1, 4 * l + k) for k in range(4)]


def down_steps(s):
    return [s - 1] if 1 <= s <= FS - 3 else {FS - 1: [FS - 3], FS: [FS - 2, FS - 1]}.get(s, [])


def plan_tiles(w):
    tiles = []

    def rows(a):
        return a.rearrange("(k p) n -> p k n", p=P)

    def ffn(block, l, gate, up, down):
        def gu(s):
            tiles.append(((block, "g", l, s), gate[:, :, s * TC:(s + 1) * TC]))
            tiles.append(((block, "u", l, s), up[:, :, s * TC:(s + 1) * TC]))

        def d(s):
            tiles.append(((block, "d", l, s), down[:, 2 * s:2 * s + 2, :]))
        for s in range(FS + 1):
            if s < FS:
                gu(s)
            for j in down_steps(s):
                d(j)

    def memory_tiles(block, l):
        for lm, k in during_attention(block, l):
            tiles.append(((2, "kv", lm, k), rows(w["xa_wkv_2"][lm])[:, :, k * TC:(k + 1) * TC]))

    for l in range(L):
        tiles.append(((1, "pp", l, 0), rows(w["w_pp"][l])))
        for k in IN1_ORDER:
            tiles.append(((1, "in", l, k), rows(w["w_in"][l])[:, :, k * TC:min((k + 1) * TC, IN1)]))
        memory_tiles(1, l)
        for k in range(4):
            tiles.append(((1, "o", l, k), rows(w["w_o"][l])[:, :, k * TC:(k + 1) * TC]))
        for k in range(4):
            tiles.append(((1, "pg", l, k), rows(w["w_pg"][l])[:, :, k * TC:(k + 1) * TC]))
        gu = rows(w["w_gu"][l])
        ffn(1, l, gu[:, :, 0:FF], gu[:, :, FF:2 * FF], rows(w["w_down"][l]))
    for l in range(L):
        for k in range(8):
            tiles.append(((2, "in", l, k), rows(w["w_in_2"][l])[:, :, k * TC:min((k + 1) * TC, IN2)]))
        for k in range(2):
            tiles.append(((2, "uq", l, k), rows(w["mla_w_uq_2"][l])[:, :, k * 384:(k + 1) * 384]))
        tiles.append(((2, "ukv", l, 0), rows(w["mla_w_ukv_2"][l])))
        tiles.append(((2, "w1", l, 0), rows(w["nsa_w1_k_2"][l])))
        tiles.append(((2, "w1", l, 1), rows(w["nsa_w1_v_2"][l])))
        memory_tiles(2, l)
        for name, key, n in (("out", "w_out_2", 4), ("xq", "xa_wq_2", 4), ("xo", "xa_wo_2", 4)):
            for k in range(n):
                tiles.append(((2, name, l, k), rows(w[key][l])[:, :, k * TC:(k + 1) * TC]))
        up = rows(w["ffn_w_up_2"][l])
        ffn(2, l, up[:, :, FF:2 * FF], up[:, :, 0:FF], rows(w["ffn_w_down_2"][l]))
    return tiles, {key: c for c, (key, _) in enumerate(tiles)}


def plan_units():
    units = []
    for l in range(L):
        units += [(1, l, kind, t) for kind in (SWA, DSA) for t in range(NT)]
    for l in range(L):
        units += [(2, l, kind, t) for kind in (SLC, WIN, MLA) for t in range(NT)]
    chunk0, m = [], 0
    for _, _, _, t in units:
        for _ in range(2):
            chunk0.append(m)
            m += t + 1
    chunk0.append(m)
    return units, chunk0


def build(nc, w, c, out):
    tiles, ti = plan_tiles(w)
    units, chunk0 = plan_units()
    n_tiles = len(tiles)

    slots = {1: SLOTS1, 2: SLOTS2}

    def memory_slot(block, l, step):
        if step not in slots[block]:
            return None
        return 16 * (block - 1) + 8 * l + slots[block].index(step)

    def unit0(block, l):
        return next(u for u, x in enumerate(units) if x[0] == block and x[1] == l)

    with ExitStack() as ctx:
        def sb(name, shape, dt=F32):
            return ctx.enter_context(nc.sbuf_tensor(name, [P] + shape, dt))

        def sem(name):
            return ctx.enter_context(nc.semaphore(name))

        with nc.sbuf_tensor("raw", [P, NL, 2048], F32) as raw:
            pass
        wlo = sb("wlo", [NL, 2048], F32R)
        whi = sb("whi", [NW, 2048], F32R)
        xtok = sb("xtok", [NT, D])
        sy = sb("sy", [2, 2048])
        xhi = sb("xhi", [KD, S], F32R)
        xlo = sb("xlo", [KD, S], F32R)
        gb = sb("gb", [2, D])
        r1 = sb("r1", [4096])
        r2 = sb("r2", [4608])
        r3 = sb("r3", [4096])
        rt = sb("rt", [2048])
        pt = sb("pt", [4, 512])
        plo = sb("plo", [512], F32R)
        rr = sb("rr", [2560], F32R)
        ident = sb("ident", [P])
        causal = sb("causal", [S])
        band = sb("band", [S])
        inv = sb("inv", [32])
        pos_i = sb("pos_i", [NT], I32)
        pos_f = sb("pos_f", [NT])
        cos64 = sb("cos64", [NT, 64])
        sin64 = sb("sin64", [NT, 64])
        cos32 = sb("cos32", [NT, 32])
        sin32 = sb("sin32", [NT, 32])
        pcol = sb("pcol", [5, P])
        stats = sb("stats", [NT, 4, 6])
        meanvar = sb("meanvar", [NT, 2])
        vare = sb("vare", [4])
        rstd = sb("rstd", [4])
        mhalf = sb("mhalf", [4])
        sinkb = sb("sinkb", [L, H])
        ikg = sb("ikg", [L, 2, 32])
        wi_s = sb("wi_s", [NT, H])
        top8 = sb("top8", [8])
        mx = sb("mx", [2, H])
        nmx = sb("nmx", [2, H])
        den = sb("den", [2, H])
        rden = sb("rden", [2, H])
        esink = sb("esink", [2, 2, H])
        memhi = sb("memhi", [KD, S], F32R)
        memlo = sb("memlo", [KD, S], F32R)
        cmpbias = sb("cmpbias", [NT, H * 16])
        valid = sb("valid", [NT])
        mcos = sb("mcos", [NT, 16])
        msin = sb("msin", [NT, 16])
        w2s = sb("w2s", [L, 2, DH])
        hcmp = sb("hcmp", [2, 2 * NC])
        kct = sb("kct", [16])
        vbd = sb("vbd", [2, 4 * DH])
        krope = sb("krope", [NT, 32])
        gates = sb("gates", [NT, 3 * H])
        varc = sb("varc", [4])
        rstdc = sb("rstdc", [4])
        cmx = sb("cmx", [NT * H])
        cden = sb("cden", [NT * H])
        coef = sb("coef", [NT * H])
        otmp = sb("otmp", [H * DH])
        xmx = sb("xmx", [NT, 4])
        xden = sb("xden", [NT, 4])
        psw = ctx.enter_context(nc.psum_tensor("psw", [P, 4, 512], F32))
        psa = ctx.enter_context(nc.psum_tensor("psa", [P, 4, 512], F32))

        tile_loaded = [sem(f"tile_loaded{i}") for i in range(NL)]
        hi_ready = sem("hi_ready")
        lo_ready = sem("lo_ready")
        tile_done = sem("tile_done")
        ident_loaded = sem("ident_loaded")
        angles_loaded = sem("angles_loaded")
        consts_loaded = sem("consts_loaded")
        params_loaded = sem("params_loaded")
        x_loaded = sem("x_loaded")
        p_loaded = sem("p_loaded")
        gb_loaded = sem("gb_loaded")
        params_turned = sem("params_turned")
        mhalf_ready = sem("mhalf_ready")
        angles_ready = sem("angles_ready")
        sines_ready = sem("sines_ready")
        tables_ready = sem("tables_ready")
        ln_var = sem("ln_var")
        ln_rstd = sem("ln_rstd")
        lo_pool = sem("lo_pool")
        part_done = sem("part_done")
        joined = sem("joined")
        x_ready = sem("x_ready")
        act_turned = sem("act_turned")
        act_hi = sem("act_hi")
        act_ready = sem("act_ready")
        p_turned = sem("p_turned")
        p_hi = sem("p_hi")
        p_ready = sem("p_ready")
        pp_part = sem("pp_part")
        pp_ready = sem("pp_ready")
        proj_ready = sem("proj_ready")
        ki_var = sem("ki_var")
        ki_rstd = sem("ki_rstd")
        qki_roped = sem("qki_roped")
        qkb_roped = sem("qkb_roped")
        qka_roped = [sem(f"qka_roped{t}") for t in range(NT)]
        heads_turned = sem("heads_turned")
        heads_ready = sem("heads_ready")
        iscores_done = sem("iscores_done")
        relu_done = sem("relu_done")
        icomb_done = sem("icomb_done")
        scores_done = sem("scores_done")
        smax_done = sem("smax_done")
        exp_done = sem("exp_done")
        pt_done = sem("pt_done")
        pt_ready = sem("pt_ready")
        pv_done = sem("pv_done")
        o_ready = sem("o_ready")
        pg_exp = sem("pg_exp")
        gate_ready = sem("gate_ready")
        hid_ready = sem("hid_ready")
        stored = sem("stored")
        alibi_loaded = sem("alibi_loaded")
        mem_loaded = sem("mem_loaded")
        proj2_ready = sem("proj2_ready")
        c_var = sem("c_var")
        c_rstd = sem("c_rstd")
        c_normed = sem("c_normed")
        c_turned = sem("c_turned")
        c_v = sem("c_v")
        cT_ready = sem("cT_ready")
        gate_exp = sem("gate_exp")
        qm_ready = sem("qm_ready")
        qm_roped = sem("qm_roped")
        kd_ready = sem("kd_ready")
        nsa_turned = sem("nsa_turned")
        nsa_ready = sem("nsa_ready")
        kvm_ready = sem("kvm_ready")
        km_roped = sem("km_roped")
        mla_turned = sem("mla_turned")
        mla_ready = sem("mla_ready")
        cmp_x = sem("cmp_x")
        cmp_added = sem("cmp_added")
        cmp_gelu = sem("cmp_gelu")
        cmp_kv = sem("cmp_kv")
        cmp_kv_ready = sem("cmp_kv_ready")
        cmp_scores = sem("cmp_scores")
        cmp_shifted = sem("cmp_shifted")
        cmp_exp = sem("cmp_exp")
        cmp_turned = sem("cmp_turned")
        cmp_pT = sem("cmp_pT")
        cmp_pv = sem("cmp_pv")
        cmp_o = sem("cmp_o")
        kv_part = sem("kv_part")
        kv_staged = sem("kv_staged")
        kv_stored = [sem(f"kv_stored{i}") for i in range(2)]
        kv_loaded = sem("kv_loaded")
        xq_ready = sem("xq_ready")
        xs_done = sem("xs_done")
        xmax_done = sem("xmax_done")
        xexp_done = sem("xexp_done")
        xp_ready = sem("xp_ready")
        xp_turned = sem("xp_turned")
        xpT_ready = sem("xpT_ready")
        conv_first = sem("conv_first")
        conv_done = sem("conv_done")

        prow = r3[:, 0:5 * P].rearrange("p (j c) -> p j c", j=5)
        angs = r3[:, 1024:1024 + 6 * NT * 32].rearrange("p (j c) -> p j c", j=6)
        iscore = r3[:, 13 * S:13 * S + NT * S].rearrange("p (t k) -> p t k", t=NT)
        dmask = r2[:, NT * 13 * P:NT * 13 * P + NT * S].rearrange("p (t k) -> p t k", t=NT)
        memory = sy[:, 1, :].rearrange("p (t d) -> p t d", t=NT)
        gb2 = r3[:, 0:2 * D].rearrange("p (i d) -> p i d", i=2)
        gbm = r3[:, 2 * D:4 * D].rearrange("p (i d) -> p i d", i=2)
        soft = sy[:].rearrange("p b (h k) -> p b h k", h=H)
        proj1 = r1[:, 0:NT * IN1].rearrange("p (t c) -> p t c", t=NT)
        roped = r2[:, 0:NT * 13 * P].rearrange("p (t c) -> p t c", t=NT)
        omix = r2[:, 0:NT * D].rearrange("p (t c) -> p t c", t=NT)
        headT = r3[:, 0:13 * S].rearrange("p (b s) -> p b s", b=13)
        relu = sy[:, 1, :].rearrange("p (h k) -> p h k", h=H)
        ple = rt[:].rearrange("p (t d) -> p t d", t=NT)
        ptok = pt[:, 0, :].rearrange("p (t d) -> p t d", t=NT)
        pT_hi = rr[:, 2048:2560].rearrange("p (k s) -> p k s", k=2)
        pT_lo = plo[:].rearrange("p (k s) -> p k s", k=2)
        stage = [r1[:, 3584:4096].rearrange("p (b c) -> p b c", b=2), gb[:, 1, 512:1024].rearrange("p (b c) -> p b c", b=2)]
        hidh = rr[:, 0:1024].rearrange("p (b c s) -> p b c s", b=2, c=2)
        hidl = rr[:, 1024:2048].rearrange("p (b c s) -> p b c s", b=2, c=2)
        alibi = rt[:].rearrange("p (h k) -> p h k", h=H)
        proj2 = r1[:, 0:NT * IN2].rearrange("p (t c) -> p t c", t=NT)
        qm = r2[:, 0:NT * H * MD].rearrange("p (t c) -> p t c", t=NT)
        kvm = r2[:, 2048:2048 + NT * H * KVW].rearrange("p (t h c) -> p t h c", t=NT, h=H)
        ctmp = r3[:, 0:5 * S].rearrange("p (k s) -> p k s", k=5)
        mqT = r3[:, 0:H * S].rearrange("p (h s) -> p h s", h=H)
        mkT = r3[:, H * S:2 * H * S].rearrange("p (h s) -> p h s", h=H)
        nsaT = gb[:].rearrange("p a b -> p (a b)")[:, 0:6 * S].rearrange("p (b s) -> p b s", b=6)
        cT_hi = rr[:, 0:5 * S].rearrange("p (k s) -> p k s", k=5)
        cT_lo = rr[:, 5 * S:10 * S].rearrange("p (k s) -> p k s", k=5)
        kdup = sy[:, 0, 0:1024].rearrange("p (t q e d) -> p t q e d", t=NT, q=4, e=2)
        nqp = sy[:, 1, 0:1024].rearrange("p (t c) -> p t c", t=NT)
        mtmp = sy[:, 0, 1024:2048].rearrange("p (i c) -> p i c", i=4)
        pcmp = pt[:, 0, :].rearrange("p (t h n) -> p t h n", t=NT, h=H)
        cx = pt[:, 1:3, :].rearrange("p a b -> p (a b)").rearrange("p (q s) -> p q s", q=4)
        cf = pt[:, 3, 0:16 * 2 * NC].rearrange("p (j g n) -> p j g n", j=16, g=2)
        scmp = pt[:, 3, 0:NT * H * 16].rearrange("p (t c) -> p t c", t=NT)
        pcT = pt[:, 1, :].rearrange("p (j q) -> p j q", j=4)
        cx_both = [rr[:, 1000 * i:1000 * i + 960].rearrange("p (j c) -> p j c", j=16) for i in range(2)]
        cx_hi = [x[:, :, 0:2 * NC] for x in cx_both]
        cx_lo = [x[:, :, 2 * NC:4 * NC] for x in cx_both]
        xkT = r1[:, 0:2048].rearrange("p (k s) -> p k s", k=KD)
        xvt = r1[:, 2048:4096].rearrange("p (t d) -> p t d", t=NT)
        xqT = r3[:, 0:2048].rearrange("p (k s) -> p k s", k=KD)
        xsoft = sy[:, 0, :].rearrange("p (t h k) -> p t h k", t=NT, h=4)
        hidf = r1[:, 0:512]
        conv_a = r1[:, 1536:2560].rearrange("p (b c s) -> p b c s", b=2, c=2)
        conv_g = r1[:, 2560:3584].rearrange("p (b c s) -> p b c s", b=2, c=2)
        gact = r1[:, 512:1536].rearrange("p (b c) -> p b c", b=2)
        egate = r1[:, 1536:3584].rearrange("p (b c) -> p b c", b=4)

        def tile_view(buf, n, i):
            ap = tiles[i][1]
            kt, cols = ap.shape[1], ap.shape[2]
            return buf[:, i % n, 0:kt * cols].rearrange("p (k c) -> p k c", k=kt)

        def tile_flat(buf, n, i):
            ap = tiles[i][1]
            return buf[:, i % n, 0:ap.shape[1] * ap.shape[2]]

        def bank2(ps, b):
            return ps[:, b, :].rearrange("p (t c) -> p t c", t=2)

        def residual_banks(k):
            return [bank2(psw, k)[:, 0, :], bank2(psw, k % 2)[:, 1, :]]

        def bc(ap, n):
            return ap.unsqueeze(1).broadcast_to([P, n, ap.shape[1]])

        def bci(ap, n):
            return ap.unsqueeze(2).broadcast_to([P, ap.shape[1], n])

        norms = {}

        def add_norm(key, g, b, place=gb):
            norms[key] = dict(n=len(norms), g=g, b=b, place=place, loads=sum("g" in x for x in norms.values()) + 1)
        add_norm((1, "in", 0), w["ln_in_g"], w["ln_in_b"])
        norms[(2, "mem", 0)] = dict(n=1, place=gbm)
        for l in range(L):
            add_norm((1, "1", l), w["ln1_g"][l], w["ln1_b"][l])
            add_norm((1, "2", l), w["ln2_g"][l], w["ln2_b"][l])
        add_norm((2, "in", 0), w["ln_in_g_2"], w["ln_in_b_2"], gb2)
        for l in range(L):
            add_norm((2, "1", l), w["ln1_g_2"][l], w["ln1_b_2"][l])
            add_norm((2, "2", l), w["ln2_g_2"][l], w["ln2_b_2"][l])
            add_norm((2, "3", l), w["ln3_g_2"][l], w["ln3_b_2"][l])

        gb_before = {1: (1, "in", 0)}
        for l in range(L):
            gb_before[ti[(1, "in", l, IN1_ORDER[6])]] = (1, "1", l)
            gb_before[ti[(1, "g", l, 2)]] = (1, "2", l)
            gb_before[ti[(2, "xq", l, 1)]] = (2, "1", l)
            gb_before[ti[(2, "xo", l, 0)]] = (2, "2", l)
            gb_before[ti[(2, "g", l, 3)]] = (2, "3", l)
        gb_before[ti[(1, "g", 1, 4)]] = (2, "in", 0)

        turn_keys = [(1, "in", 0), (2, "mem", 0)]
        for l in range(L):
            turn_keys += [(1, "mix", l), (1, "1", l)] + ([(1, "2", l)] if l + 1 < L else [])
        turn_keys += [(2, "in", 0)]
        for l in range(L):
            turn_keys += [(2, "mix", l), (2, "1", l), (2, "xa", l), (2, "2", l)] + ([(2, "3", l)] if l + 1 < L else [])
        turn = {key: e for e, key in enumerate(turn_keys)}

        last_tiles = []
        for l in range(L):
            last_tiles += [(1, "o", l, 3), (1, "d", l, FS - 1)]
        for l in range(L):
            last_tiles += [(2, "out", l, 3), (2, "xo", l, 3), (2, "d", l, FS - 1)]
        part = {key: q + 1 for q, key in enumerate(last_tiles)}
        pool_tiles = [1, 3, 5] + [ti[key] + q for key in last_tiles for q in (2, 3)]
        pool_tiles += [ti[(2, "kv", l, k)] + NW for l in range(L) for k in range(8)]
        pool_tiles = sorted(i for i in pool_tiles if i < n_tiles)
        kv_halves = nc.dram_tensor("kv_halves", (L * 8 * 2, P, TC), F32, kind="Internal").ap()

        angle_dmas = [(inv[:], c["inv"])]
        angle_dmas += [(pos_i[:, t:t + 1], w["positions"][0, t * P:(t + 1) * P].rearrange("(p o) -> p o", o=1))
                       for t in range(NT)]
        const_dmas = [(causal[:], c["causal"]), (band[:], c["band"])]
        for l in range(L):
            const_dmas += [(sinkb[:, l, :], w["attn_sinks"][l].partition_broadcast(P)),
                           (ikg[:, l, 0, :], w["idx_k_g"][l].partition_broadcast(P)),
                           (ikg[:, l, 1, :], w["idx_k_b"][l].partition_broadcast(P))]
        param_dmas = []
        param_rows = [0] * 5

        def add_param(j, row, vec):
            n = vec.shape[0] // P
            param_dmas.append((prow[row:row + n, j, :], vec.rearrange("(r c) -> r c", c=P)))
            param_rows[j] = max(param_rows[j], row + n)
        const_dmas += [(cmpbias[:].rearrange("p t c -> p (t c)"), c["cmpbias"]), (valid[:], c["valid"]),
                       (mcos[:].rearrange("p t c -> p (t c)"), c["mcos"]),
                       (msin[:].rearrange("p t c -> p (t c)"), c["msin"])]
        def cqg_row(l): return 3 * l
        def ckvg_row(l): return 6 + 2 * l
        def b1_row(l, i): return 10 + 2 * l + i
        def pe_row(l, i): return 14 + 16 * (2 * l + i)
        for l in range(L):
            const_dmas += [(w2s[:, l, 0, :], w["nsa_w2_k_2"][l]), (w2s[:, l, 1, :], w["nsa_w2_v_2"][l])]
            add_param(0, cqg_row(l), w["mla_cq_g_2"][l])
            add_param(0, ckvg_row(l), w["mla_ckv_g_2"][l])
            for i, kv in enumerate("kv"):
                add_param(0, b1_row(l, i), w[f"nsa_b1_{kv}_2"][l])
                add_param(0, pe_row(l, i), w[f"nsa_pe_{kv}_2"][l].rearrange("c d -> (c d)"))
            for j in range(3):
                add_param(1 + 2 * l + j // 2, 44 * (j % 2), w["ffn_conv_w_2"][l, j])
            add_param(2 + 2 * l, 44, w["ffn_conv_b_2"][l])
        head_groups = [(10, 11), (12,), (5, 6), (7, 8), (9,), (0, 1), (2, 3), (4,)]
        n_const_dmas, n_param_dmas = len(const_dmas), len(param_dmas)
        block = ctx.enter_context(nc.Block())

        @block.sync
        def _(sp):
            for t in range(NT):
                sp.dma_start(xtok[:, t, :], w["x"][0, t * P:(t + 1) * P, :]).then_inc(x_loaded, 16)
            sp.dma_start(ident[:], c["ident"]).then_inc(ident_loaded, 16)

            def load_gb(key):
                x = norms[key]
                if x["place"] is gb2:
                    sp.wait_ge(x_ready, XR * (norms[(1, "1", 1)]["n"] + 1))
                elif x["n"]:
                    sp.wait_ge(x_ready, XR * max(z["n"] + 1 for z in norms.values() if z["place"] is gb and z["n"] < x["n"]))
                sp.dma_start(x["place"][:, 0, :], x["g"].partition_broadcast(P)).then_inc(gb_loaded, 16)
                sp.dma_start(x["place"][:, 1, :], x["b"].partition_broadcast(P)).then_inc(gb_loaded, 16)

            small = [(dst, src, consts_loaded) for dst, src in const_dmas]
            small += [(dst, src, params_loaded) for dst, src in param_dmas]
            for i in range(n_tiles):
                key = tiles[i][0]
                if key[1] == "xq" and key[3] == 1:
                    l = key[2]
                    sp.wait_ge(o_ready, unit0(2, l) + 6)
                    for stored_half in kv_stored:
                        sp.wait_ge(stored_half, 16 * (8 + 4 * (l + 1)))
                    load_gb(gb_before[i])
                    mine = kv_halves[16 * l:16 * (l + 1)]
                    sp.dma_start(xkT, mine[0:8].rearrange("n p s -> p n s")).then_inc(kv_loaded, 16)
                    for t in range(NT):
                        sp.dma_start(xvt[:, t, :].rearrange("p (k c) -> p k c", k=4),
                                     mine[8 + t:16:2].rearrange("k p c -> p k c")).then_inc(kv_loaded, 16)
                elif i in gb_before:
                    load_gb(gb_before[i])
                if i >= NL:
                    sp.wait_ge(tile_done, i - NL + 1)
                if key == (1, "d", 1, FS - 1):
                    sp.wait_ge(hid_ready, FS + 5)
                    sp.dma_start(rt[:], c["alibi"]).then_inc(alibi_loaded, 16)
                if key[1] == "pp":
                    if key[2] >= 1:
                        sp.wait_ge(x_ready, XR * (norms[(1, "1", key[2] - 1)]["n"] + 1))
                    sp.dma_start(ptok, w["p"][key[2], 0].rearrange("(t p) d -> p t d", p=P)).then_inc(p_loaded, 16)
                sp.dma_start(tile_view(raw, NL, i), tiles[i][1]).then_inc(tile_loaded[i % NL], 16)
                if i == 2:
                    for t in range(NT):
                        sp.dma_start(memory[:, t, :], w["mem_2"][0, t * P:(t + 1) * P, :]).then_inc(mem_loaded, 16)
                    for j, vec in enumerate((w["ln_mem_g_2"], w["ln_mem_b_2"])):
                        sp.dma_start(gbm[:, j, :], vec.partition_broadcast(P)).then_inc(mem_loaded, 16)
                if i == 0:
                    for dst, src in angle_dmas:
                        sp.dma_start(dst, src).then_inc(angles_loaded, 16)
                if i >= 2:
                    for dst, src, loaded in small[0:8]:
                        sp.dma_start(dst, src).then_inc(loaded, 16)
                    small = small[8:]
            sp.wait_ge(stored, 16 * NT)
            for stored_half in kv_stored:
                sp.wait_ge(stored_half, 16 * 8 * L)

        @block.tensor
        def _(pe):
            def take(key):
                i = ti[key]
                if i in pool_tiles:
                    pe.wait_ge(lo_pool, sum(1 for x in pool_tiles if x <= i))
                else:
                    pe.wait_ge(lo_ready, i + 1 - sum(1 for x in pool_tiles if x <= i))
                return tile_view(whi, NW, ti[key]), tile_view(wlo, NL, ti[key])

            def product(o, lh, ll, rh, rl, first, last):
                pe.matmul(o, lh, rh, start=first, stop=False)
                pe.matmul(o, lh, rl, start=False, stop=False)
                return pe.matmul(o, ll, rh, start=False, stop=last)

            def by_tokens(key, outs, ah, al, ready=None):
                wh, wl = take(key)
                kt = wh.shape[1]
                for t in range(NT):
                    for k in range(kt):
                        if ready is not None and t == 0 and k % 2 == 0:
                            pe.wait_ge(act_ready, 4 * turn[ready] + k // 2 + 1)
                        tok = slice(t * P, (t + 1) * P)
                        ins = product(outs[t], ah[:, k, tok], al[:, k, tok], wh[:, k, :], wl[:, k, :],
                                      k == 0, k == kt - 1)
                ins.then_inc(tile_done, 1)

            def before_norm(block, name, l, ready):
                for k in range(2):
                    by_tokens((block, name, l, k), residual_banks(k), xhi, xlo, ready if k == 0 else None)
                pair = [take((block, name, l, k)) for k in (2, 3)]
                for t in range(NT):
                    if t:
                        pe.wait_ge(joined, 2 + 2 * sum(1 for x in last_tiles[:last_tiles.index((block, name, l, 3))]
                                                       if x[1] != "d"))
                    for k, (wh, wl) in zip((2, 3), pair):
                        tok = slice(t * P, (t + 1) * P)
                        for kk in range(KD):
                            ins = product(residual_banks(k)[t], xhi[:, kk, tok], xlo[:, kk, tok], wh[:, kk, :],
                                          wl[:, kk, :], kk == 0, kk == KD - 1)
                        if t == 1:
                            ins.then_inc(tile_done, 1)
                        elif k == 3:
                            ins.then_inc(part_done, 1)

            def by_features(key, bank, ah, al, ready=None):
                wh, wl = take(key)
                kt = wh.shape[1]
                for ch in range(TC // P):
                    for k in range(kt):
                        if ready is not None and ch == 0 and k % 2 == 0:
                            pe.wait_ge(act_ready, 4 * turn[ready] + k // 2 + 1)
                        cols = slice(ch * P, (ch + 1) * P)
                        ins = product(bank[:, ch, :], wh[:, k, cols], wl[:, k, cols], ah[:, k, :], al[:, k, :],
                                      k == 0, k == kt - 1)
                ins.then_inc(tile_done, 1)

            def turns(src, ps):
                for b in range(4):
                    for kk in range(2):
                        for t in range(NT):
                            k = 2 * b + kk
                            ins = pe.transpose(ps[:, b, kk * S + t * P:kk * S + (t + 1) * P],
                                               src[:, t, k * P:(k + 1) * P], ident[:])
                    ins.then_inc(act_turned, 1)

            def norm_turns(key, ps, src=xtok):
                for t in range(NT):
                    for b in range(4):
                        if b % 2 == 0:
                            pe.wait_ge(x_ready, XR * norms[key]["n"] + 2 * t + b // 2 + 1)
                        for kk in range(2):
                            k = 2 * b + kk
                            ins = pe.transpose(ps[:, b, kk * S + t * P:kk * S + (t + 1) * P],
                                               src[:, t, k * P:(k + 1) * P], ident[:])
                        if t == NT - 1:
                            ins.then_inc(act_turned, 1)

            def p_turns(l, bank):
                pe.wait_ge(p_loaded, 16 * (l + 1))
                for kk in range(2):
                    for t in range(NT):
                        ins = pe.transpose(psw[:, bank, kk * S + t * P:kk * S + (t + 1) * P],
                                           ptok[:, t, kk * P:(kk + 1) * P], ident[:])
                ins.then_inc(p_turned, 1)

            def memory_half(n):
                key, half = (2, "kv", n // 16, n // 2 % 8), n % 2
                if half == 0:
                    wh, wl = take(key)
                else:
                    wh, wl = tile_view(whi, NW, ti[key]), tile_view(wlo, NL, ti[key])
                if n:
                    pe.wait_ge(kv_staged, n)
                piece = slice(half * P, (half + 1) * P)
                for k in range(KD):
                    if key[3] < 4:
                        ins = product(psa[:, 3, 0:TC], wh[:, k, piece], wl[:, k, piece], memhi[:, k, :],
                                      memlo[:, k, :], k == 0, k == KD - 1)
                    else:
                        ins = product(psa[:, 3, 0:TC], memhi[:, k, piece], memlo[:, k, piece], wh[:, k, :],
                                      wl[:, k, :], k == 0, k == KD - 1)
                ins.then_inc(tile_done if half else kv_part, 1)

            def attention(block, l, qT, kT, v, before_second=lambda: None):
                first = 2 * unit0(block, l)
                count = 2 * sum(1 for x in units if x[0] == block and x[1] == l)
                for i in range(first, first + count + 2):
                    if i < first + count:
                        u, hf = divmod(i, 2)
                        kind, t = units[u][2:]
                        nk = (t + 1) * P
                        if i == first + 1:
                            before_second()
                        if i >= 2:
                            pe.wait_ge(smax_done, i - 1)
                        for b in range(2):
                            for a in range(2):
                                h = a * 4 + hf * 2 + b
                                ins = pe.matmul(psw[:, 2 * (i % 2) + a, b * S:b * S + nk],
                                                qT(kind, h, t), kT(kind, h, nk), start=True, stop=True)
                        ins.then_inc(scores_done, 1)
                    n = memory_slot(block, l, i - first)
                    if n is not None:
                        memory_half(n)
                    if i - 2 >= first:
                        n = i - 2
                        u, hf = divmod(n, 2)
                        kind, t = units[u][2:]
                        pe.wait_ge(pt_ready, chunk0[n + 1])
                        if hf == 0 and u >= 1:
                            pe.wait_ge(o_ready, u)
                        blk = [(b, a, kb) for b in range(2) for a in range(2) for kb in range(t + 1)]
                        for q, (b, a, kb) in enumerate(blk):
                            h = a * 4 + hf * 2 + b
                            m = chunk0[n] + q // 4
                            ins = pe.matmul(psa[:, 2, h * DH:(h + 1) * DH],
                                            pt[:, m % 4, (q % 4) * P:(q % 4 + 1) * P], v(kind, h, kb),
                                            start=(kb == 0), stop=(kb == t))
                        ins.then_inc(pv_done, 1)
                    if first <= i - 1 < first + count:
                        n = i - 1
                        u, hf = divmod(n, 2)
                        kind, t = units[u][2:]
                        pe.wait_ge(exp_done, n + 1)
                        blk = [(b, a, kb) for b in range(2) for a in range(2) for kb in range(t + 1)]
                        for q, (b, a, kb) in enumerate(blk):
                            h = a * 4 + hf * 2 + b
                            m = chunk0[n] + q // 4
                            if q % 4 == 0 and m >= 2:
                                pe.wait_ge(pt_ready, m - 1)
                            ins = pe.transpose(psa[:, m % 2, (q % 4) * P:(q % 4 + 1) * P],
                                               soft[:, u % 2, h, kb * P:(kb + 1) * P], ident[:])
                            if q % 4 == 3:
                                ins.then_inc(pt_done, 1)

            def ffn(block, l, f0, norm_key, before_last=lambda: None):
                for s in range(FS + 1):
                    f = f0 + s
                    if s < FS:
                        if f >= 2:
                            pe.wait_ge(hid_ready, f - 1)
                        by_features((block, "g", l, s), bank2(psw, 2 * (f % 2)), xhi, xlo,
                                    norm_key if s == 0 else None)
                        by_features((block, "u", l, s), bank2(psw, 2 * (f % 2) + 1), xhi, xlo)
                    for j in down_steps(s):
                        g = f0 + j
                        if j == FS - 1:
                            before_last()
                        pe.wait_ge(hid_ready, g + 1)
                        wh, wl = take((block, "d", l, j))
                        for t in range(NT):
                            for half in range(2):
                                for kk in range(2):
                                    tok = slice(t * P, (t + 1) * P)
                                    col = slice(half * 512, (half + 1) * 512)
                                    ins = product(psa[:, 2 * t + half, :], hidh[:, g % 2, kk, tok],
                                                  hidl[:, g % 2, kk, tok], wh[:, kk, col], wl[:, kk, col],
                                                  j == 0 and kk == 0, j == FS - 1 and kk == 1)
                            if j == FS - 1 and t == 0:
                                ins.then_inc(part_done, 1)
                        ins.then_inc(tile_done, 1)

            pe.wait_ge(ident_loaded, 16)
            p_turns(0, 0)
            for l in range(L):
                pe.wait_ge(p_ready, l + 1)
                wh, wl = take((1, "pp", l, 0))
                for k4 in range(4):
                    for t in range(NT):
                        for kk in range(2):
                            tok = slice(t * P, (t + 1) * P)
                            col = slice(k4 * TC, (k4 + 1) * TC)
                            ins = product(bank2(psw, k4)[:, t, :], pT_hi[:, kk, tok], pT_lo[:, kk, tok],
                                          wh[:, kk, col], wl[:, kk, col], kk == 0, kk == 1)
                    ins.then_inc(pp_part if k4 < 3 else tile_done, 1)
                x_in = (1, "in", 0) if l == 0 else (1, "2", l - 1)
                if l > 0:
                    pe.wait_ge(x_ready, XR * norms[x_in]["n"] + 3)
                norm_turns(x_in, psa)

                def head_turns(q):
                    for j, b in enumerate(head_groups[q]):
                        for t in range(NT):
                            ins = pe.transpose((psa if q < 2 else psw)[:, q % 4, j * S + t * P:j * S + (t + 1) * P],
                                               roped[:, t, b * P:(b + 1) * P], ident[:])
                    ins.then_inc(heads_turned, 1)

                def index_scores(t):
                    nk = (t + 1) * P
                    for h in range(H):
                        pr = slice(32 * (h % 4), 32 * (h % 4) + 32)
                        ins = pe.matmul(psa[:, h % 4, (h // 4) * S:(h // 4) * S + nk],
                                        headT[pr, 10 + h // 4, t * P:(t + 1) * P], headT[pr, 12, 0:nk],
                                        start=True, stop=True)
                    ins.then_inc(iscores_done, 1)
                for q, k in enumerate(IN1_ORDER):
                    if q < 4:
                        pe.wait_ge(pp_ready, 4 * l + q + 1)
                    else:
                        pe.wait_ge(proj_ready, 7 * l + q - 3)
                    cols = min(TC, IN1 - k * TC)
                    bank = bank2(psw, q % 4)
                    by_tokens((1, "in", l, k), [bank[:, t, 0:cols] for t in range(NT)], xhi, xlo,
                              x_in if q == 0 else None)
                    if l == 0 and q == 2:
                        norm_turns((2, "mem", 0), psa, memory)
                    if l == 0 and q == 4:
                        pe.wait_ge(act_ready, 4 * (turn[(2, "mem", 0)] + 1))
                        pe.wait_ge(params_loaded, 16 * n_param_dmas)
                        for j, n in enumerate(param_rows):
                            ins = pe.transpose(psa[:, 2 + j // 4, (j % 4) * P:(j % 4) * P + n], prow[0:n, j, :],
                                               ident[0:n, 0:n])
                        ins.then_inc(params_turned, 1)
                    if q == 4:
                        pe.wait_ge(qki_roped, NT * (l + 1))
                        head_turns(0)
                        head_turns(1)
                    if q == 5:
                        pe.wait_ge(heads_ready, 8 * l + 2)
                        index_scores(0)
                    if q == 6:
                        pe.wait_ge(relu_done, NT * l + 1)
                        index_scores(1)
                pe.wait_ge(proj_ready, 7 * (l + 1))
                for q in range(2, 8):
                    if q == 2:
                        pe.wait_ge(qkb_roped, NT * (l + 1))
                    if q == 5:
                        for t in range(NT):
                            pe.wait_ge(qka_roped[t], l + 1)
                    if q >= 6:
                        pe.wait_ge(heads_ready, 8 * l + q - 3)
                    head_turns(q)
                pe.wait_ge(heads_ready, 8 * (l + 1))
                pe.wait_ge(relu_done, NT * (l + 1))
                b0 = {SWA: 0, DSA: 5}
                attention(
                    1, l,
                    lambda kind, h, t: headT[64 * (h // 4):64 * (h // 4) + 64, b0[kind] + h % 4, t * P:(t + 1) * P],
                    lambda kind, h, nk: headT[64 * (h // 4):64 * (h // 4) + 64, b0[kind] + 4, 0:nk],
                    lambda kind, h, kb: (proj1[:, kb, VA + DH * (h // 4):VA + DH * (h // 4) + DH] if kind == SWA
                                         else proj1[:, kb, VB:VB + DH]))
                pe.wait_ge(o_ready, unit0(1, l) + 4)
                turns(omix, psw)
                before_norm(1, "o", l, (1, "mix", l))
                norm_turns((1, "1", l), psa)
                for k in range(4):
                    bank = bank2(psw, k)
                    by_tokens((1, "pg", l, k), [bank[:, t, :] for t in range(NT)], xhi, xlo,
                              (1, "1", l) if k == 0 else None)
                pe.wait_ge(pg_exp, 4 * (l + 1))
                if l + 1 < L:
                    ffn(1, l, FS * l, None, lambda: p_turns(l + 1, 2 * ((l + 1) * FS % 2)))
                else:
                    ffn(1, l, FS * l, None)

            norm_turns((2, "in", 0), psw)
            for l in range(L):
                x_in = (2, "in", 0) if l == 0 else (2, "3", l - 1)

                def latent_turns():
                    pe.wait_ge(c_normed, l + 1)
                    for b in range(3):
                        for kk in range(2 if b < 2 else 1):
                            for t in range(NT):
                                k = 2 * b + kk
                                ins = pe.transpose(psa[:, b, kk * S + t * P:kk * S + (t + 1) * P],
                                                   proj2[:, t, k * P:(k + 1) * P], ident[:])
                        ins.then_inc(c_turned, 1)

                for k in range(8):
                    if k >= 4:
                        pe.wait_ge(proj2_ready, 8 * l + k - 3)
                    cols = min(TC, IN2 - k * TC)
                    bank = bank2(psw, k % 4)
                    by_tokens((2, "in", l, k), [bank[:, t, 0:cols] for t in range(NT)], xhi, xlo,
                              x_in if k == 0 else None)
                    if k == 5:
                        latent_turns()
                pe.wait_ge(cT_ready, 3 * (l + 1))
                pe.wait_ge(proj2_ready, 8 * (l + 1))
                for j in range(2):
                    by_tokens((2, "uq", l, j), [psw[:, 2 * j + t, 0:384] for t in range(NT)],
                              cT_hi[:, 0:3, :], cT_lo[:, 0:3, :])
                for q in range(5):
                    if q == 0:
                        pe.wait_ge(kd_ready, 2 * l + 1)
                    if q == 3:
                        pe.wait_ge(kd_ready, 2 * l + 2)
                    if q == 4:
                        pe.wait_ge(nsa_ready, 5 * l + 1)
                    for kk in range(2):
                        for t in range(NT):
                            if q < 2:
                                src = nqp[:, t, (2 * q + kk) * P:(2 * q + kk + 1) * P]
                            elif q == 2:
                                c0 = (KSL, KWN)[kk]
                                src = proj2[:, t, c0:c0 + P]
                            else:
                                src = kdup[:, t, 2 * (q - 3) + kk, :, :].rearrange("p e d -> p (e d)")
                            ins = pe.transpose(psa[:, q % 4, kk * S + t * P:kk * S + (t + 1) * P], src, ident[:])
                    ins.then_inc(nsa_turned, 1)
                pe.wait_ge(qm_ready, 2 * (l + 1))
                wh, wl = take((2, "ukv", l, 0))
                for t in range(NT):
                    for half in range(2):
                        for kk in range(2):
                            tok = slice(t * P, (t + 1) * P)
                            col = slice(half * 512, (half + 1) * 512)
                            ins = product(psw[:, 2 * t + half, :], cT_hi[:, 3 + kk, tok], cT_lo[:, 3 + kk, tok],
                                          wh[:, kk, col], wl[:, kk, col], kk == 0, kk == 1)
                ins.then_inc(tile_done, 1)
                pe.wait_ge(qm_roped, l + 1)
                pe.wait_ge(nsa_ready, 5 * (l + 1))
                for b in range(4):
                    for kk in range(2):
                        for t in range(NT):
                            h = 2 * b + kk
                            ins = pe.transpose(psa[0:MD, b, kk * S + t * P:kk * S + (t + 1) * P],
                                               qm[:, t, h * MD:(h + 1) * MD], ident[:])
                    ins.then_inc(mla_turned, 1)
                pe.wait_ge(kvm_ready, l + 1)
                for i in range(2):
                    pe.wait_ge(cmp_x, 2 * l + i + 1)
                    wh, wl = take((2, "w1", l, i))
                    for j in range(16):
                        if j:
                            pe.matmul(psw[:, i, 0:2 * NC], wl[:, j, :], cx_hi[i][:, j, :], start=False, stop=False)
                        ins = pe.matmul(psw[:, i, 0:4 * NC], wh[:, j, :], cx_both[i][:, j, :], start=(j == 0),
                                        stop=(j == 15))
                        if j == 0:
                            pe.matmul(psw[:, i, 0:2 * NC], wl[:, j, :], cx_hi[i][:, j, :], start=False, stop=False)
                    ins.then_inc(tile_done, 1)
                pe.wait_ge(km_roped, l + 1)
                for b in range(4):
                    pe.wait_ge(mla_ready, 8 * l + b + 1)
                    for kk in range(2):
                        for t in range(NT):
                            h = 2 * b + kk
                            ins = pe.transpose(psa[0:MD, b, kk * S + t * P:kk * S + (t + 1) * P],
                                               kvm[:, t, h, DH:KVW], ident[:])
                    ins.then_inc(mla_turned, 1)
                pe.wait_ge(cmp_gelu, 2 * (l + 1))
                for gr in range(2):
                    pe.matmul(psw[64 * gr:64 * gr + 64, 2, 0:NC], w2s[:, l, 0, :],
                              hcmp[:, 0, gr * NC:(gr + 1) * NC], start=True, stop=True)
                for gr in range(2):
                    for i in range(4):
                        ins = pe.matmul(psw[32 * i:32 * i + NC, 3, gr * DH:(gr + 1) * DH],
                                        hcmp[:, 1, gr * NC:(gr + 1) * NC], w2s[:, l, 1, :], start=True, stop=True)
                ins.then_inc(cmp_kv, 1)
                pe.wait_ge(cmp_kv_ready, l + 1)
                for t in range(NT):
                    for r in range(4):
                        for a in range(2):
                            ins = pe.matmul(psw[:, a, t * 64 + r * 16:t * 64 + (r + 1) * 16],
                                            nsaT[64 * a:64 * a + 64, r, t * P:(t + 1) * P],
                                            kct[64 * a:64 * a + 64, :], start=True, stop=True)
                ins.then_inc(cmp_scores, 1)
                pe.wait_ge(cmp_exp, l + 1)
                pe.wait_ge(mla_ready, 8 * (l + 1))
                for t in range(NT):
                    for gr in range(2):
                        ins = pe.transpose(psa[:, 0, (2 * t + gr) * P:(2 * t + gr + 1) * P],
                                           pcmp[:, t, 4 * gr:4 * gr + 4, :].rearrange("p h n -> p (h n)"), ident[:])
                ins.then_inc(cmp_turned, 1)
                pe.wait_ge(cmp_pT, l + 1)
                for t in range(NT):
                    for gr in range(2):
                        ins = pe.matmul(psw[:, 2 + t, gr * S:(gr + 1) * S], pcT[:, 2 * t + gr, :], vbd[:, gr, :],
                                        start=True, stop=True)
                ins.then_inc(cmp_pv, 1)
                kblock = {SLC: 4, WIN: 5}
                vcol = {SLC: VSL, WIN: VWN}
                attention(
                    2, l,
                    lambda kind, h, t: (mqT[0:MD, h, t * P:(t + 1) * P] if kind == MLA else
                                        nsaT[64 * (h // 4):64 * (h // 4) + 64, h % 4, t * P:(t + 1) * P]),
                    lambda kind, h, nk: (mkT[0:MD, h, 0:nk] if kind == MLA else
                                         nsaT[64 * (h // 4):64 * (h // 4) + 64, kblock[kind], 0:nk]),
                    lambda kind, h, kb: (kvm[:, kb, h, 0:DH] if kind == MLA else
                                         proj2[:, kb, vcol[kind] + DH * (h // 4):vcol[kind] + DH * (h // 4) + DH]),
                    lambda: pe.wait_ge(cmp_o, l + 1))
                pe.wait_ge(o_ready, unit0(2, l) + 6)
                turns(omix, psw)
                before_norm(2, "out", l, (2, "mix", l))

                norm_turns((2, "1", l), psa)
                for k in range(4):
                    by_features((2, "xq", l, k), bank2(psw, k), xhi, xlo, (2, "1", l) if k == 0 else None)
                pe.wait_ge(xq_ready, 4 * (l + 1))
                pe.wait_ge(kv_loaded, 48 * (l + 1))
                for t in range(NT):
                    for h in range(4):
                        for kk in range(2):
                            ins = pe.matmul(psw[:, 2 * t + h // 2, (h % 2) * S:(h % 2 + 1) * S],
                                            xqT[:, 2 * h + kk, t * P:(t + 1) * P], xkT[:, 2 * h + kk, :],
                                            start=(kk == 0), stop=(kk == 1))
                    ins.then_inc(xs_done, 1)
                for t in range(NT):
                    pe.wait_ge(xp_ready, NT * l + t + 1)
                    for h in range(4):
                        for m in range(2):
                            ins = pe.transpose(psa[:, h, m * S + t * P:m * S + (t + 1) * P],
                                               xsoft[:, t, h, m * P:(m + 1) * P], ident[:])
                        if t == 1:
                            ins.then_inc(xp_turned, 1)
                for h in range(4):
                    pe.wait_ge(xpT_ready, 4 * l + h + 1)
                    for ch in range(2):
                        for m in range(2):
                            f = 2 * h + ch
                            ins = pe.matmul(psw[:, h, ch * S:(ch + 1) * S], xvt[:, m, f * P:(f + 1) * P],
                                            pt[:, h, m * S:(m + 1) * S], start=(m == 0), stop=(m == 1))
                    ins.then_inc(act_turned, 1)
                before_norm(2, "xo", l, (2, "xa", l))
                norm_turns((2, "2", l), psa)
                ffn(2, l, FS * (L + l), (2, "2", l))
                if l + 1 < L:
                    norm_turns((2, "3", l), psw)

        @block.scalar
        def _(act):
            nxt = [0]

            def split(i):
                act.wait_ge(tile_loaded[i % NL], 16 * (i // NL + 1))
                if i >= NW:
                    act.wait_ge(tile_done, i - NW + 1)
                nc.scalar.activation(tile_flat(whi, NW, i), tile_flat(raw, NL, i), ACT.Copy).then_inc(hi_ready, 1)

            def serve(key):
                while nxt[0] <= min(ti[key] + NW, n_tiles - 1):
                    split(nxt[0])
                    nxt[0] += 1

            def turned_hi(key, ps, hi=xhi):
                for b in range(4):
                    act.wait_ge(act_turned, 4 * turn[key] + b + 1)
                    nc.scalar.activation(hi[:, 2 * b:2 * b + 2, :], bank2(ps, b), ACT.Copy).then_inc(act_hi, 1)

            def p_high(l, bank):
                act.wait_ge(p_turned, l + 1)
                nc.scalar.activation(pT_hi, bank2(psw, bank), ACT.Copy).then_inc(p_hi, 1)

            def memory_store(n, place):
                if n % 2:
                    act.wait_ge(tile_done, ti[(2, "kv", n // 16, n // 2 % 8)] + 1)
                else:
                    act.wait_ge(kv_part, n // 2 + 1)
                if n >= 2:
                    act.wait_ge(kv_stored[n % 2], 16 * (n // 2))
                nc.scalar.activation(place, psa[:, 3, 0:TC], ACT.Copy).then_inc(kv_staged, 1)
                act.wait_ge(kv_staged, n + 1)
                act.dma_start(kv_halves[n], place).then_inc(kv_stored[n % 2], 16)

            def attention(block, l):
                first = 2 * unit0(block, l)
                count = 2 * sum(1 for x in units if x[0] == block and x[1] == l)
                for i in range(first, first + count + 1):
                    if i < first + count:
                        u, hf = divmod(i, 2)
                        kind, t = units[u][2:]
                        nk = (t + 1) * P
                        act.wait_ge(smax_done, i + 1)
                        if kind == SWA:
                            hs = esink[:, u % 2, 1, :].rearrange("p (a q) -> p a q", a=2)[:, :, 2 * hf:2 * hf + 2]
                            nc.scalar.activation(hs, esink[:, u % 2, 0, :].rearrange(
                                "p (a q) -> p a q", a=2)[:, :, 2 * hf:2 * hf + 2], ACT.Exp)
                        for b in range(2):
                            for a in range(2):
                                h = a * 4 + hf * 2 + b
                                ins = nc.scalar.activation(soft[:, u % 2, h, 0:nk], soft[:, u % 2, h, 0:nk], ACT.Exp,
                                                           bias=nmx[:, u % 2, h:h + 1], scale=1.0,
                                                           accum_out=den[:, u % 2, h:h + 1])
                        ins.then_inc(exp_done, 1)
                    half = memory_slot(block, l, i - first)
                    if half is not None:
                        memory_store(half, stage[block - 1][:, half % 2, :])
                    if i - 1 >= first:
                        n = i - 1
                        for m in range(chunk0[n], chunk0[n + 1]):
                            act.wait_ge(pt_done, m + 1)
                            if m >= 4:
                                owner = max(x for x in range(len(chunk0) - 1) if chunk0[x] <= m - 4)
                                act.wait_ge(pv_done, owner + 1)
                            nc.scalar.activation(pt[:, m % 4, :], psa[:, m % 2, :], ACT.Copy).then_inc(pt_ready, 1)
                    if half is not None and half % 2:
                        serve((2, "kv", half // 16, half // 2 % 8))

            p_high(0, 0)
            split(0)
            split(1)
            split(2)
            nxt[0] = 3

            for l in range(L):
                for k4 in range(4):
                    if k4 < 3:
                        act.wait_ge(pp_part, 3 * l + k4 + 1)
                    else:
                        act.wait_ge(tile_done, ti[(1, "pp", l, 0)] + 1)
                    nc.scalar.activation(ple[:, :, k4 * TC:(k4 + 1) * TC], bank2(psw, k4),
                                         ACT.Copy).then_inc(pp_ready, 1)
                turned_hi((1, "in", 0) if l == 0 else (1, "2", l - 1), psa)
                serve((1, "pp", l, 0))
                if l == 0:
                    act.wait_ge(angles_ready, 1)
                    nc.scalar.activation(angs[:, 4:6, :], angs[:, 4:6, :], ACT.Sin).then_inc(sines_ready, 1)

                def heads_out(q):
                    act.wait_ge(heads_turned, 8 * l + q + 1)
                    grp = head_groups[q]
                    nb = len(grp)
                    nc.scalar.activation(headT[:, grp[0]:grp[0] + nb, :],
                                         bank2(psa if q < 2 else psw, q % 4)[:, 0:nb, :], ACT.Copy).then_inc(heads_ready, 1)

                def rectified(t):
                    nk = (t + 1) * P
                    act.wait_ge(iscores_done, NT * l + t + 1)
                    if t == 1:
                        act.wait_ge(icomb_done, NT * l + 1)
                    for j in range(4):
                        ins = nc.scalar.activation(relu[:, j:8:4, 0:nk], bank2(psa, j)[:, :, 0:nk], ACT.Relu)
                    ins.then_inc(relu_done, 1)

                for q, k in enumerate(IN1_ORDER):
                    cols = min(TC, IN1 - k * TC)
                    act.wait_ge(tile_done, ti[(1, "in", l, k)] + 1)
                    nc.scalar.activation(proj1[:, :, k * TC:k * TC + cols], bank2(psw, q % 4)[:, :, 0:cols],
                                         ACT.Copy).then_inc(proj_ready, 1)
                    serve((1, "in", l, k))
                    if l == 0 and q == 2:
                        turned_hi((2, "mem", 0), psa, memhi)
                    if l == 0 and q == 4:
                        act.wait_ge(params_turned, 1)
                        for j, n in enumerate(param_rows):
                            nc.scalar.activation(pcol[:, j, 0:n], psa[:, 2 + j // 4, (j % 4) * P:(j % 4) * P + n],
                                                 ACT.Copy)
                    if q == 4:
                        heads_out(0)
                        heads_out(1)
                    if q >= 5:
                        rectified(q - 5)
                for q in range(2, 8):
                    heads_out(q)
                attention(1, l)
                turned_hi((1, "mix", l), psw)
                for k in range(4):
                    serve((1, "o", l, k))
                turned_hi((1, "1", l), psa)
                for k in range(4):
                    act.wait_ge(tile_done, ti[(1, "pg", l, k)] + 1)
                    if k == 0:
                        act.wait_ge(o_ready, unit0(1, l) + 4)
                    nc.scalar.activation(egate[:, k, :], psw[:, k, :], ACT.Exp, scale=-1.0).then_inc(pg_exp, 1)
                    serve((1, "pg", l, k))
                for s in range(FS + 1):
                    f = FS * l + s
                    if s < FS:
                        serve((1, "g", l, s))
                        if f >= 2:
                            act.wait_ge(hid_ready, f - 1)
                        act.wait_ge(tile_done, ti[(1, "g", l, s)] + 1)
                        nc.scalar.activation(gact[:, f % 2, :], psw[:, 2 * (f % 2), :],
                                             ACT.Silu).then_inc(gate_ready, 1)
                        serve((1, "u", l, s))
                    for j in down_steps(s):
                        if j == FS - 1 and l + 1 < L:
                            p_high(l + 1, 2 * ((l + 1) * FS % 2))
                        serve((1, "d", l, j))

            for stored_half in kv_stored:
                act.wait_ge(stored_half, 16 * 8)
            for l in range(L):
                turned_hi((2, "in", 0) if l == 0 else (2, "3", l - 1), psw)
                for k in range(8):
                    cols = min(TC, IN2 - k * TC)
                    act.wait_ge(tile_done, ti[(2, "in", l, k)] + 1)
                    nc.scalar.activation(proj2[:, :, k * TC:k * TC + cols], bank2(psw, k % 4)[:, :, 0:cols],
                                         ACT.Copy).then_inc(proj2_ready, 1)
                    serve((2, "in", l, k))
                    if k != 5:
                        continue
                    for b in range(3):
                        act.wait_ge(c_turned, 3 * l + b + 1)
                        for kk in range(2 if b < 2 else 1):
                            k = 2 * b + kk
                            row = cqg_row(l) + k if k < 3 else ckvg_row(l) + k - 3
                            ins = nc.scalar.activation(ctmp[:, k, :], psa[:, b, kk * S:(kk + 1) * S], ACT.Copy,
                                                       scale=pcol[:, 0, row:row + 1])
                        ins.then_inc(c_v, 1)
                act.wait_ge(proj2_ready, 8 * (l + 1))
                nc.scalar.activation(gates[:], proj2[:, :, GL:IN2], ACT.Exp, scale=-1.0).then_inc(gate_exp, 1)
                for j in range(2):
                    act.wait_ge(tile_done, ti[(2, "uq", l, j)] + 1)
                    nc.scalar.activation(qm[:, :, j * 384:(j + 1) * 384], psw[:, 2 * j:2 * j + 2, 0:384],
                                         ACT.Copy).then_inc(qm_ready, 1)
                    serve((2, "uq", l, j))
                for q in range(5):
                    act.wait_ge(nsa_turned, 5 * l + q + 1)
                    if q < 3:
                        nc.scalar.activation(nsaT[:, 2 * q:2 * q + 2, :], bank2(psa, q), ACT.Copy).then_inc(nsa_ready, 1)
                    else:
                        i = 2 * (q - 3)
                        nc.scalar.activation(cx[0:64, i:i + 2, :], bank2(psa, q % 4)[0:64], ACT.Copy)
                        nc.scalar.activation(cx[64:128, i:i + 2, 0:S - 1], bank2(psa, q % 4)[64:128, :, 1:S],
                                             ACT.Copy).then_inc(nsa_ready, 1)
                act.wait_ge(tile_done, ti[(2, "ukv", l, 0)] + 1)
                for t in range(NT):
                    kv = psw[:, 2 * t:2 * t + 2, :].rearrange("p b (h c) -> p (b h) c", h=4)
                    nc.scalar.activation(kvm[:, t, :, 0:DH], kv[:, :, DH:P], ACT.Copy)
                    ins = nc.scalar.activation(kvm[:, t, :, DH:P], kv[:, :, 0:DH], ACT.Copy)
                ins.then_inc(kvm_ready, 1)
                serve((2, "ukv", l, 0))
                for b in range(4):
                    act.wait_ge(mla_turned, 8 * l + b + 1)
                    nc.scalar.activation(mqT[0:MD, 2 * b:2 * b + 2, :], bank2(psa, b)[0:MD], ACT.Copy).then_inc(mla_ready, 1)
                for i in range(2):
                    act.wait_ge(cmp_added, 2 * l + i + 1)
                    row = b1_row(l, i)
                    nc.scalar.activation(hcmp[:, i, :], hcmp[:, i, :], ACT.Gelu_apprx_tanh,
                                         bias=pcol[:, 0, row:row + 1]).then_inc(cmp_gelu, 1)
                    serve((2, "w1", l, i))
                for b in range(4):
                    act.wait_ge(mla_turned, 8 * l + b + 5)
                    nc.scalar.activation(mkT[0:MD, 2 * b:2 * b + 2, :], bank2(psa, b)[0:MD], ACT.Copy).then_inc(mla_ready, 1)
                act.wait_ge(cmp_shifted, l + 1)
                nc.scalar.activation(pcmp[:, :, :, 0:16].rearrange("p t h n -> p (t h) n"),
                                     scmp.rearrange("p t (h n) -> p (t h) n", h=H), ACT.Exp).then_inc(cmp_exp, 1)
                act.wait_ge(cmp_turned, l + 1)
                nc.scalar.activation(pcT, psa[:, 0, :].rearrange("p (j q) -> p j q", j=4), ACT.Copy).then_inc(cmp_pT, 1)
                attention(2, l)
                turned_hi((2, "mix", l), psw)
                for k in range(4):
                    serve((2, "out", l, k))

                turned_hi((2, "1", l), psa)
                for k in range(4):
                    act.wait_ge(tile_done, ti[(2, "xq", l, k)] + 1)
                    nc.scalar.activation(xqT[:, 2 * k:2 * k + 2, :], bank2(psw, k), ACT.Copy).then_inc(xq_ready, 1)
                    serve((2, "xq", l, k))
                for t in range(NT):
                    act.wait_ge(xmax_done, NT * l + t + 1)
                    for h in range(4):
                        ins = nc.scalar.activation(xsoft[:, t, h, :], psw[:, 2 * t + h // 2, (h % 2) * S:(h % 2 + 1) * S],
                                                   ACT.Exp, bias=xmx[:, t, h:h + 1], scale=1 / 16,
                                                   accum_out=xden[:, t, h:h + 1])
                    ins.then_inc(xexp_done, 1)
                for h in range(4):
                    act.wait_ge(xp_turned, 4 * l + h + 1)
                    nc.scalar.activation(pt[:, h, :], psa[:, h, :], ACT.Copy).then_inc(xpT_ready, 1)
                turned_hi((2, "xa", l), psw)
                for k in range(4):
                    serve((2, "xo", l, k))
                turned_hi((2, "2", l), psa)
                for s in range(FS + 1):
                    f = FS * (L + l) + s
                    if s < FS:
                        for name, buf, bank, ch0 in (("g", conv_g, 2 * (f % 2), 22 + 2 * s),
                                                     ("u", conv_a, 2 * (f % 2) + 1, 2 * s)):
                            act.wait_ge(tile_done, ti[(2, name, l, s)] + 1)
                            if f >= 2:
                                act.wait_ge(hid_ready, f - 1)
                            for ch in range(2):
                                cc = ch0 + ch
                                ins = nc.scalar.activation(buf[:, f % 2, ch, :], bank2(psw, bank)[:, ch, :],
                                                           ACT.Identity, scale=pcol[:, 2 + 2 * l, cc:cc + 1],
                                                           bias=pcol[:, 2 + 2 * l, 44 + cc:45 + cc])
                            ins.then_inc(conv_first, 1)
                            serve((2, name, l, s))
                        act.wait_ge(conv_done, FS * l + s + 1)
                        nc.scalar.activation(gact[:, f % 2, :], conv_g[:, f % 2].rearrange("p c s -> p (c s)"),
                                             ACT.Silu).then_inc(gate_ready, 1)
                    for j in down_steps(s):
                        serve((2, "d", l, j))
            for t in range(NT):
                act.wait_ge(x_ready, XR * (len(norms) - 1) + 2 * (t + 1))
                act.dma_start(out[0, t * P:(t + 1) * P, :], xtok[:, t, :]).then_inc(stored, 16)
            act.wait_ge(stored, 16 * NT)

        @block.vector
        def _(dve):
            nxt = [0]
            v = nc.vector

            def split(i):
                dve.wait_ge(hi_ready, i + 1)
                v.tensor_tensor(tile_flat(wlo, NL, i), tile_flat(raw, NL, i),
                                tile_flat(whi, NW, i).bitcast(F32), ALU.subtract).then_inc(lo_ready, 1)

            def serve(key):
                while nxt[0] <= min(ti[key] + NW, n_tiles - 1):
                    if nxt[0] not in pool_tiles:
                        split(nxt[0])
                    nxt[0] += 1

            scaled = [0]

            def norm(key, x, chunks, before=lambda t: None, token_tiles=range(NT)):
                nm = norms[key]
                for t in token_tiles:
                    before(t)
                    dve.drain()
                    v.bn_aggr(meanvar[:, t, :], stats[:, t, 0:chunks, :])
                    dve.drain()
                    v.tensor_scalar(vare[:, t:t + 1], meanvar[:, t, 1:2], LN_EPS, None, ALU.add).then_inc(ln_var, 1)
                    if t == 0 and "loads" in nm:
                        dve.wait_ge(gb_loaded, 32 * nm["loads"])
                    v.scalar_tensor_tensor(out=x[:, t, :], in0=x[:, t, :], scalar=meanvar[:, t, 0:1],
                                           in1=nm["place"][:, 0, :], op0=ALU.subtract, op1=ALU.mult)
                    scaled[0] += 1
                    dve.wait_ge(ln_rstd, scaled[0])
                    dve.drain()
                    for half in range(2):
                        h = slice(half * 512, (half + 1) * 512)
                        v.scalar_tensor_tensor(out=x[:, t, h], in0=x[:, t, h], scalar=rstd[:, t:t + 1],
                                               in1=nm["place"][:, 1, h], op0=ALU.mult, op1=ALU.add).then_inc(x_ready, 1)

            def half_stats(x, t):
                for half in range(2):
                    v.bn_stats(stats[:, t, half, :], x[:, t, half * 512:(half + 1) * 512])

            def turned_lo(key, ps, hi=xhi, lo=xlo):
                for b in range(4):
                    dve.wait_ge(act_hi, 4 * turn[key] + b + 1)
                    ks = slice(2 * b, 2 * b + 2)
                    v.tensor_tensor(lo[:, ks, :], bank2(ps, b), hi[:, ks, :].bitcast(F32),
                                    ALU.subtract).then_inc(act_ready, 1)

            def p_low(l, bank):
                dve.wait_ge(p_hi, l + 1)
                v.tensor_tensor(pT_lo, bank2(psw, bank), pT_hi.bitcast(F32), ALU.subtract).then_inc(p_ready, 1)

            def rope(x, cos, sin, t1, t2, writes):
                nh, wd = x.shape[1], x.shape[2]
                hw = wd // 2
                v.tensor_tensor(t1, x, bc(cos, nh), ALU.mult)
                v.tensor_tensor(t2[:, :, 0:hw], x[:, :, hw:wd], bc(sin[:, 0:hw], nh), ALU.mult)
                v.tensor_tensor(t2[:, :, hw:wd], x[:, :, 0:hw], bc(sin[:, hw:wd], nh), ALU.mult)
                dve.drain()
                for o, sel in writes:
                    ins = v.tensor_tensor(o, sel(t1), sel(t2), ALU.add)
                return ins

            def attention(block, l, mask, scale, finish, between=lambda step: None):
                first = 2 * unit0(block, l)
                count = 2 * sum(1 for x in units if x[0] == block and x[1] == l)
                for i in range(first, first + count + 2):
                    if i < first + count:
                        u, hf = divmod(i, 2)
                        kind, t = units[u][2:]
                        nk = (t + 1) * P
                        dve.wait_ge(scores_done, i + 1)
                        if u >= 2:
                            dve.wait_ge(pt_done, chunk0[2 * (u - 1)])
                        for b in range(2):
                            for a in range(2):
                                h = a * 4 + hf * 2 + b
                                v.tensor_tensor_reduce(
                                    out=soft[:, u % 2, h, 0:nk], in0=psw[:, 2 * (i % 2) + a, b * S:b * S + nk],
                                    in1=mask(kind, h, t), scale=scale[kind], scalar=LOWEST, op0=ALU.add, op1=ALU.max,
                                    accum_out=mx[:, u % 2, h:h + 1])
                        dve.drain()

                        def hs(x):
                            return x.rearrange("p (a q) -> p a q", a=2)[:, :, 2 * hf:2 * hf + 2]
                        m, nm = hs(mx[:, u % 2, :]), hs(nmx[:, u % 2, :])
                        if kind == SWA:
                            v.tensor_tensor(m, m, hs(sinkb[:, l, :]), ALU.max)
                            dve.drain()
                            v.tensor_tensor(hs(esink[:, u % 2, 0, :]), hs(sinkb[:, l, :]), m, ALU.subtract)
                        v.tensor_scalar(nm, m, -1.0, None, ALU.mult).then_inc(smax_done, 1)
                        between(i - first)
                    if i - 2 >= first and (i - 2) % 2 == 1:
                        u = (i - 2) // 2
                        dve.wait_ge(pv_done, 2 * u + 2)
                        finish(u, units[u][2], units[u][3])

            def residual_norm(keys, norm_key):
                def piece(k, ts, ps):
                    cols = slice(k * TC, (k + 1) * TC)
                    ins = v.scalar_tensor_tensor(out=xtok[:, ts, cols], in0=xtok[:, ts, cols], scalar=ALPHA,
                                                 in1=ps, op0=ALU.mult, op1=ALU.add)
                    if k < 2:
                        ins.then_inc(joined, 1)
                    dve.drain()
                    for t in range(ts.start, ts.stop):
                        v.bn_stats(stats[:, t, k, :], xtok[:, t, cols])
                for k in range(2):
                    dve.wait_ge(tile_done, ti[keys[k]] + 1)
                    piece(k, slice(0, NT), bank2(psw, k))
                    serve(keys[k])

                def last(t):
                    for k in (2, 3):
                        if t == 0:
                            dve.wait_ge(part_done, part[keys[3]])
                        else:
                            dve.wait_ge(tile_done, ti[keys[k]] + 1)
                        piece(k, slice(t, t + 1), residual_banks(k)[t].unsqueeze(1))
                norm(norm_key, xtok, 4, last)

            def ffn_norm(block, l, norm_key, join, next_key=None):
                key = (block, "d", l, FS - 1)

                def last(t):
                    if t == 0:
                        dve.wait_ge(part_done, part[key])
                    else:
                        dve.wait_ge(tile_done, ti[key] + 1)
                    for half in range(2):
                        join(t, slice(half * 512, (half + 1) * 512), psa[:, 2 * t + half, :])
                    dve.drain()
                    half_stats(xtok, t)
                for t in range(NT):
                    norm(norm_key, xtok, 2, last, [t])
                    if next_key is not None:
                        norm(next_key, xtok, 2, lambda t: (dve.drain(), half_stats(xtok, t)), [t])

            v.memset(mhalf[:], -0.5).then_inc(mhalf_ready, 1)
            v.memset(kct[:], 0.0)
            v.memset(vbd[:], 0.0)
            p_low(0, 0)
            split(0)
            dve.wait_ge(x_loaded, 16 * NT)
            norm((1, "in", 0), xtok, 2, lambda t: half_stats(xtok, t))

            def angles():
                dve.wait_ge(angles_loaded, 16 * len(angle_dmas))
                v.tensor_copy(pos_f[:], pos_i[:])
                dve.drain()
                for t in range(NT):
                    v.tensor_scalar(angs[:, 0, t * 32:(t + 1) * 32], inv[:], pos_f[:, t:t + 1], None, ALU.mult)
                dve.drain()
                whole = float(np.float32(1 / (2 * math.pi)))
                magic = 1.5 * 2.0 ** 23
                c1 = 6.28125
                c2 = float(np.float32(np.round((2 * math.pi - c1) * 2 ** 20) / 2 ** 20))
                c3 = float(np.float32(2 * math.pi - c1 - c2))
                v.tensor_scalar(angs[:, 1, :], angs[:, 0, :], whole, magic, ALU.mult, ALU.add)
                v.tensor_scalar(angs[:, 2, :], angs[:, 0, :], whole, 0.25, ALU.mult, ALU.add)
                dve.drain()
                v.tensor_scalar(angs[:, 2, :], angs[:, 2, :], magic, -magic, ALU.add, ALU.add)
                v.tensor_scalar(angs[:, 1, :], angs[:, 1, :], -magic, None, ALU.add)
                dve.drain()
                for j in range(2):
                    src = angs[:, 0, :]
                    for cc in (c1, c2, c3):
                        v.scalar_tensor_tensor(out=angs[:, 4 + j, :], in0=angs[:, 1 + j, :], scalar=-cc, in1=src,
                                               op0=ALU.mult, op1=ALU.add)
                        src = angs[:, 4 + j, :]
                        dve.drain()
                v.tensor_scalar(angs[:, 5, :], angs[:, 5, :], math.pi / 2, None, ALU.add)
                dve.drain()
                v.tensor_scalar(angs[:, 4:6, :], angs[:, 4:6, :], 3.1415925, -3.1415925, ALU.min,
                                ALU.max).then_inc(angles_ready, 1)

            def tables():
                dve.wait_ge(sines_ready, 1)
                sn = angs[:, 4, :].rearrange("p (t c) -> p t c", t=NT)
                cs = angs[:, 5, :].rearrange("p (t c) -> p t c", t=NT)
                for half in range(2):
                    v.tensor_copy(cos64[:, :, 32 * half:32 * half + 32], cs)
                    v.tensor_copy(cos32[:, :, 16 * half:16 * half + 16], cs[:, :, 0:32:2])
                    v.tensor_scalar(sin64[:, :, 32 * half:32 * half + 32], sn, 2.0 * half - 1, None, ALU.mult)
                    ins = v.tensor_scalar(sin32[:, :, 16 * half:16 * half + 16], sn[:, :, 0:32:2], 2.0 * half - 1, None,
                                          ALU.mult)
                ins.then_inc(tables_ready, 1)

            for l in range(L):
                turned_lo((1, "in", 0) if l == 0 else (1, "2", l - 1), psa)
                if l == 0:
                    split(2)
                    nxt[0] = 3
                    angles()
                serve((1, "pp", l, 0))

                def index_sum(t):
                    nk = (t + 1) * P
                    dve.wait_ge(relu_done, NT * l + t + 1)
                    sc = iscore[:, t, 0:nk]
                    cm = causal[:, S - nk:S]
                    for h in range(H):
                        ins = v.scalar_tensor_tensor(out=sc, in0=relu[:, h, 0:nk], scalar=wi_s[:, t, h:h + 1],
                                                     in1=cm if h == 0 else sc, op0=ALU.mult, op1=ALU.add)
                        if h < H - 1:
                            dve.drain()
                    ins.then_inc(icomb_done, 1)

                t1 = sy[:, 0, 0:640]
                t2 = sy[:, 0, 640:1280]
                for q, k in enumerate(IN1_ORDER):
                    if q < 6:
                        serve((1, "in", l, k))
                    if l == 0 and q == 0:
                        tables()
                        dve.wait_ge(mem_loaded, 16 * (NT + 2))
                        norm((2, "mem", 0), memory, 2, lambda t: half_stats(memory, t))
                        dve.wait_ge(consts_loaded, 16 * n_const_dmas)
                        dve.drain()
                    if q == 1:
                        dve.wait_ge(proj_ready, 7 * l + 2)
                        for t in range(NT):
                            v.bn_stats(stats[:, t, 0, :], proj1[:, t, KI:KI + 32])
                        dve.drain()
                        for t in range(NT):
                            v.bn_aggr(meanvar[:, t, :], stats[:, t, 0:1, :])
                        dve.drain()
                        v.tensor_scalar(vare[:, 0:NT], meanvar[:, :, 1], LN_EPS, None, ALU.add).then_inc(ki_var, 1)
                        v.tensor_scalar(wi_s[:], proj1[:, :, WI:WI + H], 8 ** -0.5 * 32 ** -0.5, None, ALU.mult)
                        dve.wait_ge(ki_rstd, l + 1)
                        ki = proj1[:, :, KI:KI + 32]
                        for t in range(NT):
                            v.tensor_scalar(ki[:, t, :], ki[:, t, :], meanvar[:, t, 0:1], rstd[:, t:t + 1],
                                            ALU.subtract, ALU.mult)
                        dve.drain()
                        v.tensor_tensor(ki, ki, bc(ikg[:, l, 0, :], NT), ALU.mult)
                        dve.drain()
                        v.tensor_tensor(ki, ki, bc(ikg[:, l, 1, :], NT), ALU.add)
                        dve.drain()
                    if q == 2:
                        for t in range(NT):
                            x = proj1[:, t, QI:QI + 288].rearrange("p (h d) -> p h d", h=9)
                            a = t1[:, 0:288].rearrange("p (h d) -> p h d", h=9)
                            b = t2[:, 0:288].rearrange("p (h d) -> p h d", h=9)
                            rope(x, cos32[:, t, :], sin32[:, t, :], a, b, [
                                (roped[:, t, 10 * P:12 * P].rearrange("p (h d) -> p h d", h=8), lambda z: z[:, 0:8, :]),
                                (roped[:, t, 12 * P:13 * P].rearrange("p (h d) -> p h d", h=4),
                                 lambda z: z[:, 8:9, :].broadcast_to([P, 4, 32]))]).then_inc(qki_roped, 1)
                            dve.drain()
                    if l == 0 and q == 2:
                        turned_lo((2, "mem", 0), psa, memhi, memlo)
                    if q == 5:
                        index_sum(0)
                    if q == 4:
                        dve.wait_ge(proj_ready, 7 * l + 4)
                        for t in range(NT):
                            x = proj1[:, t, QB:QB + 576].rearrange("p (h d) -> p h d", h=9)
                            a = t1[:, 0:576].rearrange("p (h d) -> p h d", h=9)
                            b = t2[:, 0:576].rearrange("p (h d) -> p h d", h=9)
                            rope(x, cos64[:, t, :], sin64[:, t, :], a, b, [
                                (roped[:, t, 5 * P:9 * P].rearrange("p (r a d) -> p a r d", a=2, d=DH),
                                 lambda z: z[:, 0:8, :].rearrange("p (a r) d -> p a r d", a=2)),
                                (roped[:, t, 9 * P:10 * P].rearrange("p (h d) -> p h d", h=2),
                                 lambda z: z[:, 8:9, :].broadcast_to([P, 2, DH]))]).then_inc(qkb_roped, 1)
                            dve.drain()
                dve.wait_ge(proj_ready, 7 * (l + 1))
                dve.drain()
                rope(proj1[:, 1, QA:QA + 640].rearrange("p (h d) -> p h d", h=10), cos64[:, 1, :], sin64[:, 1, :],
                     t1.rearrange("p (h d) -> p h d", h=10), t2.rearrange("p (h d) -> p h d", h=10), [
                         (roped[:, 1, 0:4 * P].rearrange("p (r a d) -> p a r d", a=2, d=DH),
                          lambda z: z[:, 0:8, :].rearrange("p (a r) d -> p a r d", a=2)),
                         (roped[:, 1, 4 * P:5 * P].rearrange("p (h d) -> p h d", h=2),
                          lambda z: z[:, 8:10, :])]).then_inc(qka_roped[1], 1)
                serve((1, "in", l, IN1_ORDER[6]))
                index_sum(1)
                dve.drain()

                def top(step):
                    if step >= 4:
                        return
                    t, part_ = divmod(step, 2)
                    nk = (t + 1) * P
                    sc = iscore[:, t, 0:nk]
                    for _ in range(TOPK // 16):
                        v.max(out=top8[:], in_=sc)
                        dve.drain()
                        v.match_replace(out=sc, in_to_replace=top8[:], in_values=sc, imm_value=TAKEN)
                        dve.drain()
                    if part_:
                        v.tensor_scalar(dmask[:, t, 0:nk], sc, TAKEN / 2, MASKED, ALU.is_gt, ALU.mult)
                        dve.drain()
                        v.tensor_tensor(dmask[:, t, 0:nk], dmask[:, t, 0:nk], causal[:, S - nk:S], ALU.add)
                        dve.drain()

                def mask(kind, h, t):
                    nk = (t + 1) * P
                    return band[:, S - nk:S] if kind == SWA else dmask[:, t, 0:nk]

                def finish(u, kind, t):
                    if kind == SWA:
                        v.tensor_tensor(den[:, u % 2, :], den[:, u % 2, :], esink[:, u % 2, 1, :], ALU.add)
                        dve.drain()
                    v.reciprocal(rden[:, u % 2, :], den[:, u % 2, :])
                    dve.drain()
                    c0 = 0 if kind == SWA else H * DH
                    v.tensor_tensor(omix[:, t, c0:c0 + H * DH].rearrange("p (h d) -> p h d", h=H),
                                    psa[:, 2, :].rearrange("p (h d) -> p h d", h=H),
                                    bci(rden[:, u % 2, :], DH), ALU.mult).then_inc(o_ready, 1)
                sc = DH ** -0.5
                attention(1, l, mask, {SWA: sc, DSA: sc}, finish, top)
                turned_lo((1, "mix", l), psw)
                residual_norm([(1, "o", l, k) for k in range(4)], (1, "1", l))
                turned_lo((1, "1", l), psa)
                serve((1, "o", l, 3))
                for k in range(4):
                    dve.wait_ge(pg_exp, 4 * l + k + 1)
                    e = egate[:, k, :]
                    v.tensor_scalar(e, e, 1.0, None, ALU.add)
                    dve.drain()
                    v.reciprocal(e, e)
                    dve.drain()
                    cols = slice(k * TC, (k + 1) * TC)
                    e2 = e.rearrange("p (t c) -> p t c", t=NT)
                    v.tensor_tensor(ple[:, :, cols], ple[:, :, cols], e2, ALU.mult)
                    serve((1, "pg", l, k))
                for s in range(FS + 1):
                    f = FS * l + s
                    if s < FS:
                        serve((1, "g", l, s))
                        serve((1, "u", l, s))
                        dve.wait_ge(gate_ready, f + 1)
                        dve.wait_ge(tile_done, ti[(1, "u", l, s)] + 1)
                        dve.drain()
                        v.tensor_tensor(hidf, gact[:, f % 2, :], psw[:, 2 * (f % 2) + 1, :], ALU.mult)
                        dve.drain()
                        hh = hidh[:, f % 2, :, :].rearrange("p c s -> p (c s)")
                        hl = hidl[:, f % 2, :, :].rearrange("p c s -> p (c s)")
                        if s >= 2:
                            dve.wait_ge(tile_done, ti[(1, "d", l, s - 2)] + 1)
                        v.tensor_copy(hh, hidf)
                        dve.drain()
                        v.tensor_tensor(hl, hidf, hh.bitcast(F32), ALU.subtract).then_inc(hid_ready, 1)
                    for j in down_steps(s):
                        if j < FS - 1:
                            serve((1, "d", l, j))
                        elif l + 1 < L:
                            p_low(l + 1, 2 * ((l + 1) * FS % 2))
                    if s == 2:
                        for t in range(NT):
                            v.scalar_tensor_tensor(out=xtok[:, t, :], in0=xtok[:, t, :], scalar=ALPHA,
                                                   in1=ple[:, t, :], op0=ALU.mult, op1=ALU.add)

                def join(t, cols, ps):
                    v.tensor_tensor(xtok[:, t, cols], xtok[:, t, cols], ps, ALU.add)
                ffn_norm(1, l, (1, "2", l), join, (2, "in", 0) if l == L - 1 else None)

            serve((1, "d", L - 1, FS - 1))
            for l in range(L):
                turned_lo((2, "in", 0) if l == 0 else (2, "3", l - 1), psw)
                for k in range(8):
                    serve((2, "in", l, k))
                    if k == 2:
                        dve.wait_ge(proj2_ready, 8 * l + 3)
                        for j, (c0, n) in enumerate(((CQ, QR), (CKV, KVR))):
                            for t in range(NT):
                                src = proj2[:, t, c0:c0 + n]
                                v.tensor_tensor_reduce(out=mtmp[:, :, :].rearrange("p i c -> p (i c)")[:, 0:n], in0=src,
                                                       in1=src, scale=1.0 / n, scalar=RMS_EPS, op0=ALU.mult,
                                                       op1=ALU.add, accum_out=varc[:, 2 * j + t:2 * j + t + 1])
                                dve.drain()
                        v.tensor_scalar(varc[:], varc[:], 1.0, None, ALU.mult).then_inc(c_var, 1)
                        dve.wait_ge(c_rstd, l + 1)
                        for j, (c0, n) in enumerate(((CQ, QR), (CKV, KVR))):
                            for t in range(NT):
                                src = proj2[:, t, c0:c0 + n]
                                ins = v.tensor_scalar(src, src, rstdc[:, 2 * j + t:2 * j + t + 1], None, ALU.mult)
                        ins.then_inc(c_normed, 1)
                        kx = proj2[:, :, KR:KR + 32]
                        tm = [mtmp[:, i, 0:32].rearrange("p (t c) -> p t c", t=NT) for i in range(4)]
                        v.tensor_tensor(tm[0], kx[:, :, 0:16], mcos[:], ALU.mult)
                        v.tensor_tensor(tm[1], kx[:, :, 16:32], msin[:], ALU.mult)
                        v.tensor_tensor(tm[2], kx[:, :, 0:16], msin[:], ALU.mult)
                        v.tensor_tensor(tm[3], kx[:, :, 16:32], mcos[:], ALU.mult)
                        dve.drain()
                        v.tensor_tensor(krope[:, :, 0:16], tm[0], tm[1], ALU.subtract)
                        v.tensor_tensor(krope[:, :, 16:32], tm[2], tm[3], ALU.add)
                    if k != 5:
                        continue
                    for b in range(3):
                        dve.wait_ge(c_v, 3 * l + b + 1)
                        ks = slice(2 * b, min(2 * b + 2, 5))
                        v.tensor_copy(cT_hi[:, ks, :], ctmp[:, ks, :])
                        dve.drain()
                        v.tensor_tensor(cT_lo[:, ks, :], ctmp[:, ks, :], cT_hi[:, ks, :].bitcast(F32),
                                        ALU.subtract).then_inc(cT_ready, 1)
                for j in range(2):
                    serve((2, "uq", l, j))
                dve.wait_ge(qm_ready, 2 * (l + 1))
                qh = qm.rearrange("p t (h c) -> p t h c", h=H)
                cb = mcos[:].unsqueeze(2).broadcast_to([P, NT, H, 16])
                sb_ = msin[:].unsqueeze(2).broadcast_to([P, NT, H, 16])
                tm = [mtmp[:, i, :].rearrange("p (t h c) -> p t h c", t=NT, h=H) for i in range(4)]
                q1, q2 = qh[:, :, :, DH:DH + 16], qh[:, :, :, DH + 16:MD]
                dve.drain()
                v.tensor_tensor(tm[0], q1, cb, ALU.mult)
                v.tensor_tensor(tm[1], q2, sb_, ALU.mult)
                v.tensor_tensor(tm[2], q1, sb_, ALU.mult)
                v.tensor_tensor(tm[3], q2, cb, ALU.mult)
                dve.drain()
                v.tensor_tensor(q1, tm[0], tm[1], ALU.subtract)
                v.tensor_tensor(q2, tm[2], tm[3], ALU.add).then_inc(qm_roped, 1)
                dve.wait_ge(gate_exp, l + 1)
                v.tensor_scalar(gates[:], gates[:], 1.0, None, ALU.add)
                dve.drain()
                v.reciprocal(gates[:], gates[:])
                dve.wait_ge(tile_done, ti[(2, "ukv", l, 0)] + 1)
                for i in range(2):
                    dve.wait_ge(nsa_ready, 5 * l + 4 + i)
                    dve.drain()
                    for gr in range(2):
                        for jh in range(2):
                            src = cx[:, 2 * i + gr, :].rearrange("p (n r) -> p r n", r=16)[:, 0:16:2, jh:jh + NC]
                            row = pe_row(l, i) + 8 * jh
                            v.tensor_tensor(cf[:, 8 * jh:8 * jh + 8, gr, :], src,
                                            pcol[:, 0, row:row + 8].unsqueeze(2).broadcast_to([P, 8, NC]), ALU.add)
                    dve.drain()
                    cff = cf.rearrange("p j g n -> p j (g n)")
                    v.tensor_copy(cx_hi[i], cff)
                    dve.drain()
                    v.tensor_tensor(cx_lo[i], cff, cx_hi[i].bitcast(F32), ALU.subtract).then_inc(cmp_x, 1)
                dve.wait_ge(kvm_ready, l + 1)
                v.tensor_copy(kvm[:, :, :, P:KVW],
                              krope[:].unsqueeze(2).broadcast_to([P, NT, H, 32])).then_inc(km_roped, 1)
                serve((2, "ukv", l, 0))
                for i in range(2):
                    dve.wait_ge(tile_done, ti[(2, "w1", l, i)] + 1)
                    v.tensor_copy(hcmp[:, i, :], psw[:, i, 0:2 * NC])
                    dve.drain()
                    v.tensor_tensor(hcmp[:, i, :], hcmp[:, i, :], psw[:, i, 2 * NC:4 * NC],
                                    ALU.add).then_inc(cmp_added, 1)
                    if i == 0:
                        serve((2, "w1", l, 0))
                dve.drain()
                v.memset(pcmp, 0.0)
                dve.wait_ge(cmp_kv, l + 1)
                dve.drain()
                v.tensor_copy(kct[:, 0:NC], psw[:, 2, 0:NC])
                for i in range(4):
                    ins = v.tensor_copy(vbd[32 * i:32 * i + NC, :, i * DH:(i + 1) * DH],
                                        psw[32 * i:32 * i + NC, 3, 0:2 * DH].rearrange("p (g d) -> p g d", g=2))
                ins.then_inc(cmp_kv_ready, 1)
                dve.wait_ge(cmp_scores, l + 1)
                for a in range(2):
                    v.scalar_tensor_tensor(out=scmp[:, :, a * 64:(a + 1) * 64],
                                           in0=psw[:, a, 0:128].rearrange("p (t c) -> p t c", t=NT), scalar=DH ** -0.5,
                                           in1=cmpbias[:, :, a * 64:(a + 1) * 64], op0=ALU.mult, op1=ALU.add)
                dve.drain()
                s3 = scmp.rearrange("p t (h n) -> p (t h) n", h=H)
                v.tensor_reduce(cmx[:], s3, AX.X, ALU.max)
                dve.drain()
                v.tensor_tensor(s3, s3, bci(cmx[:], 16), ALU.subtract).then_inc(cmp_shifted, 1)
                serve((2, "w1", l, 1))
                dve.wait_ge(cmp_exp, l + 1)
                v.tensor_reduce(cden[:], pcmp[:, :, :, 0:16].rearrange("p t h n -> p (t h) n"), AX.X, ALU.add)
                dve.drain()
                v.reciprocal(cden[:], cden[:])
                dve.drain()
                g4 = gates[:].rearrange("p t (h b) -> p b t h", b=3)
                cf3 = coef[:].rearrange("p (t h) -> p t h", t=NT)
                v.tensor_tensor(cf3, cden[:].rearrange("p (t h) -> p t h", t=NT), g4[:, 0], ALU.mult)
                dve.drain()
                v.tensor_tensor(cf3, cf3, bci(valid[:], H), ALU.mult)
                dve.drain()
                dve.wait_ge(cmp_pv, l + 1)
                for t in range(NT):
                    ins = v.tensor_tensor(omix[:, t, 512:1024].rearrange("p (h d) -> p h d", h=H),
                                          psw[:, 2 + t, :].rearrange("p (h d) -> p h d", h=H),
                                          bci(coef[:, t * H:(t + 1) * H], DH), ALU.mult)
                ins.then_inc(cmp_o, 1)
                if l == 0:
                    dve.wait_ge(alibi_loaded, 16)

                def mask2(kind, h, t):
                    nk = (t + 1) * P
                    return causal[:, S - nk:S] if kind == MLA else alibi[:, h, S - nk:S]

                def finish2(u, kind, t):
                    rd = rden[:, u % 2, :]
                    v.reciprocal(rd, den[:, u % 2, :])
                    dve.drain()
                    ps = psa[:, 2, :].rearrange("p (h d) -> p h d", h=H)
                    if kind == MLA:
                        v.tensor_tensor(omix[:, t, 0:512].rearrange("p (h d) -> p h d", h=H), ps, bci(rd, DH),
                                        ALU.mult).then_inc(o_ready, 1)
                        return
                    v.tensor_tensor(rd, rd, g4[:, 1 if kind == SLC else 2, t, :], ALU.mult)
                    dve.drain()
                    v.tensor_tensor(otmp[:].rearrange("p (h d) -> p h d", h=H), ps, bci(rd, DH), ALU.mult)
                    dve.drain()
                    v.tensor_tensor(omix[:, t, 512:1024], omix[:, t, 512:1024], otmp[:], ALU.add).then_inc(o_ready, 1)
                attention(2, l, mask2, {SLC: DH ** -0.5, WIN: DH ** -0.5, MLA: MD ** -0.5}, finish2)
                turned_lo((2, "mix", l), psw)
                residual_norm([(2, "out", l, k) for k in range(4)], (2, "1", l))
                turned_lo((2, "1", l), psa)
                serve((2, "out", l, 3))
                for k in range(4):
                    serve((2, "xq", l, k))
                for t in range(NT):
                    dve.wait_ge(xs_done, NT * l + t + 1)
                    v.tensor_reduce(xmx[:, t, :], psw[:, 2 * t:2 * t + 2, :].rearrange("p b (h k) -> p (b h) k", h=2),
                                    AX.X, ALU.max)
                    dve.drain()
                    v.tensor_scalar(xmx[:, t, :], xmx[:, t, :], -1 / 16, None, ALU.mult).then_inc(xmax_done, 1)
                for t in range(NT):
                    dve.wait_ge(xexp_done, NT * l + t + 1)
                    v.reciprocal(xden[:, t, :], xden[:, t, :])
                    dve.drain()
                    v.tensor_tensor(xsoft[:, t], xsoft[:, t], bci(xden[:, t, :], S), ALU.mult).then_inc(xp_ready, 1)
                turned_lo((2, "xa", l), psw)
                residual_norm([(2, "xo", l, k) for k in range(4)], (2, "2", l))
                turned_lo((2, "2", l), psa)
                serve((2, "xo", l, 3))
                for s in range(FS + 1):
                    f = FS * (L + l) + s
                    if s < FS:
                        serve((2, "g", l, s))
                        dve.wait_ge(conv_first, 2 * (FS * l + s + 1))
                        for tap, lag in ((1, 1), (0, 2)):
                            j = 1 + 2 * l
                            for buf, bank, ch0 in ((conv_g, 2 * (f % 2), 22 + 2 * s), (conv_a, 2 * (f % 2) + 1, 2 * s)):
                                for ch in range(2):
                                    cc = 44 * tap + ch0 + ch
                                    o = buf[:, f % 2, ch, lag:S]
                                    ins = v.scalar_tensor_tensor(out=o, in0=bank2(psw, bank)[:, ch, 0:S - lag],
                                                                 scalar=pcol[:, j, cc:cc + 1], in1=o, op0=ALU.mult,
                                                                 op1=ALU.add)
                            if tap:
                                dve.drain()
                        ins.then_inc(conv_done, 1)
                        serve((2, "u", l, s))
                        dve.wait_ge(gate_ready, f + 1)
                        dve.drain()
                        v.tensor_tensor(hidf, gact[:, f % 2, :], conv_a[:, f % 2].rearrange("p c s -> p (c s)"),
                                        ALU.mult)
                        dve.drain()
                        hh = hidh[:, f % 2, :, :].rearrange("p c s -> p (c s)")
                        hl = hidl[:, f % 2, :, :].rearrange("p c s -> p (c s)")
                        if s >= 2:
                            dve.wait_ge(tile_done, ti[(2, "d", l, s - 2)] + 1)
                        v.tensor_copy(hh, hidf)
                        dve.drain()
                        v.tensor_tensor(hl, hidf, hh.bitcast(F32), ALU.subtract).then_inc(hid_ready, 1)
                    for j in down_steps(s):
                        if j < FS - 1:
                            serve((2, "d", l, j))

                def join(t, cols, ps):
                    v.scalar_tensor_tensor(out=xtok[:, t, cols], in0=xtok[:, t, cols], scalar=ALPHA, in1=ps,
                                           op0=ALU.mult, op1=ALU.add)
                ffn_norm(2, l, (2, "3", l), join)

        @block.gpsimd
        def _(pool):
            g = nc.gpsimd

            scaled = [0]

            def norm_scale(token_tiles=range(NT)):
                for t in token_tiles:
                    scaled[0] += 1
                    pool.wait_ge(ln_var, scaled[0])
                    g.tensor_tensor(rstd[:, t:t + 1], vare[:, t:t + 1], mhalf[:, t:t + 1],
                                    ALU.pow).then_inc(ln_rstd, 1)

            def low_parts(c, after=(2, 3)):
                for i in [c + q for q in after]:
                    if i < n_tiles:
                        pool.wait_ge(hi_ready, i + 1)
                        g.tensor_tensor(tile_flat(wlo, NL, i), tile_flat(raw, NL, i),
                                        tile_flat(whi, NW, i).bitcast(F32), ALU.subtract).then_inc(lo_pool, 1)

            pool.wait_ge(mhalf_ready, 1)
            norm_scale()
            low_parts(0, (1, 3))
            norm_scale()
            low_parts(0, (5,))
            pool.wait_ge(tables_ready, 1)
            for l in range(L):
                pool.wait_ge(ki_var, l + 1)
                g.tensor_tensor(rstd[:, 0:NT], vare[:, 0:NT], mhalf[:, 0:NT], ALU.pow).then_inc(ki_rstd, 1)
                t1 = pt[:, 1:3, :].rearrange("p a b -> p (a b)")[:, 0:640].rearrange("p (h d) -> p h d", h=10)
                t2 = pt[:, 2:4, :].rearrange("p a b -> p (a b)")[:, 384:1024].rearrange("p (h d) -> p h d", h=10)
                x = proj1[:, 0, QA:QA + 640].rearrange("p (h d) -> p h d", h=10)
                for h0, h1 in ((0, H), (H, H + 2)):
                    pool.wait_ge(proj_ready, 7 * l + (6 if h0 == 0 else 7))
                    n, hs = h1 - h0, slice(h0, h1)
                    g.tensor_tensor(t1[:, hs], x[:, hs], bc(cos64[:, 0, :], n), ALU.mult)
                    g.tensor_tensor(t2[:, hs, 0:32], x[:, hs, 32:64], bc(sin64[:, 0, 0:32], n), ALU.mult)
                    g.tensor_tensor(t2[:, hs, 32:64], x[:, hs, 0:32], bc(sin64[:, 0, 32:64], n), ALU.mult)
                    pool.drain()
                    if h0 == 0:
                        g.tensor_tensor(roped[:, 0, 0:4 * P].rearrange("p (r a d) -> p a r d", a=2, d=DH),
                                        t1[:, 0:8, :].rearrange("p (a r) d -> p a r d", a=2),
                                        t2[:, 0:8, :].rearrange("p (a r) d -> p a r d", a=2), ALU.add)
                    else:
                        g.tensor_tensor(roped[:, 0, 4 * P:5 * P].rearrange("p (h d) -> p h d", h=2),
                                        t1[:, 8:10, :], t2[:, 8:10, :], ALU.add).then_inc(qka_roped[0], 1)
                for lm, k in during_attention(1, l):
                    low_parts(ti[(2, "kv", lm, k)], (NW,))
                norm_scale()
                low_parts(ti[(1, "o", l, 3)])
                for t in range(NT):
                    for _ in range(2 if l == L - 1 else 1):
                        norm_scale([t])
                low_parts(ti[(1, "d", l, FS - 1)])

            for l in range(L):
                pool.wait_ge(c_var, l + 1)
                g.tensor_tensor(rstdc[:], varc[:], mhalf[:], ALU.pow).then_inc(c_rstd, 1)
                pool.wait_ge(proj2_ready, 8 * l + 5)
                for t in range(NT):
                    ins = g.tensor_copy(nqp[:, t, :].rearrange("p (r g d) -> p g r d", r=4, g=2),
                                        proj2[:, t, NQ:NQ + 512].rearrange("p (g r d) -> p g r d", g=2, r=4))
                ins.then_inc(kd_ready, 1)
                pool.wait_ge(proj2_ready, 8 * l + 6)
                for e in range(2):
                    ins = g.tensor_copy(kdup[:, :, :, e, :],
                                        proj2[:, :, KC:KC + 256].rearrange("p t (q d) -> p t q d", q=4))
                ins.then_inc(kd_ready, 1)
                for lm, k in during_attention(2, l):
                    low_parts(ti[(2, "kv", lm, k)], (NW,))
                norm_scale()
                low_parts(ti[(2, "out", l, 3)])
                norm_scale()
                low_parts(ti[(2, "xo", l, 3)])
                norm_scale()
                low_parts(ti[(2, "d", l, FS - 1)])


_NAMES = [
    "x", "p", "positions", "ln_in_g", "ln_in_b", "w_in", "attn_sinks", "idx_k_g", "idx_k_b", "w_o", "ln1_g", "ln1_b",
    "w_gu", "w_down", "w_pg", "w_pp", "ln2_g", "ln2_b", "mem_2", "ln_in_g_2", "ln_in_b_2", "ln_mem_g_2",
    "ln_mem_b_2", "w_in_2", "mla_cq_g_2", "mla_w_uq_2", "mla_ckv_g_2", "mla_w_ukv_2", "nsa_pe_k_2", "nsa_w1_k_2",
    "nsa_b1_k_2", "nsa_w2_k_2", "nsa_pe_v_2", "nsa_w1_v_2", "nsa_b1_v_2", "nsa_w2_v_2", "w_out_2", "ln1_g_2",
    "ln1_b_2", "xa_wq_2", "xa_wkv_2", "xa_wo_2", "ln2_g_2", "ln2_b_2", "ffn_w_up_2", "ffn_conv_w_2",
    "ffn_conv_b_2", "ffn_w_down_2", "ln3_g_2", "ln3_b_2",
]


def kernel(**inputs):
    import concourse.bacc as bacc
    from concourse.bass_utils import run_bass_kernel_spmd

    nc = bacc.Bacc("TRN2", target_bir_lowering=False, num_devices=1, dynamic_dma_scratch_size=1024)
    arrays, w, c = {}, {}, {}
    for name in _NAMES:
        a = np.ascontiguousarray(inputs[name])
        arrays[f"in_{name}"] = a
        w[name] = nc.dram_tensor(f"in_{name}", a.shape, mybir.dt.from_np(a.dtype), kind="ExternalInput").ap()
    for name, a in constants().items():
        arrays[f"table_{name}"] = a
        c[name] = nc.dram_tensor(f"table_{name}", a.shape, F32, kind="ExternalInput").ap()
    out = nc.dram_tensor("out_0", (1, S, D), F32, kind="ExternalOutput").ap()
    build(nc, w, c, out)
    r = run_bass_kernel_spmd(nc, [arrays], core_ids=[0])
    return r.results[0]["out_0"]
```
